# Optimizing a Trainium2 kernel written in Bass

```python
import jax, jax.numpy as jnp
from jax import lax
import numpy as np
import math
import jax
import jax.numpy as jnp

D_MODEL = 1024
BATCH = 1
SEQ = 1024
DEPTH = 1

HEAD_DIM = 64
ATTN_HEADS = 8
ATTN_W = ATTN_HEADS * HEAD_DIM
CONV_W = 256
MEM_HEADS = 4
MEM_W = MEM_HEADS * HEAD_DIM
MIX_W = ATTN_W + CONV_W + MEM_W
N_MEM = 256
DILATED_PATTERNS = ((128, 1), (512, 4), (2048, 16))
ROPE_THETA = 500000.0
ROT_DIM = HEAD_DIM // 4
CONV_K = 31
FFN_CONV_K = 3
D_FF = 2816
IN_COLS = 3 * ATTN_W + 2 * CONV_W + MEM_W
SPLITS = (ATTN_W, 2 * ATTN_W, 3 * ATTN_W, 3 * ATTN_W + 2 * CONV_W)
NORM_EPS = 1e-6
NEG_INF = -1e30


def rms_norm(x, g):
    xf = x.astype(jnp.float32)
    y = xf * lax.rsqrt(jnp.mean(xf * xf, axis=-1, keepdims=True) + NORM_EPS)
    return (y * g.astype(jnp.float32)).astype(x.dtype)

def layer_norm(x, g, b):
    xf = x.astype(jnp.float32)
    mu = jnp.mean(xf, axis=-1, keepdims=True)
    var = jnp.mean(jnp.square(xf - mu), axis=-1, keepdims=True)
    y = (xf - mu) * lax.rsqrt(var + NORM_EPS)
    return (y * g.astype(jnp.float32) + b.astype(jnp.float32)).astype(x.dtype)

def partial_rotary(x, positions):
    inv_freq = ROPE_THETA ** (-jnp.arange(0, ROT_DIM, 2, dtype=jnp.float32) / ROT_DIM)
    ang = positions.astype(jnp.float32)[..., None] * inv_freq
    cos = jnp.cos(ang)[:, :, None, :]
    sin = jnp.sin(ang)[:, :, None, :]
    xr = x[..., :ROT_DIM].astype(jnp.float32)
    x1, x2 = xr[..., : ROT_DIM // 2], xr[..., ROT_DIM // 2:]
    rot = jnp.concatenate([x1 * cos - x2 * sin, x2 * cos + x1 * sin], axis=-1)
    return jnp.concatenate([rot.astype(x.dtype), x[..., ROT_DIM:]], axis=-1)

def depthwise_conv(x, w, b):
    k = w.shape[0]
    y = lax.conv_general_dilated(
        x, w[:, None, :].astype(x.dtype), window_strides=(1,),
        padding=[(k // 2, k // 2)], dimension_numbers=("NWC", "WIO", "NWC"),
        feature_group_count=x.shape[-1])
    return y + b.astype(x.dtype)

def banded_attention(q, k, v, half):
    n, L, H, Dh = q.shape
    blk = half
    nb = -(-L // blk)
    Lp = nb * blk
    qb = jnp.pad(q, ((0, 0), (0, Lp - L), (0, 0), (0, 0))).reshape(n, nb, blk, H, Dh)

    def halo(t):
        tp = jnp.pad(t, ((0, 0), (blk, Lp - L + blk), (0, 0), (0, 0))).reshape(n, nb + 2, blk, H, Dh)
        return jnp.concatenate([tp[:, :-2], tp[:, 1:-1], tp[:, 2:]], axis=2)

    kb, vb = halo(k), halo(v)
    s = jnp.einsum("nbqhd,nbkhd->nbhqk", qb, kb).astype(jnp.float32) * (Dh ** -0.5)
    bidx = jnp.arange(nb)[:, None, None]
    qi = jnp.arange(blk)[None, :, None]
    kj = jnp.arange(3 * blk)[None, None, :]
    key_pos = bidx * blk - blk + kj
    valid = (jnp.abs(kj - blk - qi) <= half) & (key_pos >= 0) & (key_pos < L)
    s = jnp.where(valid[None, :, None], s, NEG_INF)
    m = jnp.max(s, axis=-1, keepdims=True)
    p = jnp.exp(s - m)
    den = jnp.sum(p, axis=-1, keepdims=True)
    o = jnp.einsum("nbhqk,nbkhd->nbqhd", p, vb.astype(jnp.float32))
    o = o / jnp.transpose(den, (0, 1, 3, 2, 4))
    lse = jnp.transpose((m + jnp.log(den))[..., 0], (0, 1, 3, 2))
    return o.reshape(n, Lp, H, Dh)[:, :L], lse.reshape(n, Lp, H)[:, :L]

def dilated_attention(q, k, v, window, dil):
    B, S, H, Dh = q.shape
    L = S // dil

    def to_sub(t):
        return t.reshape(B, L, dil, H, Dh).transpose(0, 2, 1, 3, 4).reshape(B * dil, L, H, Dh)

    o, lse = banded_attention(to_sub(q), to_sub(k), to_sub(v), window // (2 * dil))
    o = o.reshape(B, dil, L, H, Dh).transpose(0, 2, 1, 3, 4).reshape(B, S, H, Dh)
    lse = lse.reshape(B, dil, L, H).transpose(0, 2, 1, 3).reshape(B, S, H)
    return o, lse

def first_inputs(seed: int = 0) -> dict:
    key = jax.random.key(seed)
    ks = jax.random.split(key, 24)
    f32 = jnp.float32

    def nrm(k, shape, scale):
        return jax.random.normal(k, shape, f32) * scale

    def gain(k, shape):
        return 1.0 + 0.02 * jax.random.normal(k, shape, f32)

    offsets = jax.random.randint(ks[2], (BATCH, 1), 0, 1024, dtype=jnp.int32)
    positions = (jnp.arange(SEQ, dtype=jnp.int32)[None, :] + offsets).astype(jnp.int32)
    return {
        "x": nrm(ks[0], (BATCH, SEQ, D_MODEL), 1.0),
        "mem": nrm(ks[1], (BATCH, N_MEM, D_MODEL), 1.0),
        "positions": positions,
        "mix_norm_g": gain(ks[3], (DEPTH, D_MODEL)),
        "mem_norm_g": gain(ks[4], (DEPTH, D_MODEL)),
        "w_in": nrm(ks[5], (DEPTH, D_MODEL, IN_COLS), D_MODEL ** -0.5),
        "w_mem_kv": nrm(ks[6], (DEPTH, D_MODEL, 2 * MEM_W), D_MODEL ** -0.5),
        "q_norm_g": gain(ks[7], (DEPTH, HEAD_DIM)),
        "k_norm_g": gain(ks[8], (DEPTH, HEAD_DIM)),
        "mq_norm_g": gain(ks[9], (DEPTH, HEAD_DIM)),
        "mk_norm_g": gain(ks[10], (DEPTH, HEAD_DIM)),
        "conv_dw_w": nrm(ks[11], (DEPTH, CONV_K, CONV_W), CONV_K ** -0.5),
        "conv_dw_b": nrm(ks[12], (DEPTH, CONV_W), 0.02),
        "conv_ln_g": gain(ks[13], (DEPTH, CONV_W)),
        "conv_ln_b": nrm(ks[14], (DEPTH, CONV_W), 0.02),
        "w_out": nrm(ks[15], (DEPTH, MIX_W, D_MODEL), MIX_W ** -0.5),
        "ffn_norm_g": gain(ks[16], (DEPTH, D_MODEL)),
        "w_up": nrm(ks[17], (DEPTH, D_MODEL, 2 * D_FF), D_MODEL ** -0.5),
        "ffn_dw_w": nrm(ks[18], (DEPTH, FFN_CONV_K, 2 * D_FF), FFN_CONV_K ** -0.5),
        "ffn_dw_b": nrm(ks[19], (DEPTH, 2 * D_FF), 0.02),
        "w_down": nrm(ks[20], (DEPTH, D_FF, D_MODEL), D_FF ** -0.5),
    }

def first_block(x, mem, positions, mix_norm_g, mem_norm_g, w_in, w_mem_kv, q_norm_g, k_norm_g,
              mq_norm_g, mk_norm_g, conv_dw_w, conv_dw_b, conv_ln_g, conv_ln_b, w_out,
              ffn_norm_g, w_up, ffn_dw_w, ffn_dw_b, w_down):
    B, S, _ = x.shape
    h = x
    for l in range(DEPTH):
        hn = rms_norm(h, mix_norm_g[l])
        proj = hn @ w_in[l]
        q, k, v, glu, qm = jnp.split(proj, SPLITS, axis=-1)

        q = partial_rotary(rms_norm(q.reshape(B, S, ATTN_HEADS, HEAD_DIM), q_norm_g[l]), positions)
        k = partial_rotary(rms_norm(k.reshape(B, S, ATTN_HEADS, HEAD_DIM), k_norm_g[l]), positions)
        v = v.reshape(B, S, ATTN_HEADS, HEAD_DIM)
        outs, lses = [], []
        for window, dil in DILATED_PATTERNS:
            o, lse = dilated_attention(q, k, v, window, dil)
            outs.append(o)
            lses.append(lse)
        wts = jax.nn.softmax(jnp.stack(lses, axis=0), axis=0)
        attn = jnp.sum(wts[..., None] * jnp.stack(outs, axis=0), axis=0)
        attn = attn.astype(h.dtype).reshape(B, S, ATTN_W)

        ga, gg = jnp.split(glu, 2, axis=-1)
        c = ga * jax.nn.sigmoid(gg)
        c = depthwise_conv(c, conv_dw_w[l], conv_dw_b[l])
        c = jax.nn.silu(layer_norm(c, conv_ln_g[l], conv_ln_b[l]))

        qm = rms_norm(qm.reshape(B, S, MEM_HEADS, HEAD_DIM), mq_norm_g[l])
        kvm = rms_norm(mem, mem_norm_g[l]) @ w_mem_kv[l]
        km, vm = jnp.split(kvm, 2, axis=-1)
        km = rms_norm(km.reshape(B, N_MEM, MEM_HEADS, HEAD_DIM), mk_norm_g[l])
        vm = vm.reshape(B, N_MEM, MEM_HEADS, HEAD_DIM)
        sm = jnp.einsum("bshd,bmhd->bhsm", qm, km).astype(jnp.float32) * (HEAD_DIM ** -0.5)
        pm = jax.nn.softmax(sm, axis=-1)
        mo = jnp.einsum("bhsm,bmhd->bshd", pm, vm.astype(jnp.float32))
        mo = mo.astype(h.dtype).reshape(B, S, MEM_W)

        mixed = jnp.concatenate([attn, c, mo], axis=-1)
        h = h + mixed @ w_out[l]

        f = rms_norm(h, ffn_norm_g[l]) @ w_up[l]
        f = depthwise_conv(f, ffn_dw_w[l], ffn_dw_b[l])
        fg, fu = jnp.split(f, 2, axis=-1)
        h = h + (jax.nn.silu(fg) * fu) @ w_down[l]
    return h


GRID_W = 64
CTX_LEN = 256
ROPE_THETA_2 = 10000.0
F32 = jnp.float32

A_HEADS = 4
A_QK = HEAD_DIM
A_V = 2 * HEAD_DIM
A_QBLOCK = 128
B_HEADS = 4
B_DK = HEAD_DIM // 2
B_DV = HEAD_DIM
B_GATE_RANK = 16
B_GATE_TAU = 16.0
B_CHUNK = 64
C_HEADS = 4
C_DH = HEAD_DIM
NA_ROWS = 8
NA_COLS = 16

A_WIDTH = A_HEADS * A_V
B_WIDTH = B_HEADS * B_DV
C_WIDTH = C_HEADS * C_DH
MIX_WIDTH = A_WIDTH + B_WIDTH + C_WIDTH

IN_SIZES = (A_HEADS * 2 * A_QK, A_HEADS * 2 * A_QK, A_WIDTH,
            B_HEADS * B_DK, B_HEADS * B_DK, B_WIDTH, B_WIDTH, 2 * B_GATE_RANK,
            C_WIDTH, C_WIDTH, C_WIDTH)
IN_WIDTH = sum(IN_SIZES)

N_GROUPS = 4
EXPERTS_PER_GROUP = 8
N_EXPERTS = N_GROUPS * EXPERTS_PER_GROUP
TOP_K = 2
EXPERT_HIDDEN = 512
MOE_BLOCK = 128


def rms_norm_2(x, g):
    xf = x.astype(F32)
    y = xf * lax.rsqrt(jnp.mean(xf * xf, axis=-1, keepdims=True) + NORM_EPS)
    return (y * g.astype(F32)).astype(x.dtype)

def split_in(p):
    return jnp.split(p, np.cumsum(IN_SIZES)[:-1].tolist(), axis=-1)

def axial_rope_tables(n_tokens, dtype):
    t = jnp.arange(n_tokens)
    row = (t // GRID_W).astype(F32)
    col = (t % GRID_W).astype(F32)
    n_freq = HEAD_DIM // 4
    inv = ROPE_THETA_2 ** (-jnp.arange(n_freq, dtype=F32) / n_freq)
    ang_r = row[:, None] * inv
    ang_c = col[:, None] * inv
    return (jnp.cos(ang_r).astype(dtype), jnp.sin(ang_r).astype(dtype),
            jnp.cos(ang_c).astype(dtype), jnp.sin(ang_c).astype(dtype))

def apply_axial_rope(x, tabs):
    cr, sr, cc, sc = (tb.reshape((tb.shape[0],) + (1,) * (x.ndim - 3) + (tb.shape[1],)) for tb in tabs)
    x1, x2, x3, x4 = jnp.split(x, 4, axis=-1)
    return jnp.concatenate([x1 * cr - x2 * sr, x2 * cr + x1 * sr,
                            x3 * cc - x4 * sc, x4 * cc + x3 * sc], axis=-1)

def diff_attention(q, k, v, qc, kc, vc, lam, lam_init, g_sub, need_ctx):
    B_, S = q.shape[:2]
    L = qc.shape[1]
    scale = A_QK ** -0.5
    k_all = jnp.concatenate([kc, k], axis=1)
    v_all = jnp.concatenate([vc, v], axis=1)

    def attend(qb, kb, vb):
        s = jnp.einsum('bqhmd,bkhmd->bhmqk', qb, kb).astype(F32) * scale
        p = jax.nn.softmax(s, axis=-1)
        d = p[:, :, 0] - lam * p[:, :, 1]
        return jnp.einsum('bhqk,bkhv->bqhv', d.astype(vb.dtype), vb)

    nb = S // A_QBLOCK
    qblocks = jnp.moveaxis(q.reshape((B_, nb, A_QBLOCK) + q.shape[2:]), 1, 0)
    o = lax.map(lambda qb: attend(qb, k_all, v_all), qblocks)
    o = jnp.moveaxis(o, 0, 1).reshape(B_, S, A_HEADS, A_V)
    out = (rms_norm_2(o, g_sub) * (1.0 - lam_init)).reshape(B_, S, A_WIDTH)
    out_c = None
    if need_ctx:
        oc = attend(qc, kc, vc)
        out_c = (rms_norm_2(oc, g_sub) * (1.0 - lam_init)).reshape(B_, L, A_WIDTH)
    return out, out_c

def gla_scan(q, k, v, log_a, s0):
    B_, H, T, dk = q.shape
    n = T // B_CHUNK

    def chunks(t):
        return jnp.moveaxis(t.reshape(B_, H, n, B_CHUNK, t.shape[-1]), 2, 0)

    causal = jnp.tril(jnp.ones((B_CHUNK, B_CHUNK), dtype=bool))

    def step(s, inp):
        qc, kc, vc, ac = inp
        b = jnp.cumsum(ac, axis=2)
        rel = jnp.where(causal[:, :, None], b[:, :, :, None, :] - b[:, :, None, :, :], -jnp.inf)
        a_intra = jnp.einsum('bhtsd,bhsd->bhts', qc[:, :, :, None, :] * jnp.exp(rel), kc)
        o = (jnp.einsum('bhts,bhsv->bhtv', a_intra, vc)
             + jnp.einsum('bhtd,bhdv->bhtv', qc * jnp.exp(b), s))
        b_end = b[:, :, -1, :]
        s = (jnp.exp(b_end)[..., None] * s
             + jnp.einsum('bhsd,bhsv->bhdv', kc * jnp.exp(b_end[:, :, None, :] - b), vc))
        return s, o

    s_final, o = lax.scan(step, s0, (chunks(q), chunks(k), chunks(v), chunks(log_a)))
    o = jnp.moveaxis(o, 0, 2).reshape(B_, H, T, v.shape[-1])
    return o, s_final

def gla_mixer(q, k, v, r, glow, qc, kc, vc, rc, glowc, w_dec, b_dec, g_out, need_ctx):
    B_ = q.shape[0]

    def heads(t, d):
        return jnp.transpose(t.reshape(t.shape[0], t.shape[1], -1, d), (0, 2, 1, 3)).astype(F32)

    def decay(gl, direction):
        z = gl[..., direction * B_GATE_RANK:(direction + 1) * B_GATE_RANK] @ w_dec[direction] + b_dec[direction]
        return heads(jax.nn.log_sigmoid(z.astype(F32)) / B_GATE_TAU, B_DK)

    def flip(t):
        return jnp.flip(t, axis=2)

    scale = B_DK ** -0.5
    ql, kl, vl = heads(q, B_DK) * scale, heads(k, B_DK), heads(v, B_DV)
    qx, kx, vx = heads(qc, B_DK) * scale, heads(kc, B_DK), heads(vc, B_DV)
    s0 = jnp.zeros((B_, B_HEADS, B_DK, B_DV), F32)
    ox_f, sx_f = gla_scan(qx, kx, vx, decay(glowc, 0), s0)
    ol_f, _ = gla_scan(ql, kl, vl, decay(glow, 0), sx_f)
    ox_b, sx_b = gla_scan(flip(qx), flip(kx), flip(vx), flip(decay(glowc, 1)), s0)
    ol_b, _ = gla_scan(flip(ql), flip(kl), flip(vl), flip(decay(glow, 1)), sx_b)

    def readout(o, gate):
        o = jnp.transpose(rms_norm_2(o, g_out), (0, 2, 1, 3)).reshape(gate.shape[0], gate.shape[1], B_WIDTH)
        return (o * jax.nn.silu(gate.astype(F32))).astype(gate.dtype)

    out = readout(ol_f + flip(ol_b), r)
    out_c = readout(ox_f + flip(ox_b), rc) if need_ctx else None
    return out, out_c

def neighborhood_attention(q, k, v, qc, kc, vc, rpb, need_ctx):
    B_, S, H, dh = q.shape
    L = qc.shape[1]
    rows = S // GRID_W
    wr = min(NA_ROWS, rows)
    scale = dh ** -0.5

    def grid(t):
        return jnp.transpose(t.reshape(B_, rows, GRID_W, H, dh), (0, 3, 1, 2, 4))

    qg, kg, vg = grid(q), grid(k), grid(v)
    r = jnp.arange(rows)
    row_idx = jnp.clip(r - wr // 2, 0, rows - wr)[:, None] + jnp.arange(wr)
    cq = jnp.arange(GRID_W)
    col_start = jnp.clip(cq - NA_COLS // 2, 0, GRID_W - NA_COLS)
    col_mask = (cq[None, :] >= col_start[:, None]) & (cq[None, :] < col_start[:, None] + NA_COLS)
    k_rows = kg[:, :, row_idx]
    v_rows = vg[:, :, row_idx]
    s_nb = jnp.einsum('bhrqd,bhrwkd->bhrqwk', qg, k_rows).astype(F32) * scale
    dr = row_idx - r[:, None] + (NA_ROWS - 1)
    dc = jnp.clip(cq[None, :] - cq[:, None], -(NA_COLS - 1), NA_COLS - 1) + (NA_COLS - 1)
    bias = rpb[:, dr[:, None, :, None], dc[None, :, None, :]].astype(F32)
    s_nb = jnp.where(col_mask[:, None, :], s_nb + bias, -jnp.inf)
    s_c = jnp.einsum('bhrqd,bchd->bhrqc', qg, kc).astype(F32) * scale
    n_nb = wr * GRID_W
    p = jax.nn.softmax(jnp.concatenate([s_nb.reshape(B_, H, rows, GRID_W, n_nb), s_c], axis=-1), axis=-1)
    p_nb = p[..., :n_nb].reshape(s_nb.shape).astype(v.dtype)
    p_c = p[..., n_nb:].astype(v.dtype)
    o = (jnp.einsum('bhrqwk,bhrwkd->bhrqd', p_nb, v_rows)
         + jnp.einsum('bhrqc,bchd->bhrqd', p_c, vc))
    out = jnp.transpose(o, (0, 2, 3, 1, 4)).reshape(B_, S, H * dh)
    out_c = None
    if need_ctx:
        sc = jnp.einsum('bqhd,bkhd->bhqk', qc, kc).astype(F32) * scale
        out_c = jnp.einsum('bhqk,bkhd->bqhd', jax.nn.softmax(sc, axis=-1).astype(vc.dtype), vc).reshape(B_, L, H * dh)
    return out, out_c

def hier_moe(h, w_rg, b_rg, w_re, b_re, w_up, w_down):
    n_tok, D = h.shape
    n_assign = n_tok * TOP_K
    n_blocks = -(-(n_assign + N_EXPERTS * (MOE_BLOCK - 1)) // MOE_BLOCK)
    logit_g = (h @ w_rg + b_rg).astype(F32)
    grp = jnp.argmax(logit_g, axis=-1)
    p_grp = jnp.take_along_axis(jax.nn.softmax(logit_g, axis=-1), grp[:, None], axis=1)
    logit_e = (h @ w_re + b_re).astype(F32).reshape(n_tok, N_GROUPS, EXPERTS_PER_GROUP)
    logit_e = jnp.take_along_axis(logit_e, grp[:, None, None], axis=1)[:, 0]
    top_v, top_i = lax.top_k(logit_e, TOP_K)
    gate = jax.nn.softmax(top_v, axis=-1) * p_grp
    expert = (grp[:, None] * EXPERTS_PER_GROUP + top_i).reshape(-1)
    order = jnp.argsort(expert)
    e_sorted = expert[order]
    tok_sorted = order // TOP_K
    counts = jnp.bincount(expert, length=N_EXPERTS)
    padded = (counts + MOE_BLOCK - 1) // MOE_BLOCK * MOE_BLOCK
    start = jnp.cumsum(counts) - counts
    pad_end = jnp.cumsum(padded)
    pad_start = pad_end - padded
    dest = pad_start[e_sorted] + jnp.arange(n_assign) - start[e_sorted]
    buf = jnp.zeros((n_blocks * MOE_BLOCK, D), h.dtype).at[dest].set(h[tok_sorted])
    blk_expert = jnp.minimum(jnp.searchsorted(pad_end, jnp.arange(n_blocks) * MOE_BLOCK, side='right'), N_EXPERTS - 1)

    def expert_block(args):
        xb, e = args
        g, u = jnp.split(xb @ w_up[e], 2, axis=-1)
        return (jax.nn.silu(g) * u) @ w_down[e]

    y = lax.map(expert_block, (buf.reshape(n_blocks, MOE_BLOCK, D), blk_expert)).reshape(-1, D)
    y = y[dest] * gate.reshape(-1)[order][:, None].astype(h.dtype)
    return jax.ops.segment_sum(y, tok_sorted, num_segments=n_tok)

def hybrid_layer(x, xc, c_act, cc_act, rope, layer_idx, need_ctx,
                 w_mod, b_mod, g1, g2, w_in, w_out, lam, g_sub,
                 w_dec, b_dec, g_gla, rpb, w_rg, b_rg, w_re, b_re, w_up, w_down):
    B_, S, D = x.shape
    L = xc.shape[1]
    mod = (c_act @ w_mod + b_mod).reshape(B_, 6, 1, D)
    modc = (cc_act @ w_mod + b_mod).reshape(6, D)
    h = rms_norm_2(x, g1) * (1 + mod[:, 1]) + mod[:, 0]
    hc = rms_norm_2(xc, g1) * (1 + modc[1]) + modc[0]
    qa, ka, va, qb, kb, vb, rb, gb, qn, kn, vn = split_in(h @ w_in)
    qa_c, ka_c, va_c, qb_c, kb_c, vb_c, rb_c, gb_c, qn_c, kn_c, vn_c = split_in(hc @ w_in)

    lam_init = 0.8 - 0.6 * math.exp(-0.3 * layer_idx)
    lam_f = lam.astype(F32)
    lam_val = jnp.exp(jnp.sum(lam_f[0] * lam_f[1])) - jnp.exp(jnp.sum(lam_f[2] * lam_f[3])) + lam_init

    def a_qk(t):
        return t.reshape(t.shape[0], t.shape[1], A_HEADS, 2, A_QK)

    ya, ya_c = diff_attention(apply_axial_rope(a_qk(qa), rope), apply_axial_rope(a_qk(ka), rope),
                              va.reshape(B_, S, A_HEADS, A_V), a_qk(qa_c), a_qk(ka_c),
                              va_c.reshape(B_, L, A_HEADS, A_V), lam_val, lam_init, g_sub, need_ctx)
    yb, yb_c = gla_mixer(qb, kb, vb, rb, gb, qb_c, kb_c, vb_c, rb_c, gb_c, w_dec, b_dec, g_gla, need_ctx)

    def c_heads(t):
        return t.reshape(t.shape[0], t.shape[1], C_HEADS, C_DH)

    yn, yn_c = neighborhood_attention(c_heads(qn), c_heads(kn), c_heads(vn),
                                      c_heads(qn_c), c_heads(kn_c), c_heads(vn_c), rpb, need_ctx)
    x = x + mod[:, 2] * (jnp.concatenate([ya, yb, yn], axis=-1) @ w_out)
    h2 = rms_norm_2(x, g2) * (1 + mod[:, 4]) + mod[:, 3]
    if need_ctx:
        xc = xc + modc[2] * (jnp.concatenate([ya_c, yb_c, yn_c], axis=-1) @ w_out)
        h2c = rms_norm_2(xc, g2) * (1 + modc[4]) + modc[3]
        f = hier_moe(jnp.concatenate([h2.reshape(-1, D), h2c.reshape(-1, D)], axis=0),
                     w_rg, b_rg, w_re, b_re, w_up, w_down)
        x = x + mod[:, 5] * f[:B_ * S].reshape(B_, S, D)
        xc = xc + modc[5] * f[B_ * S:].reshape(B_, L, D)
    else:
        f = hier_moe(h2.reshape(-1, D), w_rg, b_rg, w_re, b_re, w_up, w_down)
        x = x + mod[:, 5] * f.reshape(B_, S, D)
    return x, xc

def second_inputs(seed: int = 0) -> dict:
    key = jax.random.key(seed)
    ks = jax.random.split(key, 23)
    D = D_MODEL

    def nrm(k, shape, s):
        return jax.random.normal(k, shape, F32) * s

    return {
        'x': nrm(ks[0], (BATCH, SEQ, D), 1.0),
        'c': nrm(ks[1], (BATCH, D), 1.0),
        'ctx': nrm(ks[2], (BATCH, CTX_LEN, D), 1.0),
        'c_ctx': nrm(ks[3], (D,), 1.0),
        'w_mod': nrm(ks[4], (DEPTH, D, 6 * D), 0.5 * D ** -0.5),
        'b_mod': nrm(ks[5], (DEPTH, 6 * D), 0.02),
        'norm1_g': 1.0 + nrm(ks[6], (DEPTH, D), 0.02),
        'norm2_g': 1.0 + nrm(ks[7], (DEPTH, D), 0.02),
        'w_in': nrm(ks[8], (DEPTH, D, IN_WIDTH), D ** -0.5),
        'w_out': nrm(ks[9], (DEPTH, MIX_WIDTH, D), MIX_WIDTH ** -0.5),
        'diff_lambda': nrm(ks[10], (DEPTH, 4, A_QK), 0.1),
        'diff_sub_g': 1.0 + nrm(ks[11], (DEPTH, A_V), 0.02),
        'gla_w_decay': nrm(ks[12], (DEPTH, 2, B_GATE_RANK, B_HEADS * B_DK), B_GATE_RANK ** -0.5),
        'gla_b_decay': nrm(ks[13], (DEPTH, 2, B_HEADS * B_DK), 0.1),
        'gla_norm_g': 1.0 + nrm(ks[14], (DEPTH, B_DV), 0.02),
        'na_rel_bias': nrm(ks[15], (DEPTH, C_HEADS, 2 * NA_ROWS - 1, 2 * NA_COLS - 1), 0.02),
        'w_router_group': nrm(ks[16], (DEPTH, D, N_GROUPS), D ** -0.5),
        'b_router_group': nrm(ks[17], (DEPTH, N_GROUPS), 0.01),
        'w_router_expert': nrm(ks[18], (DEPTH, D, N_EXPERTS), D ** -0.5),
        'b_router_expert': nrm(ks[19], (DEPTH, N_EXPERTS), 0.01),
        'w_expert_up': nrm(ks[20], (DEPTH, N_EXPERTS, D, 2 * EXPERT_HIDDEN), D ** -0.5),
        'w_expert_down': nrm(ks[21], (DEPTH, N_EXPERTS, EXPERT_HIDDEN, D), EXPERT_HIDDEN ** -0.5),
        'final_g': 1.0 + nrm(ks[22], (D,), 0.02),
    }

def second_block(x, c, ctx, c_ctx, w_mod, b_mod, norm1_g, norm2_g, w_in, w_out,
              diff_lambda, diff_sub_g, gla_w_decay, gla_b_decay, gla_norm_g, na_rel_bias,
              w_router_group, b_router_group, w_router_expert, b_router_expert,
              w_expert_up, w_expert_down, final_g):
    rope = axial_rope_tables(x.shape[1], x.dtype)
    c_act = jax.nn.silu(c)
    cc_act = jax.nn.silu(c_ctx)
    xc = ctx
    for l in range(DEPTH):
        x, xc = hybrid_layer(x, xc, c_act, cc_act, rope, l, l < DEPTH - 1,
                             w_mod[l], b_mod[l], norm1_g[l], norm2_g[l], w_in[l], w_out[l],
                             diff_lambda[l], diff_sub_g[l], gla_w_decay[l], gla_b_decay[l],
                             gla_norm_g[l], na_rel_bias[l], w_router_group[l], b_router_group[l],
                             w_router_expert[l], b_router_expert[l], w_expert_up[l], w_expert_down[l])
    return rms_norm_2(x, final_g)


def setup_inputs(seed=0):
    out = dict(first_inputs(seed))
    for name, value in second_inputs(seed + 1).items():
        if name != "x":
            out[name + "_2"] = value
    return out


def reference(
    x, mem, positions, mix_norm_g, mem_norm_g, w_in, w_mem_kv, q_norm_g, k_norm_g, mq_norm_g,
    mk_norm_g, conv_dw_w, conv_dw_b, conv_ln_g, conv_ln_b, w_out, ffn_norm_g, w_up, ffn_dw_w,
    ffn_dw_b, w_down, c_2, ctx_2, c_ctx_2, w_mod_2, b_mod_2, norm1_g_2, norm2_g_2, w_in_2,
    w_out_2, diff_lambda_2, diff_sub_g_2, gla_w_decay_2, gla_b_decay_2, gla_norm_g_2,
    na_rel_bias_2, w_router_group_2, b_router_group_2, w_router_expert_2, b_router_expert_2,
    w_expert_up_2, w_expert_down_2, final_g_2,
):
    x = first_block(
        x, mem, positions, mix_norm_g, mem_norm_g, w_in, w_mem_kv, q_norm_g, k_norm_g,
        mq_norm_g, mk_norm_g, conv_dw_w, conv_dw_b, conv_ln_g, conv_ln_b, w_out, ffn_norm_g,
        w_up, ffn_dw_w, ffn_dw_b, w_down,
    )
    return second_block(
        x, c_2, ctx_2, c_ctx_2, w_mod_2, b_mod_2, norm1_g_2, norm2_g_2, w_in_2, w_out_2,
        diff_lambda_2, diff_sub_g_2, gla_w_decay_2, gla_b_decay_2, gla_norm_g_2, na_rel_bias_2,
        w_router_group_2, b_router_group_2, w_router_expert_2, b_router_expert_2, w_expert_up_2,
        w_expert_down_2, final_g_2,
    )


_drawn_inputs = setup_inputs


def setup_inputs(seed=0):
    import zlib

    import numpy as np

    out = dict(_drawn_inputs(seed))
    spreads = {}
    factors = {'mix_norm_g': 5.757,
     'mem_norm_g': 8.0,
     'q_norm_g': 8.0,
     'k_norm_g': 8.0,
     'mq_norm_g': 8.0,
     'mk_norm_g': 8.0,
     'conv_dw_b': 4.134,
     'conv_ln_g': 5.199,
     'conv_ln_b': 6.263,
     'ffn_norm_g': 3.53,
     'ffn_dw_b': 3.458,
     'b_mod_2': 2.802,
     'norm1_g_2': 8.0,
     'norm2_g_2': 5.651,
     'diff_lambda_2': 4.728,
     'diff_sub_g_2': 43.133,
     'gla_w_decay_2': 3.892,
     'gla_b_decay_2': 8.0,
     'gla_norm_g_2': 8.0,
     'na_rel_bias_2': 64.0,
     'b_router_group_2': 8.0,
     'b_router_expert_2': 27.761,
     'final_g_2': 8.823}
    for name, (base, spread) in spreads.items():
        noise = np.random.default_rng([zlib.crc32(name.encode()), seed]).standard_normal(out[name].shape)
        drawn = base * np.exp(spread * noise) if base else spread * noise
        out[name] = jnp.asarray(drawn.astype(out[name].dtype))
    for name, factor in factors.items():
        out[name] = (out[name] * factor).astype(out[name].dtype)
    return out
```

```python
from contextlib import ExitStack

import numpy as np

import concourse.bass as bass
from concourse import mybir

F32 = mybir.dt.float32
I32 = mybir.dt.int32
U32 = mybir.dt.uint32
ACT = mybir.ActivationFunctionType
ALU = mybir.AluOpType
AX = mybir.AxisListType

P = 128
T = 1024
D = 1024
KD = D // P
NMEM = 256
NCTX = 256
FF = 2816
KF = FF // P
BANK = 512
EPS = 1e-6
NEG = -1e30
SCALE = 64.0 ** -0.5


class Phase:

    def __init__(self, nc, tag):
        self.nc, self.tag, self.ctx, self.sems = nc, tag, ExitStack(), []

    def __enter__(self):
        return self

    def __exit__(self, *e):
        self.nc.clear_and_free_semaphores(self.sems)
        self.nc.all_engine_barrier(sem_only=True)
        return self.ctx.__exit__(*e)

    def sb(self, name, shape, dt=F32):
        return self.ctx.enter_context(self.nc.sbuf_tensor(f"{self.tag}_{name}", shape, dt))

    def ps(self, name, shape, dt=F32):
        return self.ctx.enter_context(self.nc.psum_tensor(f"{self.tag}_{name}", shape, dt))

    def sem(self, name):
        self.sems.append(self.nc.alloc_semaphore(f"{self.tag}_{name}"))
        return self.sems[-1]


class Steps:

    def __init__(self, eng, sem):
        self.eng, self.sem, self.n, self.i, self.k = eng, sem, 0, None, 0

    def enter(self, i, per):
        self.i, self.per, self.k = i, per, 0

    def leave(self, trips):
        assert self.k == self.per, (self.k, self.per)
        self.n, self.i = self.n + trips * self.per, None

    def done(self, ins):
        ins.then_inc(self.sem, 1)
        if self.i is None:
            self.n += 1
            self.eng.wait_ge(self.sem, self.n)
        else:
            self.k += 1
            self.eng.wait_ge(self.sem, self.i * self.per + (self.n + self.k))


def chunks(n, size=BANK):
    return [(a, min(size, n - a)) for a in range(0, n, size)]


def at(ap, i):
    return ap[:, bass.ds(i, 1), :].rearrange("p a n -> p (a n)")


def cols(ap):
    return [ap[:, k, :] for k in range(ap.shape[1])]


def load_all(nc, tag, pairs):
    with Phase(nc, tag) as ph:
        loaded = ph.sem("loaded")
        with nc.Block() as block:
            @block.sync
            def _(sp):
                for dst, src in pairs:
                    sp.dma_start(dst, src).then_inc(loaded, 16)
                sp.wait_ge(loaded, 16 * len(pairs))


def store_all(nc, tag, pairs):
    load_all(nc, tag, pairs)


def rms_norm(nc, tag, cst, x, out, gain, shift=None, width=D):
    K, n = x.shape[1], x.shape[2]
    parts = chunks(n)
    with Phase(nc, tag) as ph:
        sq = ph.sb("sq", [P, 2, BANK])
        sd = ph.sb("sd", [P, 2, BANK])
        ms = ph.ps("ms", [P, 2, BANK])
        sq_ready, summed, sd_ready = ph.sem("sq_ready"), ph.sem("summed"), ph.sem("sd_ready")
        step = ph.sem("step")
        with nc.Block() as block:
            @block.scalar
            def _(act):
                def root(h):
                    a, w = parts[h]
                    act.wait_ge(summed, K * (h + 1))
                    nc.scalar.activation(sd[:, h % 2, 0:w], ms[:, h % 2, 0:w], ACT.Sqrt, bias=cst["eps"],
                                         scale=1.0 / width).then_inc(sd_ready, 1)
                for h, (a, w) in enumerate(parts):
                    for k in range(K):
                        j = h * K + k
                        if j >= 2:
                            act.wait_ge(summed, j - 1)
                        nc.scalar.activation(sq[:, j % 2, 0:w], x[:, k, a:a + w], ACT.Square).then_inc(sq_ready, 1)
                    root(h)

            @block.tensor
            def _(pe):
                for h, (a, w) in enumerate(parts):
                    if h >= 2:
                        pe.wait_ge(sd_ready, h - 1)
                    for k in range(K):
                        j = h * K + k
                        pe.wait_ge(sq_ready, j + 1)
                        nc.tensor.matmul(ms[:, h % 2, 0:w], cst["ones"], sq[:, j % 2, 0:w], start=(k == 0),
                                         stop=(k == K - 1)).then_inc(summed, 1)

            @block.vector
            def _(dve):
                st = Steps(dve, step)
                for h, (a, w) in enumerate(parts):
                    dve.wait_ge(sd_ready, h + 1)
                    st.done(nc.vector.reciprocal(sd[:, h % 2, 0:w], sd[:, h % 2, 0:w]))
                    for k in range(K):
                        last = nc.vector.scalar_tensor_tensor(out=out[:, k, a:a + w], in0=x[:, k, a:a + w],
                                                              scalar=gain[:, k:k + 1], in1=sd[:, h % 2, 0:w],
                                                              op0=ALU.mult, op1=ALU.mult)
                    if shift is not None:
                        st.done(last)
                        for k in range(K):
                            nc.vector.tensor_scalar(out[:, k, a:a + w], out[:, k, a:a + w], shift[:, k:k + 1],
                                                    None, ALU.add)


def project(nc, tag, w_dram, src, n, count, dst=None, add_to=None, gate=None, first=0):
    K = len(src)
    parts = chunks(n)
    wide = len(parts) * BANK
    with Phase(nc, tag) as ph:
        w = ph.sb("w", [P, 2, K, P])
        acc = ph.ps("acc", [P, 2, wide])
        w_ready = [ph.sem("w_ready0"), ph.sem("w_ready1")]
        mm_done, acc_free = ph.sem("mm_done"), ph.sem("acc_free")
        pairs, tail = count // 2, count % 2
        with nc.Block() as block:
            @block.sync
            def _(sp):
                def load(i, u):
                    sp.wait_ge(mm_done, i * 2 + (u + 1))
                    sp.dma_start(w[:, u], w_dram[bass.ds(i * 2 + (u + first), 1)].rearrange(
                        "a p (k n) -> p (a k) n", k=K)).then_inc(w_ready[u], 16)
                with sp.Fori(0, pairs) as i:
                    for u in range(2):
                        load(i, u)
                if tail:
                    load(pairs, 0)

            @block.tensor
            def _(pe):
                pe.sem_inc(mm_done, 2)

                def tile(i, u):
                    pe.wait_ge(w_ready[u], i * 16 + 16)
                    pe.wait_ge(acc_free, i * 2 + (u + 1))
                    for a, width in parts:
                        for k in range(K):
                            mm = nc.tensor.matmul(acc[:, u, a:a + width], w[:, u, k, :], src[k][:, a:a + width],
                                                  start=(k == 0), stop=(k == K - 1))
                    mm.then_inc(mm_done, 1)
                with pe.Fori(0, pairs) as i:
                    for u in range(2):
                        tile(i, u)
                if tail:
                    tile(pairs, 0)

            if dst is not None:
                @block.scalar
                def _(act):
                    act.sem_inc(acc_free, 2)

                    def keep(i, u):
                        act.wait_ge(mm_done, i * 2 + (u + 3))
                        nc.scalar.activation(at(dst, i * 2 + u), acc[:, u, 0:n], ACT.Copy).then_inc(acc_free, 1)
                    with act.Fori(0, pairs) as i:
                        for u in range(2):
                            keep(i, u)
                    if tail:
                        keep(pairs, 0)
            else:
                @block.vector
                def _(dve):
                    dve.sem_inc(acc_free, 2)
                    with dve.Fori(0, pairs) as i:
                        for u in range(2):
                            dve.wait_ge(mm_done, i * 2 + (u + 3))
                            o = at(add_to, i * 2 + u)
                            if gate is None:
                                nc.vector.tensor_tensor(o, acc[:, u, 0:n], o, ALU.add).then_inc(acc_free, 1)
                            else:
                                nc.vector.scalar_tensor_tensor(out=o, in0=acc[:, u, 0:n],
                                                               scalar=gate[:, bass.ds(i * 2 + u, 1)], in1=o,
                                                               op0=ALU.mult, op1=ALU.add).then_inc(acc_free, 1)


def project_rows(nc, tag, w_dram, src, n, dst):
    K, cols = w_dram.shape[1], w_dram.shape[2]
    cc = chunks(cols)
    tiles = n // P
    with Phase(nc, tag) as ph:
        w = ph.sb("w", [P, K, BANK])
        acc = ph.ps("acc", [P, 2, BANK])
        w_ready, mm_done, acc_free = ph.sem("w_ready"), ph.sem("mm_done"), ph.sem("acc_free")
        with nc.Block() as block:
            @block.sync
            def _(sp):
                for c, (a, width) in enumerate(cc):
                    if c:
                        sp.wait_ge(mm_done, c * tiles)
                    sp.dma_start(w[:, :, 0:width], w_dram[:, :, a:a + width]).then_inc(w_ready, 16)

            @block.tensor
            def _(pe):
                for c, (a, width) in enumerate(cc):
                    pe.wait_ge(w_ready, 16 * (c + 1))
                    for t in range(tiles):
                        j = c * tiles + t
                        if j >= 2:
                            pe.wait_ge(acc_free, j - 1)
                        for k in range(K):
                            mm = nc.tensor.matmul(acc[:, j % 2, 0:width], src[k][:, t * P:(t + 1) * P],
                                                  w[:, k, 0:width], start=(k == 0), stop=(k == K - 1))
                        mm.then_inc(mm_done, 1)

            @block.scalar
            def _(act):
                for c, (a, width) in enumerate(cc):
                    for t in range(tiles):
                        j = c * tiles + t
                        act.wait_ge(mm_done, j + 1)
                        nc.scalar.activation(dst[:, t, a:a + width], acc[:, j % 2, 0:width],
                                             ACT.Copy).then_inc(acc_free, 1)


def head_prep(nc, tag, cst, x, n, tiles, gain=None, rope=None, blk=("blk64", 64)):
    parts = chunks(n)
    wide = len(parts) * BANK
    per = (2 if gain is not None else 0) + (3 if rope else 0)
    with Phase(nc, tag) as ph:
        sq = ph.sb("sq", [P, n])
        sd = ph.sb("sd", [P, n])
        turn = ph.sb("turn", [P, n])
        ms, rot_ps = ph.ps("ms", [P, wide]), ph.ps("rot", [P, wide])
        sq_ready, summed, sd_ready, normed = (ph.sem(s) for s in ("sq_ready", "summed", "sd_ready", "normed"))
        turned, step = ph.sem("turned"), ph.sem("step")
        with nc.Block() as block:
            if gain is not None:
                @block.scalar
                def _(act):
                    with act.Fori(0, tiles) as i:
                        act.wait_ge(summed, i)
                        nc.scalar.activation(sq[:], at(x, i), ACT.Square).then_inc(sq_ready, 1)
                        act.wait_ge(summed, i + 1)
                        act.wait_ge(normed, i)
                        nc.scalar.activation(sd[:], ms[:, 0:n], ACT.Sqrt, bias=cst["eps"],
                                             scale=1.0 / blk[1]).then_inc(sd_ready, 1)

            @block.tensor
            def _(pe):
                with pe.Fori(0, tiles) as i:
                    if gain is not None:
                        pe.wait_ge(sq_ready, i + 1)
                        pe.wait_ge(sd_ready, i)
                        for a, w in parts:
                            mm = nc.tensor.matmul(ms[:, a:a + w], cst[blk[0]], sq[:, a:a + w], start=True, stop=True)
                        mm.then_inc(summed, 1)
                    if rope:
                        if gain is not None:
                            pe.wait_ge(normed, i + 1)
                        else:
                            pe.wait_ge(normed, i)
                        for a, w in parts:
                            mm = nc.tensor.matmul(rot_ps[:, a:a + w], rope[0], at(x, i)[:, a:a + w], start=True, stop=True)
                        mm.then_inc(turned, 1)

            @block.vector
            def _(dve):
                st = Steps(dve, step)
                with dve.Fori(0, tiles) as i:
                    st.enter(i, per)
                    xi = at(x, i)
                    if gain is not None:
                        dve.wait_ge(sd_ready, i + 1)
                        st.done(nc.vector.reciprocal(sd[:], sd[:]))
                        st.done(nc.vector.scalar_tensor_tensor(out=xi, in0=xi, scalar=gain, in1=sd[:],
                                                               op0=ALU.mult, op1=ALU.mult))
                        dve.sem_inc(normed, 1)
                    if rope:
                        dve.wait_ge(turned, i + 1)
                        st.done(nc.vector.tensor_tensor(turn[:], rot_ps[:, 0:n], rope[2], ALU.mult))
                        st.done(nc.vector.tensor_tensor(xi, xi, rope[1], ALU.mult))
                        st.done(nc.vector.tensor_tensor(xi, xi, turn[:], ALU.add))
                        if gain is None:
                            dve.sem_inc(normed, 1)
                st.leave(tiles)


def attention(nc, tag, cst, pairs, q, keys, v, KT, bias=None, diff=None, window=None, scratch=None):
    out = q
    tiles = T // P
    nk = sum(n for _, n in keys)
    seen = KT if window is None else len(window[0])
    NS = seen * P
    ng = -(-seen // 4)
    wide = -(-NS // BANK) * BANK
    PTS = 1 if wide > 2 * BANK else 2
    if window is not None:
        units = [(t, u) for t in range(tiles) for u in range(2)]
    elif diff is not None:
        units = [(t, u) for t in range(tiles) for u in range(2)]
    else:
        units = [(c * 4 + t, u) for c in range(2) for u in range(2) for t in range(4)]
    U = len(units)
    merged = 2 if diff is not None else 1
    M = U // merged
    share = 1 if window is not None else 4
    J = M // share
    G = M * ng
    NP = 2 * merged
    with Phase(nc, tag) as ph:
        if scratch is None:
            qs, ks, prob = ph.sb("qs", [P, T]), ph.sb("ks", [P, nk]), ph.sb("prob", [P, NP, NS])
        else:
            flat = scratch[:].rearrange("p a b -> p (a b)")
            qs, ks = flat[:, 0:T], flat[:, T:T + nk]
            prob = flat[:, T + nk:T + nk + NP * NS].rearrange("p (a b) -> p a b", a=NP)
        vs = ph.sb("vs", [P, KT, 1 if diff is not None else 2, P])
        probT = ph.sb("probT", [P, 2, seen, share * P])
        negm = ph.sb("negm", [P, NP])
        den = ph.sb("den", [P, NP])
        rden = ph.sb("rden", [P, 2, share * P])
        s_ps = ph.ps("s_ps", [P, 2, wide])
        t_ps = ph.ps("t_ps", [P, PTS, 4, P])
        o_ps = ph.ps("o_ps", [P, PTS, BANK])
        ones_set, staged, s_ready, s_free = (ph.sem(s) for s in ("ones_set", "staged", "s_ready", "s_free"))
        max_ready, p_ready, d_ready = (ph.sem(s) for s in ("max_ready", "p_ready", "d_ready"))
        t_ready, t_free, o_ready, o_free, step = (ph.sem(s) for s in ("t_ready", "t_free", "o_ready", "o_free", "step"))
        NST = 1 + len(keys) + (1 if diff is not None else 2)
        with nc.Block() as block:
            @block.gpsimd
            def _(pool):
                if diff is None:
                    nc.gpsimd.memset(vs[:], 1.0).then_inc(ones_set, 1)
                    pool.wait_ge(ones_set, 1)
                with pool.Fori(0, pairs) as m:
                    pool.wait_ge(o_ready, m * J + 2)
                    nc.gpsimd.tensor_copy(qs[:, 0:T], at(q, m)).then_inc(staged, 1)
                    a = 0
                    for kap, n in keys:
                        nc.gpsimd.tensor_copy(ks[:, a:a + n], at(kap, m)).then_inc(staged, 1)
                        a += n
                    if diff is not None:
                        nc.gpsimd.tensor_copy(vs[:, :, 0, :], v[:, :, bass.ds(m * P, P)]).then_inc(staged, 1)
                    else:
                        nc.gpsimd.tensor_copy(vs[:, :, 0, 0:64], v[:, :, bass.ds(m * P, 64)]).then_inc(staged, 1)
                        nc.gpsimd.tensor_copy(vs[:, :, 1, 64:128], v[:, :, bass.ds(m * P + 64, 64)]).then_inc(staged, 1)

            @block.tensor
            def _(pe):
                pe.sem_inc(o_ready, 2)
                pe.sem_inc(t_ready, 2 * ng)
                with pe.Fori(0, pairs) as m:
                    pe.wait_ge(staged, m * NST + NST)

                    def scores(n):
                        t, u = units[n]
                        pe.wait_ge(s_free, m * U + (n + 1))
                        r = slice(64 * u, 64 * u + 64)
                        if window is None:
                            runs = [(a, a, w) for a, w in chunks(nk)]
                        else:
                            k0, nw = window[t][0] * P, (seen - 2) * P
                            runs = [(a, k0 + a, w) for a, w in chunks(nw)]
                            runs += [(a, nk - NCTX + a - nw, min(w, BANK - a % BANK)) for a, w in [(nw, NCTX)]]
                        for o, a, w in runs:
                            mm = nc.tensor.matmul(s_ps[:, n % 2, o:o + w], qs[r, t * P:(t + 1) * P], ks[r, a:a + w],
                                                  start=True, stop=True)
                        mm.then_inc(s_ready, 1)

                    def turn(k):
                        pe.wait_ge(d_ready if diff is not None else p_ready, m * M + (k + 1))
                        p = prob[:, (k % 2) * merged, :]
                        for g in range(ng):
                            j = k * ng + g
                            pe.wait_ge(t_free, m * G + (j + 1))
                            for x in range(4 * g, min(4 * g + 4, seen)):
                                mm = nc.tensor.transpose(t_ps[:, j % PTS, x - 4 * g, :], p[:, x * P:(x + 1) * P],
                                                         cst["ident"])
                            mm.then_inc(t_ready, 1)

                    def values(j):
                        pe.wait_ge(t_free, m * G + (PTS + (j + 1) * share * ng))
                        pe.wait_ge(o_free, m * J + (j + 1))
                        u = 0 if diff is not None else units[j * share * merged][1]
                        t = units[j * share * merged][0]
                        for x in range(seen):
                            kt = x if window is None else window[t][x]
                            mm = nc.tensor.matmul(o_ps[:, j % PTS, 0:share * P], vs[:, kt, u, :],
                                                  probT[:, j % 2, x, :], start=(x == 0), stop=(x == seen - 1))
                        mm.then_inc(o_ready, 1)

                    for n in range(merged):
                        scores(n)
                    for k in range(M):
                        for n in range((k + 1) * merged, min((k + 2) * merged, U)):
                            scores(n)
                        turn(k)
                        if k % share == 0 and k:
                            values(k // share - 1)
                    values(J - 1)

            @block.scalar
            def _(act):
                act.sem_inc(t_free, PTS)
                if bias is None:
                    act.sem_inc(s_free, 2)
                with act.Fori(0, pairs) as m:
                    def exps(n):
                        act.wait_ge(max_ready, m * U + (n + 1))
                        src, sc = (s_ps[:, n % 2, 0:NS], SCALE) if bias is None else (prob[:, n % NP, :], 1.0)
                        if bias is None:
                            act.wait_ge(t_ready, m * G + (n // merged + 1) * ng)
                        kw = {"accum_out": den[:, n % NP:n % NP + 1]} if diff is not None else {}
                        ins = nc.scalar.activation(prob[:, n % NP, :], src, ACT.Exp, bias=negm[:, n % NP:n % NP + 1],
                                                   scale=sc, **kw)
                        ins.then_inc(p_ready, 1)
                        if bias is None:
                            act.wait_ge(p_ready, m * U + (n + 1))
                            act.sem_inc(s_free, 1)

                    def keep(k):
                        if k % share == 0:
                            act.wait_ge(o_ready, m * J + (k // share + 1))
                        for g in range(ng):
                            j = k * ng + g
                            act.wait_ge(t_ready, m * G + (j + 1 + 2 * ng))
                            x1 = min(4, seen - 4 * g)
                            nc.scalar.activation(
                                probT[:, (k // share) % 2, 4 * g:4 * g + x1, (k % share) * P:(k % share + 1) * P],
                                t_ps[:, j % PTS, 0:x1, :], ACT.Copy).then_inc(t_free, 1)

                    for n in range(merged):
                        exps(n)
                    for k in range(M):
                        for n in range((k + 1) * merged, min((k + 2) * merged, U)):
                            exps(n)
                        keep(k)

            @block.vector
            def _(dve):
                st = Steps(dve, step)
                dve.sem_inc(o_free, PTS)
                if bias is not None:
                    dve.sem_inc(s_free, 2)
                nb = len(bias(0, 0, 0)) if bias is not None else 0
                per = U * (nb if nb else 1) + (0 if diff is not None else J) + (2 * M if diff is not None else 0)
                with dve.Fori(0, pairs) as m:
                    st.enter(m, per)

                    def top(n):
                        t, u = units[n]
                        dve.wait_ge(s_ready, m * U + (n + 1))
                        s = s_ps[:, n % 2, 0:NS]
                        nm = negm[:, n % NP:n % NP + 1]
                        if bias is not None:
                            dve.wait_ge(t_ready, m * G + (n + 1) * ng)
                            b = bias(m, u, t)
                            w = b[0].shape[1]
                            p = prob[:, n % NP, :]
                            ins = nc.vector.scalar_tensor_tensor(out=p[:, 0:w], in0=s[:, 0:w], scalar=SCALE, in1=b[0],
                                                                 op0=ALU.mult, op1=ALU.add)
                            if w < NS:
                                ins = nc.vector.tensor_scalar(p[:, w:NS], s[:, w:NS], SCALE, None, ALU.mult)
                            st.done(ins)
                            dve.sem_inc(s_free, 1)
                            for more in b[1:]:
                                st.done(nc.vector.tensor_tensor(p[:, 0:w], p[:, 0:w], more, ALU.add))
                            nc.vector.tensor_reduce(nm, p, AX.X, ALU.max, negate=True).then_inc(max_ready, 1)
                        else:
                            if n >= 0:
                                dve.wait_ge(p_ready, m * U + max(n + 1 - NP, 0))
                            st.done(nc.vector.tensor_reduce(nm, s, AX.X, ALU.max, negate=True))
                            nc.vector.tensor_scalar(nm, nm, SCALE, None, ALU.mult).then_inc(max_ready, 1)

                    def mix(k):
                        dve.wait_ge(p_ready, m * U + (2 * k + 2))
                        a = (k % 2) * 2
                        st.done(nc.vector.reciprocal(den[:, a:a + 2], den[:, a:a + 2]))
                        nc.vector.tensor_scalar(prob[:, a, :], prob[:, a, :], den[:, a:a + 1], None, ALU.mult)
                        st.done(nc.vector.tensor_scalar(prob[:, a + 1, :], prob[:, a + 1, :], den[:, a + 1:a + 2],
                                                        diff, ALU.mult, ALU.mult))
                        nc.vector.tensor_tensor(prob[:, a, :], prob[:, a, :], prob[:, a + 1, :],
                                                ALU.add).then_inc(d_ready, 1)

                    def result(j):
                        t, u = units[j * share * merged]
                        dve.wait_ge(o_ready, m * J + (j + 3))
                        o = o_ps[:, j % PTS, 0:share * P]
                        cols = slice(t * P, (t + share) * P)
                        if diff is not None:
                            nc.vector.tensor_copy(at(out, m)[:, cols], o).then_inc(o_free, 1)
                            return
                        mine, dens = slice(64 * u, 64 * u + 64), slice(64 - 64 * u, 128 - 64 * u)
                        st.done(nc.vector.reciprocal(rden[mine, j % 2, :], o[dens]))
                        nc.vector.tensor_tensor(at(out, m)[mine, cols], o[mine], rden[mine, j % 2, :],
                                                ALU.mult).then_inc(o_free, 1)

                    for n in range(merged):
                        top(n)
                    for k in range(M):
                        for n in range((k + 1) * merged, min((k + 2) * merged, U)):
                            top(n)
                        if diff is not None:
                            mix(k)
                        if k % share == 0 and k >= share:
                            result(k // share - 1)
                    result(J - 1)
                st.leave(pairs)


def rope_tables(nc, tag, cst, pos_dram, cos, sin):
    MAGIC = 12582912.0
    C1, C2 = 6.28125, 2 * np.pi - 6.28125
    C2a = float(np.float32(np.round(C2 * 2 ** 20) / 2 ** 20))
    C3 = float(np.float32(2 * np.pi - C1 - C2a))
    with Phase(nc, tag) as ph:
        posi = ph.sb("posi", [P, T], I32)
        ang, turns, red = ph.sb("ang", [P, T]), ph.sb("turns", [P, T]), ph.sb("red", [P, T])
        loaded, step, reduced, used = (ph.sem(s) for s in ("loaded", "step", "reduced", "used"))
        with nc.Block() as block:
            @block.sync
            def _(sp):
                sp.dma_start(posi[:], pos_dram.partition_broadcast(P)).then_inc(loaded, 16)

            @block.vector
            def _(dve):
                st = Steps(dve, step)
                dve.wait_ge(loaded, 16)
                st.done(nc.vector.tensor_copy(ang[:], posi[:]))
                st.done(nc.vector.tensor_scalar(ang[:], ang[:], cst["freq"], None, ALU.mult))
                for j, quarter in enumerate((0.0, 0.25)):
                    if j:
                        dve.wait_ge(used, 1)
                    st.done(nc.vector.tensor_scalar(turns[:], ang[:], 1 / (2 * np.pi), quarter, ALU.mult, ALU.add))
                    st.done(nc.vector.tensor_scalar(turns[:], turns[:], MAGIC, None, ALU.add))
                    st.done(nc.vector.tensor_scalar(turns[:], turns[:], MAGIC, None, ALU.subtract))
                    st.done(nc.vector.scalar_tensor_tensor(out=red[:], in0=turns[:], scalar=-C1, in1=ang[:],
                                                           op0=ALU.mult, op1=ALU.add))
                    st.done(nc.vector.scalar_tensor_tensor(out=red[:], in0=turns[:], scalar=-C2a, in1=red[:],
                                                           op0=ALU.mult, op1=ALU.add))
                    st.done(nc.vector.scalar_tensor_tensor(out=red[:], in0=turns[:], scalar=-C3, in1=red[:],
                                                           op0=ALU.mult, op1=ALU.add))
                    st.done(nc.vector.tensor_scalar(red[:], red[:], quarter * 2 * np.pi, 3.1415925, ALU.add, ALU.min))
                    nc.vector.tensor_scalar(red[:], red[:], -3.1415925, None, ALU.max).then_inc(reduced, 1)

            @block.scalar
            def _(act):
                for j, table in enumerate((sin, cos)):
                    act.wait_ge(reduced, j + 1)
                    nc.scalar.activation(table, red[:], ACT.Sin).then_inc(used, 1)


def conv_mixer(nc, tag, cst, a, g, taps, taps_b, ln_g, ln_b):
    K = taps.shape[2]
    half = K // 2
    C = a.shape[1]
    parts = chunks(T)
    with Phase(nc, tag) as ph:
        y = ph.sb("y", [P, C, T])
        sq = ph.sb("sq", [P, C, T])
        sd = ph.sb("sd", [P, T])
        mean_ps, var_ps = ph.ps("mean", [P, T]), ph.ps("var", [P, T])
        gated, conved, mean_ready, centred, squared, var_ready, sd_ready, normed, step = (ph.sem(s) for s in (
            "gated", "conved", "mean_ready", "centred", "squared", "var_ready", "sd_ready", "normed", "step"))
        with nc.Block() as block:
            @block.scalar
            def _(act):
                for c in range(C):
                    nc.scalar.activation(g[:, c, :], g[:, c, :], ACT.Sigmoid).then_inc(gated, 1)
                for c in range(C):
                    act.wait_ge(centred, c + 1)
                    nc.scalar.activation(sq[:, c, :], y[:, c, :], ACT.Square).then_inc(squared, 1)
                act.wait_ge(var_ready, 1)
                nc.scalar.activation(sd[:], var_ps[:], ACT.Sqrt, bias=cst["eps"], scale=1.0 / (C * P)).then_inc(sd_ready, 1)
                for c in range(C):
                    act.wait_ge(normed, c + 1)
                    nc.scalar.activation(a[:, c, :], y[:, c, :], ACT.Silu, bias=ln_b[:, c:c + 1])

            @block.tensor
            def _(pe):
                for o, w in parts:
                    for c in range(C):
                        pe.wait_ge(conved, c + 1)
                        mm = nc.tensor.matmul(mean_ps[:, o:o + w], cst["ones"], y[:, c, o:o + w], start=(c == 0),
                                              stop=(c == C - 1))
                mm.then_inc(mean_ready, 1)
                for o, w in parts:
                    for c in range(C):
                        pe.wait_ge(squared, c + 1)
                        mm = nc.tensor.matmul(var_ps[:, o:o + w], cst["ones"], sq[:, c, o:o + w], start=(c == 0),
                                              stop=(c == C - 1))
                mm.then_inc(var_ready, 1)

            @block.vector
            def _(dve):
                st = Steps(dve, step)
                for c in range(C):
                    dve.wait_ge(gated, c + 1)
                    st.done(nc.vector.tensor_tensor(a[:, c, :], a[:, c, :], g[:, c, :], ALU.mult))
                    st.done(nc.vector.tensor_scalar(y[:, c, :], a[:, c, :], taps[:, c, half:half + 1],
                                                    taps_b[:, c:c + 1], ALU.mult, ALU.add))
                    for t in range(K):
                        if t == half:
                            continue
                        s = t - half
                        lo, hi = max(0, -s), T - max(0, s)
                        st.done(nc.vector.scalar_tensor_tensor(out=y[:, c, lo:hi], in0=a[:, c, lo + s:hi + s],
                                                               scalar=taps[:, c, t:t + 1], in1=y[:, c, lo:hi],
                                                               op0=ALU.mult, op1=ALU.add))
                    dve.sem_inc(conved, 1)
                dve.wait_ge(mean_ready, 1)
                for c in range(C):
                    nc.vector.scalar_tensor_tensor(out=y[:, c, :], in0=mean_ps[:], scalar=-1.0 / (C * P),
                                                   in1=y[:, c, :], op0=ALU.mult, op1=ALU.add).then_inc(centred, 1)
                dve.wait_ge(sd_ready, 1)
                st.done(nc.vector.reciprocal(sd[:], sd[:]))
                for c in range(C):
                    nc.vector.scalar_tensor_tensor(out=y[:, c, :], in0=y[:, c, :], scalar=ln_g[:, c:c + 1],
                                                   in1=sd[:], op0=ALU.mult, op1=ALU.mult).then_inc(normed, 1)


def ffn_up(nc, tag, w_dram, src, hidden):
    K = len(src)
    W = K * 2 * P
    parts = chunks(T)
    with Phase(nc, tag) as ph:
        w = ph.sb("w", [P, 2, W + 8])
        y = ph.sb("y", [P, 2, T])
        acc = ph.ps("acc", [P, 2, 2, T // 2])
        acc2 = ph.ps("acc2", [P, 2, 2, T // 2])
        accs = (acc, acc2)
        w_ready = [ph.sem("w_ready0"), ph.sem("w_ready1")]
        mm_done, middle, conved, silu_done, hid_done, step = (ph.sem(s) for s in (
            "mm_done", "middle", "conved", "silu_done", "hid_done", "step"))
        with nc.Block() as block:
            @block.sync
            def _(sp):
                with sp.Fori(0, KF // 2) as i:
                    for u in range(2):
                        sp.wait_ge(hid_done, i * 2 + (u + 1))
                        sp.dma_start(w[:, u], w_dram[bass.ds(i * 2 + u, 1)].rearrange(
                            "a p n -> p (a n)")).then_inc(w_ready[u], 16)

            @block.tensor
            def _(pe):
                with pe.Fori(0, KF // 2) as i:
                    for u in range(2):
                        pe.wait_ge(w_ready[u], i * 16 + 16)
                        pe.wait_ge(hid_done, i * 2 + (u + 1))
                        for s in range(2):
                            for c, (a, width) in enumerate(parts):
                                for k in range(K):
                                    mm = nc.tensor.matmul(accs[u][:, s, c, :], w[:, u, (2 * k + s) * P:(2 * k + s + 1) * P],
                                                          src[k][:, a:a + width], start=(k == 0), stop=(k == K - 1))
                            mm.then_inc(mm_done, 1)

            @block.scalar
            def _(act):
                with act.Fori(0, KF // 2) as i:
                    for u in range(2):
                        act.wait_ge(hid_done, i * 2 + (u + 2))
                        for s in range(2):
                            act.wait_ge(mm_done, i * 4 + (2 * u + s + 1))
                            f = accs[u][:, s].rearrange("p c n -> p (c n)")
                            nc.scalar.activation(y[:, s, :], f, ACT.Identity, bias=w[:, u, W + 4 * s + 3:W + 4 * s + 4],
                                                 scale=w[:, u, W + 4 * s + 1:W + 4 * s + 2]).then_inc(middle, 1)
                        act.wait_ge(conved, i * 2 + (u + 1))
                        nc.scalar.activation(y[:, 0, :], y[:, 0, :], ACT.Silu).then_inc(silu_done, 1)

            @block.vector
            def _(dve):
                st = Steps(dve, step)
                dve.sem_inc(hid_done, 2)
                with dve.Fori(0, KF // 2) as i:
                    st.enter(i, 8)
                    for u in range(2):
                        for s in range(2):
                            dve.wait_ge(middle, i * 4 + (2 * u + s + 1))
                            f = accs[u][:, s].rearrange("p c n -> p (c n)")
                            st.done(nc.vector.scalar_tensor_tensor(out=y[:, s, 1:T], in0=f[:, 0:T - 1],
                                                                   scalar=w[:, u, W + 4 * s:W + 4 * s + 1],
                                                                   in1=y[:, s, 1:T], op0=ALU.mult, op1=ALU.add))
                            st.done(nc.vector.scalar_tensor_tensor(out=y[:, s, 0:T - 1], in0=f[:, 1:T],
                                                                   scalar=w[:, u, W + 4 * s + 2:W + 4 * s + 3],
                                                                   in1=y[:, s, 0:T - 1], op0=ALU.mult, op1=ALU.add))
                            if s == 0:
                                dve.sem_inc(conved, 1)
                        dve.wait_ge(silu_done, i * 2 + (u + 1))
                        nc.vector.tensor_tensor(at(hidden, i * 2 + u), y[:, 0, :], y[:, 1, :], ALU.mult).then_inc(hid_done, 1)
                st.leave(KF // 2)




def modulation(nc, tag, cst, vecs, din, mod, a1, ac, a2, ac_shift, neg_lam, sub_g):
    with Phase(nc, tag + "s") as ph:
        cs = ph.sb("cs", [P, 2, KD])
        act_c = ph.sb("act_c", [P, KD, 2])
        lam = ph.sb("lam", [P, 2])
        sum_ps = ph.ps("sum", [P, 2])
        silu_done, step, prod_ready, sum_ready, exp_ready, ready = (ph.sem(s) for s in (
            "silu_done", "step", "prod_ready", "sum_ready", "exp_ready", "ready"))
        with nc.Block() as block:
            @block.scalar
            def _(act):
                nc.scalar.activation(cs[:].rearrange("p a k -> p (a k)"), vecs["c"], ACT.Silu).then_inc(silu_done, 1)
                act.wait_ge(sum_ready, 1)
                nc.scalar.activation(lam[:], sum_ps[:], ACT.Exp).then_inc(exp_ready, 1)

            @block.tensor
            def _(pe):
                pe.wait_ge(prod_ready, 1)
                nc.tensor.matmul(sum_ps[:], cst["ones"], lam[:], start=True, stop=True).then_inc(sum_ready, 1)

            @block.vector
            def _(dve):
                st = Steps(dve, step)
                l = vecs["lam"]
                nc.vector.tensor_tensor(lam[:, 0:1], l[:, 0:1], l[:, 1:2], ALU.mult)
                nc.vector.tensor_tensor(lam[:, 1:2], l[:, 2:3], l[:, 3:4], ALU.mult).then_inc(prod_ready, 1)
                dve.wait_ge(silu_done, 1)
                for a in range(2):
                    nc.vector.tensor_copy(act_c[:, :, a:a + 1], cs[:, a, :].unsqueeze(2))
                nc.vector.tensor_scalar(sub_g, vecs["sub_g"], 0.8, None, ALU.mult)
                dve.wait_ge(exp_ready, 1)
                st.done(nc.vector.tensor_tensor(neg_lam, lam[:, 1:2], lam[:, 0:1], ALU.subtract))
                nc.vector.tensor_scalar(neg_lam, neg_lam, -0.2, None, ALU.add)
        project(nc, tag, din["w_mod"], cols(act_c), 2, 6 * KD, dst=mod)
    with Phase(nc, tag + "g") as ph:
        step = ph.sem("step")
        with nc.Block() as block:
            @block.vector
            def _(dve):
                st = Steps(dve, step)
                for a in range(2):
                    st.done(nc.vector.tensor_tensor(mod[:, :, a], mod[:, :, a], vecs["b_mod"], ALU.add))
                for o, g, j, a in ((a1, "g1", 1, 0), (ac, "g1", 1, 1), (a2, "g2", 4, 0)):
                    nc.vector.scalar_tensor_tensor(out=o, in0=mod[:, j * KD:(j + 1) * KD, a], scalar=1.0,
                                                   in1=vecs[g], op0=ALU.add, op1=ALU.mult)
                nc.vector.tensor_copy(ac_shift, mod[:, 0:KD, 1])


def gla_decay(nc, tag, cst, w_dec, b_dec, low, n, decay):
    parts = chunks(n)
    with Phase(nc, tag) as ph:
        z = ph.sb("z", [P, 2, n])
        e = ph.sb("e", [P, 2, n])
        z_ps = ph.ps("z_ps", [P, 2, len(parts) * BANK])
        z_ready, z_kept, log_ready, sum_ready, step, own = (ph.sem(s) for s in (
            "z_ready", "z_kept", "log_ready", "sum_ready", "step", "own"))
        with nc.Block() as block:
            @block.tensor
            def _(pe):
                for d in range(2):
                    for a, w in parts:
                        mm = nc.tensor.matmul(z_ps[:, d, a:a + w], w_dec[0:32, d, :], low[0:32, a:a + w], start=True,
                                              stop=True)
                    mm.then_inc(z_ready, 1)

            @block.scalar
            def _(act):
                st = Steps(act, own)
                for d in range(2):
                    act.wait_ge(z_ready, d + 1)
                    st.done(nc.scalar.activation(z[:, d, :], z_ps[:, d, 0:n], ACT.Identity, bias=b_dec[:, d:d + 1]))
                    act.sem_inc(z_kept, 1)
                    st.done(nc.scalar.activation(e[:, d, :], z[:, d, :], ACT.Abs))
                    st.done(nc.scalar.activation(e[:, d, :], e[:, d, :], ACT.Exp, scale=-1.0))
                    nc.scalar.activation(e[:, d, :], e[:, d, :], ACT.Ln, bias=cst["one"]).then_inc(log_ready, 1)
                for d in range(2):
                    act.wait_ge(sum_ready, d + 1)
                    nc.scalar.activation(decay[:, d, :], z[:, d, :], ACT.Exp, scale=1.0 / 16)

            @block.vector
            def _(dve):
                for d in range(2):
                    dve.wait_ge(log_ready, d + 1)
                    nc.vector.scalar_tensor_tensor(out=z[:, d, :], in0=z[:, d, :], scalar=0.0, in1=e[:, d, :],
                                                   op0=ALU.min, op1=ALU.subtract).then_inc(sum_ready, 1)


def gla_context(nc, tag, cst, k, vb, decay, state):
    n = NCTX
    with Phase(nc, tag) as ph:
        tail = ph.sb("tail", [P, 2, n])
        zero = ph.sb("zero", [P, n])
        kt = ph.sb("kt", [P, 2, 2, P])
        t_ps = ph.ps("t_ps", [P, 2, 2, P])
        s_ps = ph.ps("s_ps", [P, 2, 4 * 64])
        scaled, turned, kept, done, step = (ph.sem(s) for s in ("scaled", "turned", "kept", "done", "step"))
        with nc.Block() as block:
            @block.vector
            def _(dve):
                st = Steps(dve, step)
                nc.vector.memset(zero[:], 0.0)
                nc.vector.memset(tail[:, 0, n - 1:n], 1.0)
                st.done(nc.vector.memset(tail[:, 1, 0:1], 1.0))
                nc.vector.tensor_tensor_scan(tail[:, 0, n - 2::-1], decay[:, 0, n - 1:0:-1], zero[:, 1:n], 1.0,
                                             ALU.mult, ALU.add)
                st.done(nc.vector.tensor_tensor_scan(tail[:, 1, 1:n], decay[:, 1, 0:n - 1], zero[:, 1:n], 1.0,
                                                     ALU.mult, ALU.add))
                for d in range(2):
                    nc.vector.tensor_tensor(tail[:, d, :], tail[:, d, :], k, ALU.mult).then_inc(scaled, 1)
                dve.wait_ge(turned, 1)
                nc.vector.tensor_copy(kt[:], t_ps[:]).then_inc(kept, 1)
                dve.wait_ge(done, 1)
                for d in range(2):
                    for h in range(4):
                        r = slice(32 * h, 32 * h + 32)
                        nc.vector.tensor_copy(state[r, :, d], s_ps[r, d, 64 * h:64 * h + 64])

            @block.tensor
            def _(pe):
                pe.wait_ge(scaled, 2)
                for d in range(2):
                    for t in range(2):
                        mm = nc.tensor.transpose(t_ps[:, d, t, :], tail[:, d, t * P:(t + 1) * P], cst["ident"])
                mm.then_inc(turned, 1)
                pe.wait_ge(kept, 1)
                for d in range(2):
                    for t in range(2):
                        mm = nc.tensor.matmul(s_ps[:, d, :], kt[:, d, t, :], vb[:, t, :], start=(t == 0), stop=(t == 1))
                mm.then_inc(done, 1)


def gla_scan(nc, tag, cst, q, k, decay, state, v_dram, o_dram):
    DV = 64
    with Phase(nc, tag) as ph:
        vb = ph.sb("vb", [P, 2, T])
        kv = ph.sb("kv", [P, 2, T])
        s = ph.sb("s", [P, 2, 2, T])
        qs = ph.sb("qs", [P, 2, T])
        init = ph.sb("init", [P, 2, 2])
        orow = ph.sb("orow", [4, 2, T])
        o_ps = ph.ps("o_ps", [P, 2, T])
        v_ready = [ph.sem("v_ready0"), ph.sem("v_ready1")]
        stored = [ph.sem("stored0"), ph.sem("stored1")]
        kv_ready, scanned, summed, weighted, o_ready, o_kept, step, qscaled = (ph.sem(x) for x in (
            "kv_ready", "scanned", "summed", "weighted", "o_ready", "o_kept", "step", "qscaled"))
        with nc.Block() as block:
            @block.sync
            def _(sp):
                with sp.Fori(0, DV // 2) as i:
                    for u in range(2):
                        sp.wait_ge(kv_ready, i * 2 + (u + 1))
                        for h in range(4):
                            row = v_dram[h, bass.ds(i * 2 + u, 1), :].rearrange("a t -> (a t)")
                            sp.dma_start(vb[32 * h:32 * h + 32, u, :], row.partition_broadcast(32)).then_inc(v_ready[u], 16)

            @block.gpsimd
            def _(pool):
                pool.sem_inc(kv_ready, 2)
                with pool.Fori(0, DV // 2) as i:
                    def outer(j, u):
                        pool.wait_ge(v_ready[u], j * 64 + 64)
                        pool.wait_ge(scanned, j * 2 + (u + 1))
                        nc.gpsimd.tensor_tensor(kv[:, u, :], k, vb[:, u, :], ALU.mult).then_inc(kv_ready, 1)

                    for u in range(2):
                        outer(i, u)
                    for u in range(2):
                        pool.wait_ge(scanned, i * 2 + (u + 3))
                        nc.gpsimd.tensor_tensor(s[:, u, 0, :], s[:, u, 0, :], s[:, u, 1, :], ALU.add).then_inc(summed, 1)

            @block.vector
            def _(dve):
                st = Steps(dve, step)
                dve.sem_inc(scanned, 2)
                st.done(nc.vector.tensor_scalar(q, q, 32.0 ** -0.5, None, ALU.mult))
                with dve.Fori(0, DV // 2) as i:
                    st.enter(i, 2)

                    def scan(u):
                        dve.wait_ge(kv_ready, i * 2 + (u + 3))
                        st.done(nc.vector.tensor_copy(init[:, u, :], at(state, i * 2 + u)))
                        nc.vector.tensor_tensor_scan(s[:, u, 0, :], decay[:, 0, :], kv[:, u, :], init[:, u, 0:1],
                                                     ALU.mult, ALU.add)
                        nc.vector.tensor_tensor_scan(s[:, u, 1, ::-1], decay[:, 1, ::-1], kv[:, u, ::-1],
                                                     init[:, u, 1:2], ALU.mult, ALU.add).then_inc(scanned, 1)

                    def weigh(u):
                        dve.wait_ge(summed, i * 2 + (u + 1))
                        dve.wait_ge(o_ready, i * 2 + (u + 1))
                        nc.vector.tensor_tensor(qs[:, u, :], s[:, u, 0, :], q, ALU.mult).then_inc(weighted, 1)

                    scan(0)
                    scan(1)
                    weigh(0)
                    weigh(1)
                st.leave(DV // 2)

            @block.tensor
            def _(pe):
                pe.sem_inc(o_ready, 2)
                with pe.Fori(0, DV // 2) as i:
                    for u in range(2):
                        pe.wait_ge(weighted, i * 2 + (u + 1))
                        pe.wait_ge(o_kept, i * 2 + (u + 1))
                        for a, w in chunks(T):
                            mm = nc.tensor.matmul(o_ps[0:4, u, a:a + w], cst["heads32"], qs[:, u, a:a + w], start=True,
                                                  stop=True)
                        mm.then_inc(o_ready, 1)

            @block.scalar
            def _(act):
                act.sem_inc(o_kept, 2)
                act.sem_inc(stored[0], 16)
                act.sem_inc(stored[1], 16)
                with act.Fori(0, DV // 2) as i:
                    for u in range(2):
                        act.wait_ge(o_ready, i * 2 + (u + 3))
                        act.wait_ge(stored[u], i * 16 + 16)
                        nc.scalar.activation(orow[:, u, :], o_ps[0:4, u, :], ACT.Copy).then_inc(o_kept, 1)
                        act.wait_ge(o_kept, i * 2 + (u + 3))
                        act.dma_start(o_dram[:, bass.ds(i * 2 + u, 1), :].rearrange("h a t -> h (a t)"),
                                      orow[:, u, :]).then_inc(stored[u], 16)
                for u in range(2):
                    act.wait_ge(stored[u], 16 + 16 * (DV // 2))


def gated(nc, tag, x, gate):
    with Phase(nc, tag) as ph:
        silu_done = ph.sem("silu_done")
        with nc.Block() as block:
            @block.scalar
            def _(act):
                for c in range(x.shape[1]):
                    nc.scalar.activation(gate[:, c, :], gate[:, c, :], ACT.Silu).then_inc(silu_done, 1)

            @block.vector
            def _(dve):
                for c in range(x.shape[1]):
                    dve.wait_ge(silu_done, c + 1)
                    nc.vector.tensor_tensor(x[:, c, :], x[:, c, :], gate[:, c, :], ALU.mult)


E_ = 32
NB = 48
TT = T // P


def router(nc, tag, cst, vecs, din, n, h2_dram, r):
    with Phase(nc, tag) as ph:
        w = ph.sb("w", [P, KD, 36])
        lgT = ph.sb("lgT", [36, T])
        row = ph.sb("row", [P, 2, D])
        lg = ph.sb("lg", [P, TT, 36])
        pen, le, cand, eq = (ph.sb(x, [P, TT, E_]) for x in ("pen", "le", "cand", "eq"))
        oh = ph.sb("oh", [P, 2, TT, E_])
        both = ph.sb("both", [P, TT, E_])
        g4, g4b = ph.sb("g4", [P, TT, 4]), ph.sb("g4b", [P, TT, 4])
        c1, top, low, pg = (ph.sb(x, [P, TT]) for x in ("c1", "top", "low", "pg"))
        base, nblk, incl, onesr = (ph.sb(x, [P, E_]) for x in ("base", "nblk", "incl", "onesr"))
        cmp = ph.sb("cmp", [P, NB, E_])
        bex = ph.sb("bex", [P, NB])
        slotf, blkf = ph.sb("slotf", [P, 2, TT]), ph.sb("blkf", [P, 2, TT])
        l_ps = ph.ps("l_ps", [P, T])
        lt_ps = ph.ps("lt_ps", [P, TT, 36])
        r_ps = ph.ps("r_ps", [P, 2, T // 2])
        pre_ps = ph.ps("pre_ps", [P, TT, E_])
        tot_ps = ph.ps("tot_ps", [P, E_])
        loaded, l_ready, l_kept, lt_ready, lt_kept, row_ready, row_kept, stored, stepv, exp_a, exp_a_done = (
            ph.sem(x) for x in ("loaded", "l_ready", "l_kept", "lt_ready", "lt_kept", "row_ready", "row_kept", "stored",
                                "step", "exp_a", "exp_a_done"))
        both_ready, pre_ready, row_stored = ph.sem("both_ready"), ph.sem("pre_ready"), [ph.sem("row_stored0"), ph.sem("row_stored1")]
        with nc.Block() as block:
            @block.sync
            def _(sp):
                sp.dma_start(w[:], din["w_route"]).then_inc(loaded, 16)
                for t in range(TT):
                    sp.wait_ge(row_kept, 2 * (t + 1))
                    sp.dma_start(h2_dram[t * P:(t + 1) * P, :], row[:, t % 2, :]).then_inc(row_stored[t % 2], 16)
                for u in range(2):
                    sp.wait_ge(row_stored[u], 16 * TT // 2)

            @block.tensor
            def _(pe):
                pe.wait_ge(loaded, 16)
                for a, wd in chunks(T):
                    for k in range(KD):
                        mm = nc.tensor.matmul(l_ps[0:36, a:a + wd], w[:, k, :], n[:, k, a:a + wd], start=(k == 0),
                                              stop=(k == KD - 1))
                mm.then_inc(l_ready, 1)
                pe.wait_ge(l_kept, 1)
                for t in range(TT):
                    mm = nc.tensor.transpose(lt_ps[:, t, :], lgT[:, t * P:(t + 1) * P], cst["ident"][0:36, 0:36])
                mm.then_inc(lt_ready, 1)
                for t in range(TT):
                    for half in range(2):
                        j = 2 * t + half
                        if j >= 2:
                            pe.wait_ge(row_kept, j - 1)
                        for k in range(4):
                            mm = nc.tensor.transpose(r_ps[:, half, k * P:(k + 1) * P],
                                                     n[:, half * 4 + k, t * P:(t + 1) * P], cst["ident"])
                        mm.then_inc(row_ready, 1)
                pe.wait_ge(both_ready, 1)
                for t in range(TT):
                    for s in range(t):
                        nc.tensor.matmul(pre_ps[:, t, :], cst["ones"], both[:, s, :], start=(s == 0), stop=False)
                    nc.tensor.matmul(pre_ps[:, t, :], cst["before"], both[:, t, :], start=(t == 0), stop=True)
                for t in range(TT):
                    mm = nc.tensor.matmul(tot_ps[:], cst["ones"], both[:, t, :], start=(t == 0), stop=(t == TT - 1))
                mm.then_inc(pre_ready, 1)

            @block.scalar
            def _(act):
                act.wait_ge(l_ready, 1)
                nc.scalar.activation(lgT[:], l_ps[0:36, :], ACT.Identity, bias=vecs["b_route"][0:36]).then_inc(l_kept, 1)
                for t in range(TT):
                    for half in range(2):
                        j = 2 * t + half
                        if half == 0 and t >= 2:
                            act.wait_ge(row_stored[t % 2], 16 * (t // 2))
                        act.wait_ge(row_ready, j + 1)
                        nc.scalar.activation(row[:, t % 2, half * 512:half * 512 + 512], r_ps[:, half, :],
                                             ACT.Copy).then_inc(row_kept, 1)
                for j, (x, flat) in enumerate(((g4, "p t g -> p (t g)"), (top, None))):
                    act.wait_ge(exp_a, j + 1)
                    y = x[:].rearrange(flat) if flat else x[:]
                    nc.scalar.activation(y, y, ACT.Exp).then_inc(exp_a_done, 1)

            @block.vector
            def _(dve):
                st = Steps(dve, stepv)
                V = nc.vector

                def spread(x, m):
                    return x.unsqueeze(2).broadcast_to([P, TT, m])

                def choose(logits, m, onehot, best, tmp):
                    index = cst["index"][:, 0:m].unsqueeze(1).broadcast_to([P, TT, m])
                    st.done(V.tensor_reduce(best, logits, AX.X, ALU.max))
                    st.done(V.tensor_tensor(tmp, logits, spread(best, m), ALU.is_equal))
                    st.done(V.tensor_tensor(tmp, tmp, index, ALU.mult))
                    st.done(V.tensor_reduce(c1[:], tmp, AX.X, ALU.min))
                    st.done(V.tensor_tensor(onehot, tmp, spread(c1[:], m), ALU.is_equal))

                dve.wait_ge(lt_ready, 1)
                st.done(V.tensor_copy(lg[:], lt_ps[:]))
                lgG = lg[:, :, 0:4]
                choose(lgG, 4, g4b[:], pg[:], g4[:])
                st.done(V.tensor_tensor(g4[:], lgG, spread(pg[:], 4), ALU.subtract))
                dve.sem_inc(exp_a, 1)
                st.done(V.tensor_scalar(g4b[:], g4b[:], -1.0, 1e30, ALU.add, ALU.mult))
                for g in range(4):
                    st.done(V.tensor_tensor(le[:, :, g * 8:g * 8 + 8], lg[:, :, 4 + g * 8:12 + g * 8],
                                            g4b[:, :, g:g + 1].broadcast_to([P, TT, 8]), ALU.add))
                choose(le[:], E_, oh[:, 0], top[:], cand[:])
                st.done(V.scalar_tensor_tensor(out=pen[:], in0=oh[:, 0], scalar=-2e30, in1=le[:], op0=ALU.mult,
                                               op1=ALU.add))
                choose(pen[:], E_, oh[:, 1], low[:], cand[:])
                st.done(V.tensor_tensor(top[:], low[:], top[:], ALU.subtract))
                dve.sem_inc(exp_a, 1)
                st.done(V.tensor_tensor(both[:], oh[:, 0], oh[:, 1], ALU.add))
                dve.sem_inc(both_ready, 1)
                dve.wait_ge(exp_a_done, 2)
                st.done(V.tensor_reduce(pg[:], g4[:], AX.X, ALU.add))
                st.done(V.tensor_scalar(low[:], top[:], 1.0, None, ALU.add))
                st.done(V.tensor_tensor(low[:], low[:], pg[:], ALU.mult))
                st.done(V.reciprocal(r["gate"][:, 0], low[:]))
                st.done(V.tensor_tensor(r["gate"][:, 1], r["gate"][:, 0], top[:], ALU.mult))
                dve.wait_ge(pre_ready, 1)
                st.done(V.tensor_scalar(nblk[:], tot_ps[:], 127.0, 1.0 / P, ALU.add, ALU.mult))
                st.done(V.tensor_scalar(nblk[:], nblk[:], -0.498, None, ALU.add))
                st.done(V.tensor_scalar(nblk[:], nblk[:], 12582912.0, None, ALU.add))
                st.done(V.tensor_scalar(nblk[:], nblk[:], 12582912.0, None, ALU.subtract))
                st.done(V.memset(onesr[:], 1.0))
                st.done(V.tensor_tensor_scan(incl[:], onesr[:], nblk[:], 0.0, ALU.mult, ALU.add))
                st.done(V.tensor_tensor(base[:], incl[:], nblk[:], ALU.subtract))
                st.done(V.tensor_scalar(base[:], base[:], float(P), None, ALU.mult))
                st.done(V.tensor_tensor(le[:], pre_ps[:], base[:].unsqueeze(1).broadcast_to([P, TT, E_]), ALU.add))
                for a in range(2):
                    st.done(V.tensor_tensor(cand[:], oh[:, a], le[:], ALU.mult))
                    st.done(V.tensor_reduce(slotf[:, a], cand[:], AX.X, ALU.add))
                st.done(V.tensor_copy(r["slot"], slotf[:]))
                st.done(V.tensor_scalar(blkf[:], slotf[:], 1.0 / P, -0.498, ALU.mult, ALU.add))
                st.done(V.tensor_scalar(blkf[:], blkf[:], 12582912.0, None, ALU.add))
                st.done(V.tensor_scalar(blkf[:], blkf[:], 12582912.0, 1.0 - P * NB, ALU.subtract, ALU.mult))
                st.done(V.scalar_tensor_tensor(out=slotf[:], in0=slotf[:], scalar=float(NB), in1=blkf[:],
                                               op0=ALU.mult, op1=ALU.add))
                st.done(V.tensor_copy(r["place"], slotf[:]))
                st.done(V.tensor_tensor(cmp[:], incl[:].unsqueeze(1).broadcast_to([P, NB, E_]),
                                        cst["block"].unsqueeze(2).broadcast_to([P, NB, E_]), ALU.is_le))
                st.done(V.tensor_reduce(bex[:], cmp[:], AX.X, ALU.add))
                st.done(V.tensor_scalar(bex[:], bex[:], float(E_ - 1), None, ALU.min))
                st.done(V.tensor_copy(r["block"], bex[:]))


def dispatch(nc, tag, cst, r, ids_dram, ids):
    with Phase(nc, tag) as ph:
        token = ph.sb("token", [P, TT], I32)
        zero = ph.sb("zero", [P, NB], I32)
        made, cleared, scattered, read = (ph.sem(x) for x in ("made", "cleared", "scattered", "read"))
        with nc.Block() as block:
            @block.gpsimd
            def _(pool):
                nc.gpsimd.memset(zero[:], 0).then_inc(made, 1)
                nc.gpsimd.iota(token[:], [[P, TT]], base=0, channel_multiplier=1).then_inc(made, 1)
                pool.wait_ge(made, 2)
                pool.dma_start(ids_dram.rearrange("(p b) a -> p (b a)", b=NB), zero[:]).then_inc(cleared, 16)
                pool.wait_ge(cleared, 16)
                for a in range(2):
                    for t in range(TT):
                        pool.indirect_dma_start(ids_dram, bass.IndirectOffsetOnAxis(ap=r["place"][:, a, t:t + 1], axis=0),
                                                token[:, t:t + 1], None).then_inc(scattered, 16)
                pool.wait_ge(scattered, 16 * 2 * TT)
                pool.dma_start(ids, ids_dram.rearrange("(p b) a -> p (b a)", b=NB)).then_inc(read, 16)
                pool.wait_ge(read, 16)


def experts(nc, tag, cst, din, r, ids, h2_dram, y_dram):
    H = 512
    KH = H // P
    with Phase(nc, tag) as ph:
        wu = ph.sb("wu", [P, 2, KD, 2 * H])
        wd = ph.sb("wd", [P, 2, KH, D])
        xb = ph.sb("xb", [P, 2, D])
        xT = ph.sb("xT", [P, 2, KD, P])
        idx = ph.sb("idx", [P, 2], I32)
        hid = ph.sb("hid", [P, 2, H])
        hT = ph.sb("hT", [P, KH, P])
        y = ph.sb("y", [P, 2, D])
        x_ps = ph.ps("x_ps", [P, KD, P])
        up_ps = ph.ps("up_ps", [P, 2, H])
        h_ps = ph.ps("h_ps", [P, KH, P])
        y_ps = ph.ps("y_ps", [P, D])
        u_ready = [ph.sem("u_ready0"), ph.sem("u_ready1")]
        d_ready = [ph.sem("d_ready0"), ph.sem("d_ready1")]
        x_ready = [ph.sem("x_ready0"), ph.sem("x_ready1")]
        stored = [ph.sem("stored0"), ph.sem("stored1")]
        idx_seen = ph.sem("idx_seen")
        idx_set, turned, xT_ready, up_done, silu_done, hid_ready, h_turned, hT_ready, y_done, y_kept = (ph.sem(x) for x in (
            "idx_set", "turned", "xT_ready", "up_done", "silu_done", "hid_ready", "h_turned", "hT_ready", "y_done",
            "y_kept"))
        with nc.Block() as block:
            @block.sync
            def _(sp):
                with sp.Fori(0, NB // 2) as i:
                    for u in range(2):
                        e = sp.value_load(r["block"][0:1, bass.ds(i * 2 + u, 1)], min_val=0, max_val=E_ - 1)
                        sp.wait_ge(up_done, i * 2 + (u + 1))
                        sp.dma_start(wu[:, u], din["w_eup"][bass.ds(e, 1)].rearrange(
                            "a (k p) n -> p (a k) n", p=P)).then_inc(u_ready[u], 16)
                        sp.wait_ge(y_done, i * 2 + (u + 1))
                        sp.dma_start(wd[:, u], din["w_edown"][bass.ds(e, 1)].rearrange(
                            "a (k p) n -> p (a k) n", p=P)).then_inc(d_ready[u], 16)

            @block.gpsimd
            def _(pool):
                with pool.Fori(0, NB // 2) as i:
                    for u in range(2):
                        pool.wait_ge(turned, i * 2 + (u + 1))
                        nc.gpsimd.tensor_copy(idx[:, u:u + 1], ids[:, bass.ds(i * 2 + u, 1)]).then_inc(idx_set, 1)
                        pool.wait_ge(idx_set, i * 2 + (u + 1))
                        pool.sem_inc(idx_seen, 1)
                        pool.indirect_dma_start(xb[:, u, :], None, h2_dram,
                                                bass.IndirectOffsetOnAxis(ap=idx[:, u:u + 1], axis=0)
                                                ).then_inc(x_ready[u], 16)

            @block.tensor
            def _(pe):
                pe.sem_inc(turned, 2)
                pe.sem_inc(up_done, 2)
                pe.sem_inc(y_done, 2)

                def turn(i, u):
                    pe.wait_ge(x_ready[u], i * 16 + 16)
                    pe.wait_ge(xT_ready, i * 2 + u)
                    for k in range(KD):
                        mm = nc.tensor.transpose(x_ps[:, k, :], xb[:, u, k * P:(k + 1) * P], cst["ident"])
                    mm.then_inc(turned, 1)

                def up(i, u):
                    pe.wait_ge(xT_ready, i * 2 + (u + 1))
                    pe.wait_ge(u_ready[u], i * 16 + 16)
                    pe.wait_ge(hid_ready, i * 2 + u)
                    for s in range(2):
                        for k in range(KD):
                            mm = nc.tensor.matmul(up_ps[:, s, :], xT[:, u, k, :], wu[:, u, k, s * H:(s + 1) * H],
                                                  start=(k == 0), stop=(k == KD - 1))
                    mm.then_inc(up_done, 1)

                def down(i, u):
                    pe.wait_ge(hid_ready, i * 2 + (u + 1))
                    pe.wait_ge(hT_ready, i * 2 + u)
                    for k in range(KH):
                        mm = nc.tensor.transpose(h_ps[:, k, :], hid[:, 1, k * P:(k + 1) * P], cst["ident"])
                    mm.then_inc(h_turned, 1)
                    pe.wait_ge(hT_ready, i * 2 + (u + 1))
                    pe.wait_ge(d_ready[u], i * 16 + 16)
                    pe.wait_ge(y_kept, i * 2 + u)
                    for a, w in chunks(D):
                        for k in range(KH):
                            mm = nc.tensor.matmul(y_ps[:, a:a + w], hT[:, k, :], wd[:, u, k, a:a + w], start=(k == 0),
                                                  stop=(k == KH - 1))
                    mm.then_inc(y_done, 1)

                turn(0, 0)
                with pe.Fori(0, NB // 2 - 1) as i:
                    up(i, 0)
                    turn(i, 1)
                    down(i, 0)
                    up(i, 1)
                    turn(i + 1, 0)
                    down(i, 1)
                last = NB // 2 - 1
                up(last, 0)
                turn(last, 1)
                down(last, 0)
                up(last, 1)
                down(last, 1)

            @block.scalar
            def _(act):
                act.sem_inc(stored[0], 16)
                act.sem_inc(stored[1], 16)

                def keep_x(i, u):
                    act.wait_ge(turned, i * 2 + (u + 3))
                    act.wait_ge(up_done, i * 2 + (u + 1))
                    nc.scalar.activation(xT[:, u], x_ps[:], ACT.Copy).then_inc(xT_ready, 1)

                def silu(i, u):
                    act.wait_ge(up_done, i * 2 + (u + 3))
                    act.wait_ge(hid_ready, i * 2 + u)
                    nc.scalar.activation(hid[:, 0, :], up_ps[:, 0, :], ACT.Silu).then_inc(silu_done, 1)

                def keep_y(i, u):
                    act.wait_ge(y_done, i * 2 + (u + 3))
                    act.wait_ge(stored[u], i * 16 + 16)
                    nc.scalar.activation(y[:, u, :], y_ps[:], ACT.Copy).then_inc(y_kept, 1)
                    act.wait_ge(y_kept, i * 2 + (u + 1))
                    act.dma_start(y_dram[bass.ds(i * 2 + u, 1)].rearrange("a p n -> p (a n)"),
                                  y[:, u, :]).then_inc(stored[u], 16)

                keep_x(0, 0)
                with act.Fori(0, NB // 2 - 1) as i:
                    silu(i, 0)
                    keep_x(i, 1)
                    keep_y(i, 0)
                    silu(i, 1)
                    keep_x(i + 1, 0)
                    keep_y(i, 1)
                last = NB // 2 - 1
                silu(last, 0)
                keep_x(last, 1)
                keep_y(last, 0)
                silu(last, 1)
                keep_y(last, 1)
                for u in range(2):
                    act.wait_ge(stored[u], 16 + 16 * (NB // 2))

            @block.vector
            def _(dve):
                with dve.Fori(0, NB // 2) as i:
                    for u in range(2):
                        dve.wait_ge(silu_done, i * 2 + (u + 1))
                        dve.wait_ge(h_turned, i * 2 + u)
                        nc.vector.tensor_tensor(hid[:, 1, :], hid[:, 0, :], up_ps[:, 1, :], ALU.mult).then_inc(hid_ready, 1)
                        dve.wait_ge(h_turned, i * 2 + (u + 1))
                        dve.wait_ge(y_done, i * 2 + (u + 2))
                        nc.vector.tensor_copy(hT[:], h_ps[:]).then_inc(hT_ready, 1)


def combine(nc, tag, cst, r, y_dram, gate5, h):
    with Phase(nc, tag) as ph:
        f = ph.sb("f", [P, 2, 2, D])
        f_ps = ph.ps("f_ps", [P, 2, 4, P])
        got = [ph.sem("got0"), ph.sem("got1")]
        mixed, turned, added, step = (ph.sem(x) for x in ("mixed", "turned", "added", "step"))
        with nc.Block() as block:
            @block.gpsimd
            def _(pool):
                for t in range(TT):
                    if t >= 2:
                        pool.wait_ge(turned, 2 * (t - 1))
                    for a in range(2):
                        pool.indirect_dma_start(f[:, t % 2, a, :], None, y_dram,
                                                bass.IndirectOffsetOnAxis(ap=r["slot"][:, a, t:t + 1], axis=0)
                                                ).then_inc(got[t % 2], 16)

            @block.vector
            def _(dve):
                st = Steps(dve, step)
                for t in range(TT):
                    dve.wait_ge(got[t % 2], 32 * (t // 2 + 1))
                    st.done(nc.vector.tensor_scalar(f[:, t % 2, 0, :], f[:, t % 2, 0, :], r["gate"][:, 0, t:t + 1], None,
                                                    ALU.mult))
                    nc.vector.scalar_tensor_tensor(out=f[:, t % 2, 0, :], in0=f[:, t % 2, 1, :],
                                                   scalar=r["gate"][:, 1, t:t + 1], in1=f[:, t % 2, 0, :], op0=ALU.mult,
                                                   op1=ALU.add).then_inc(mixed, 1)
                    for half in range(2):
                        dve.wait_ge(turned, 2 * t + half + 1)
                        for k in range(4):
                            o = h[:, half * 4 + k, t * P:(t + 1) * P]
                            ins = nc.vector.scalar_tensor_tensor(out=o, in0=f_ps[:, half, k, :],
                                                                 scalar=gate5[:, half * 4 + k:half * 4 + k + 1], in1=o,
                                                                 op0=ALU.mult, op1=ALU.add)
                        ins.then_inc(added, 1)

            @block.tensor
            def _(pe):
                for t in range(TT):
                    pe.wait_ge(mixed, t + 1)
                    for half in range(2):
                        if t:
                            pe.wait_ge(added, 2 * t + half - 1)
                        for k in range(4):
                            mm = nc.tensor.transpose(f_ps[:, half, k, :], f[:, t % 2, 0, (half * 4 + k) * P:(half * 4 + k + 1) * P],
                                                     cst["ident"])
                        mm.then_inc(turned, 1)


def second_block(nc, din, cst, vecs, h, upto):
    h_dram = nc.dram_tensor("h_dram", (P, KD, T), F32).ap()
    v_dram = nc.dram_tensor("v_dram", (2, P, T), F32).ap()
    o_dram = nc.dram_tensor("o_dram", (2, P, T), F32).ap()
    with ExitStack() as outer:
        def keep(name, shape, dt=F32):
            return outer.enter_context(nc.sbuf_tensor(name, shape, dt))

        mod = keep("mod", [P, 6 * KD, 2])
        a1, ac, a2, shc = (keep(x, [P, KD]) for x in ("a1", "ac", "a2", "shc"))
        neg_lam, sub_g = keep("neg_lam", [P, 1]), keep("sub_g", [P, 1])
        modulation(nc, "md", cst, vecs, din, mod, a1[:], ac[:], a2[:], shc[:], neg_lam[:], sub_g[:])

        def m(j):
            return mod[:, j * KD:(j + 1) * KD, 0]

        store_all(nc, "sh", [(h_dram, h[:])])
        with ExitStack() as ctx:
            def sb(name, shape, dt=F32):
                return ctx.enter_context(nc.sbuf_tensor(name, shape, dt))

            pr = sb("pr", [P, 19, T])
            pc = sb("pc", [P, 8, NCTX])
            v2 = sb("v2", [P, TT + 2, 768])
            with nc.sbuf_tensor("vbc", [P, 2, 256], F32) as vbc, nc.sbuf_tensor("state", [P, 64, 2], F32) as state:
                rms_norm(nc, "m1", cst, h, h, a1, m(0))
                project(nc, "q2", din["w_in2"], cols(h), T, 19, dst=pr)
                project_rows(nc, "r2", din["w_v2"][:, :, 0:768], cols(h), T, v2)
                nctx = h[:, 0:2, :].rearrange("p a (b c) -> p (a b) c", c=NCTX)
                load_all(nc, "lc", [(nctx, din["ctx"])])
                rms_norm(nc, "mc", cst, nctx, nctx, ac, shc)
                project(nc, "qc", din["w_in2"], cols(nctx), NCTX, 8, dst=pc)
                project_rows(nc, "rc", din["w_v2"][:, :, 0:768], cols(nctx), NCTX, v2[:, TT:, :])
                project_rows(nc, "rb", din["w_v2"][:, :, 768:1024], cols(nctx), NCTX, vbc)
                if upto == 21:
                    return
                store_all(nc, "sv", [(v_dram.rearrange("a p t -> p a t"), pr[:, 15:17, :])])
                decay = h[:, 0:2, :]
                decay_c = h[:, 2, 0:2 * NCTX].rearrange("p (a t) -> p a t", a=2)
                wdec = h[:, 3, 0:2 * P].rearrange("p (a t) -> p a t", a=2)
                load_all(nc, "ldw", [(wdec[0:32], din["w_dec"])])
                gla_decay(nc, "dx", cst, wdec, vecs["b_dec"], pr[:, 7, :], T, decay)
                gla_decay(nc, "dc", cst, wdec, vecs["b_dec"], pc[:, 7, :], NCTX, decay_c)
                gla_context(nc, "gc", cst, pc[:, 6, :], vbc, decay_c, state)
                gla_scan(nc, "gs", cst, pr[:, 14, :], pr[:, 6, :], decay, state,
                         v_dram.rearrange("a (h v) t -> (a h) v t", v=64), o_dram.rearrange("a (h v) t -> (a h) v t", v=64))
                load_all(nc, "lo", [(pr[:, 15:17, :], o_dram.rearrange("a p t -> p a t"))])
            head_prep(nc, "hg", cst, pr[:, 15:17, :], T, 2, vecs["gla_g"])
            gated(nc, "gg", pr[:, 15:17, :], pr[:, 17:19, :])
            if upto == 22:
                return
            load_all(nc, "lt", [(h[:, 0, :], din["cos2"]), (h[:, 1, :], din["sin2"])])
            rope2 = (cst["rot2"], h[:, 0, :], h[:, 1, :])
            head_prep(nc, "ra", cst, pr[:, 0:4, :], T, 4, None, rope2)
            head_prep(nc, "rq", cst, pr[:, 8:12, :], T, 4, None, rope2)
            attention(nc, "ad", cst, 4, pr[:, 8:12, :], [(pr[:, 0:4, :], T), (pc[:, 0:4, :], NCTX)], v2[:, :, 0:512],
                      TT + 2, diff=neg_lam[:], scratch=h)
            head_prep(nc, "hs", cst, pr[:, 8:12, :], T, 4, sub_g[:], blk=("ones", P))
            with nc.sbuf_tensor("near", [P, TT, 640], F32) as near, nc.sbuf_tensor("tab", [P, 4, 18 * 64], F32) as tab:
                load_all(nc, "ln", [(near[:], din["near"]), (tab[:], din["rpb"])])

                def bias(m_, u, t):
                    d0 = min(max(2 * t - 4, 0), 6) - 2 * t + 8
                    return [at(tab, m_ * 2 + u)[:, d0 * 64:d0 * 64 + 640], near[:, t, :]]
                window = [[min(max(2 * t - 4, 0), 6) // 2 + x for x in range(5)] + [TT, TT + 1] for t in range(TT)]
                attention(nc, "an", cst, 2, pr[:, 12:14, :], [(pr[:, 4:6, :], T), (pc[:, 4:6, :], NCTX)],
                          v2[:, :, 512:768], TT + 2, bias=bias, window=window, scratch=h)
            if upto == 23:
                return
            load_all(nc, "lh", [(h[:], h_dram)])
            mixed = cols(pr[:, 8:12, :]) + cols(pr[:, 15:17, :]) + cols(pr[:, 12:14, :])
            project(nc, "o2", din["w_out2"], mixed, T, KD, add_to=h, gate=m(2))
        if upto == 24:
            return
        h2_dram = nc.dram_tensor("h2_dram", (T, D), F32).ap()
        y_dram = nc.dram_tensor("y_dram", (NB * P, D), F32).ap()
        ids_dram = nc.dram_tensor("ids_dram", (NB * P, 1), I32).ap()
        slot, gates = keep("slot", [P, 2, TT], I32), keep("gates", [P, 2, TT])
        blk, ids = keep("blk", [P, NB], I32), keep("ids", [P, NB], I32)
        place = keep("place", [P, 2, TT], I32)
        r = {"slot": slot[:], "place": place[:], "gate": gates[:], "block": blk[:]}
        with nc.sbuf_tensor("n2", [P, KD, T], F32) as n:
            rms_norm(nc, "m2", cst, h, n, a2, m(3))
            router(nc, "ro", cst, vecs, din, n, h2_dram, r)
        dispatch(nc, "di", cst, r, ids_dram, ids[:])
        experts(nc, "ex", cst, din, r, ids[:], h2_dram, y_dram.rearrange("(b p) n -> b p n", p=P))
        combine(nc, "co", cst, r, y_dram, m(5), h)
        rms_norm(nc, "fin", cst, h, h, vecs["final_g"])




def constants():
    f = np.float32
    ident = np.eye(P, dtype=f)
    blk64 = np.kron(np.eye(2), np.ones((64, 64))).astype(f)
    rot1 = np.zeros((P, P), f)
    rot2 = np.zeros((P, P), f)
    freq = np.zeros((P, 1), f)
    inv = (np.float32(500000.0) ** (-np.arange(0, 16, 2, dtype=f) / np.float32(16))).astype(f)
    for h in (0, 64):
        for d in range(8):
            rot1[h + d + 8, h + d], rot1[h + d, h + d + 8] = -1, 1
            freq[h + d] = freq[h + d + 8] = inv[d]
        for b in (0, 32):
            for d in range(16):
                rot2[h + b + d + 16, h + b + d], rot2[h + b + d, h + b + d + 16] = -1, 1
    before = np.triu(np.ones((P, P)), 1).astype(f)
    off = np.arange(-(T - 1) - P, T + P)
    count = sum(((off % dil == 0) & (abs(off) <= window // 2)).astype(int)
                for window, dil in ((128, 1), (512, 4), (2048, 16)))
    logc = np.where(count > 0, np.log(np.maximum(count, 1)), NEG).astype(f)
    y = np.arange(1920)[None, :] - 896 - np.arange(P)[:, None]
    dilated = logc[y + (T - 1) + P]
    t = np.arange(T)
    inv2 = (np.float32(10000.0) ** (-np.arange(16, dtype=f) / np.float32(16))).astype(f)
    ang_r, ang_c = (t // 64).astype(f)[:, None] * inv2, (t % 64).astype(f)[:, None] * inv2
    cos2 = np.tile(np.concatenate([np.cos(ang_r)] * 2 + [np.cos(ang_c)] * 2, axis=1).T, (2, 1)).astype(f)
    sin2 = np.tile(np.concatenate([np.sin(ang_r)] * 2 + [np.sin(ang_c)] * 2, axis=1).T, (2, 1)).astype(f)
    p = np.arange(P)
    near = np.zeros((P, 8, 10, 64), f)
    for q in range(8):
        r, base = 2 * q + p // 64, min(max(2 * q - 4, 0), 6)
        r0 = np.clip(r - 4, 0, 8)
        c0 = np.clip(p % 64 - 8, 0, 48)
        kr, kc = base + np.arange(10), np.arange(64)
        rows = (kr[None] >= r0[:, None]) & (kr[None] < r0[:, None] + 8)
        colm = (kc[None] >= c0[:, None]) & (kc[None] < c0[:, None] + 16)
        near[:, q] = np.where(rows[:, :, None] & colm[:, None, :], 0, NEG)
    small = {"ones": np.ones((P, P), f), "ident": ident, "blk64": blk64, "rot1": rot1, "rot2": rot2,
             "before": before, "freq": freq, "eps": np.full((P, 1), EPS, f), "one": np.ones((P, 1), f),
             "heads32": np.kron(np.eye(4), np.ones((32, 1))).astype(f),
             "index": np.tile(np.arange(E_, dtype=f) - 1024, (P, 1)),
             "block": np.tile(np.arange(NB, dtype=f), (P, 1))}
    return small, {"dilated": dilated, "cos2": cos2, "sin2": sin2, "near": near.reshape(P, 8 * 640)}


def program(nc, din, out, upto=99):
    small, tables = constants()
    with ExitStack() as ctx:
        def sb(name, shape, dt=F32):
            return ctx.enter_context(nc.sbuf_tensor(name, shape, dt))

        width = sum(a.shape[1] for a in small.values())
        pack = sb("pack", [P, width])
        cst, o = {}, 0
        for name, a in small.items():
            cst[name] = pack[:, o:o + a.shape[1]]
            o += a.shape[1]
        vec = sb("vec", [P, din["vec"].shape[1]])
        vecs, o = {}, 0
        for name, n in VECS:
            vecs[name] = vec[:, o:o + n]
            o += n
        h = sb("h", [P, KD, T])
        load_all(nc, "load", [(pack[:], din["pack"]), (vec[:], din["vec"]), (h[:], din["x"])])
        first_block(nc, din, cst, vecs, h, upto)
        if upto > 20:
            second_block(nc, din, cst, vecs, h, upto)
        store_all(nc, "store", [(out, h[:])])


def first_block(nc, din, cst, vecs, h, upto):
    with ExitStack() as ctx:
        def sb(name, shape, dt=F32):
            return ctx.enter_context(nc.sbuf_tensor(name, shape, dt))

        proj = sb("proj", [P, 14, T])
        km = sb("km", [P, 2, NMEM])
        v = sb("v", [P, T // P, 512])
        vm = sb("vm", [P, NMEM // P, NMEM])
        with nc.sbuf_tensor("n", [P, KD, T], F32) as n:
            rms_norm(nc, "n1", cst, h, n, vecs["mix_g"])
            project(nc, "pin", din["w_in"], cols(n), T, 14, dst=proj)
            project_rows(nc, "pv", din["w_v"], cols(n), T, v)
            mem = n[:, 0:2, :].rearrange("p a (b c) -> p (a b) c", c=NMEM)
            load_all(nc, "lm", [(mem, din["mem"])])
            rms_norm(nc, "nm", cst, mem, mem, vecs["mem_g"])
            project(nc, "pkm", din["w_km"], cols(mem), NMEM, 2, dst=km)
            project_rows(nc, "pvm", din["w_vm"], cols(mem), NMEM, vm)
        if upto == 1:
            return
        with nc.sbuf_tensor("cos", [P, T], F32) as cos, nc.sbuf_tensor("sin", [P, T], F32) as sin:
            rope_tables(nc, "rt", cst, din["positions"], cos[:], sin[:])
            rope = (cst["rot1"], cos[:], sin[:])
            head_prep(nc, "hq", cst, proj[:, 0:4, :], T, 4, vecs["q_g"], rope)
            head_prep(nc, "hk", cst, proj[:, 4:8, :], T, 4, vecs["k_g"], rope)
            head_prep(nc, "hm", cst, proj[:, 12:14, :], T, 2, vecs["mq_g"])
            head_prep(nc, "hkm", cst, km, NMEM, 2, vecs["mk_g"])
        conv_mixer(nc, "cv", cst, proj[:, 8:10, :], proj[:, 10:12, :],
                   vecs["cv_w"].rearrange("p (c k) -> p c k", c=2), vecs["cv_b"], vecs["ln_g"], vecs["ln_b"])
        if upto == 2:
            return
        with nc.sbuf_tensor("dil", [P, 1920], F32) as dil:
            load_all(nc, "ld", [(dil[:], din["dilated"])])
            attention(nc, "a1", cst, 4, proj[:, 0:4, :], [(proj[:, 4:8, :], T)], v, T // P,
                      bias=lambda m, u, t: [dil[:, 896 - P * t:896 - P * t + T]])
        attention(nc, "am", cst, 2, proj[:, 12:14, :], [(km, NMEM)], vm, NMEM // P)
        if upto == 3:
            return
        mixed = cols(proj[:, 0:4, :]) + cols(proj[:, 8:10, :]) + cols(proj[:, 12:14, :])
        project(nc, "po", din["w_out"], mixed, T, KD, add_to=h)
    if upto == 4:
        return
    with ExitStack() as ctx:
        hidden = ctx.enter_context(nc.sbuf_tensor("hidden", [P, KF, T], F32))
        with nc.sbuf_tensor("nf", [P, KD, T], F32) as n:
            rms_norm(nc, "nf", cst, h, n, vecs["ffn_g"])
            ffn_up(nc, "fu", din["w_up"], cols(n), hidden)
        project(nc, "fd", din["w_down"], cols(hidden), T, KD, add_to=h)


VECS = [("mix_g", KD), ("mem_g", KD), ("ffn_g", KD), ("q_g", 1), ("k_g", 1), ("mq_g", 1), ("mk_g", 1),
        ("cv_w", 62), ("cv_b", 2), ("ln_g", 2), ("ln_b", 2),
        ("c", 2 * KD), ("g1", KD), ("g2", KD), ("final_g", KD), ("b_mod", 6 * KD), ("lam", 4), ("sub_g", 1),
        ("gla_g", 1), ("b_dec", 2), ("b_route", 1)]


def lay_out(x):
    def col(a):
        return a.reshape(-1, P).T

    def wtiles(w):
        K, M = w.shape[0] // P, w.shape[1] // P
        return w.reshape(K, P, M, P).transpose(2, 1, 0, 3).reshape(M, P, K * P)

    def wrows(w):
        return w.reshape(-1, P, w.shape[1]).transpose(1, 0, 2)

    small, tables = constants()
    w_in = x["w_in"][0]
    v = {"mix_g": col(x["mix_norm_g"][0]), "mem_g": col(x["mem_norm_g"][0]), "ffn_g": col(x["ffn_norm_g"][0]),
         "q_g": np.tile(x["q_norm_g"][0], 2)[:, None], "k_g": np.tile(x["k_norm_g"][0], 2)[:, None],
         "mq_g": np.tile(x["mq_norm_g"][0], 2)[:, None], "mk_g": np.tile(x["mk_norm_g"][0], 2)[:, None],
         "cv_w": x["conv_dw_w"][0].T.reshape(2, P, 31).transpose(1, 0, 2).reshape(P, 62),
         "cv_b": col(x["conv_dw_b"][0]), "ln_g": col(x["conv_ln_g"][0]), "ln_b": col(x["conv_ln_b"][0])}
    d = {"pack": np.concatenate(list(small.values()), axis=1), "dilated": tables["dilated"],
         "x": x["x"][0].T.reshape(KD, P, T).transpose(1, 0, 2),
         "mem": x["mem"][0].T.reshape(KD, P, NMEM).transpose(1, 0, 2),
         "positions": x["positions"][0],
         "w_in": wtiles(np.concatenate([w_in[:, 0:1024], w_in[:, 1536:2304]], axis=1)),
         "w_v": wrows(w_in[:, 1024:1536]),
         "w_km": wtiles(x["w_mem_kv"][0][:, 0:256]), "w_vm": wrows(x["w_mem_kv"][0][:, 256:512]),
         "w_out": wtiles(x["w_out"][0]), "w_down": wtiles(x["w_down"][0])}
    up = x["w_up"][0].reshape(KD, P, 2, KF, P).transpose(3, 1, 0, 2, 4).reshape(KF, P, KD * 2 * P)
    taps = np.concatenate([x["ffn_dw_w"][0], x["ffn_dw_b"]], axis=0).reshape(4, 2, KF, P).transpose(2, 3, 1, 0)
    d["w_up"] = np.concatenate([up, taps.reshape(KF, P, 8)], axis=2)
    more(x, d, v, tables, col, wtiles, wrows)
    d["vec"] = np.concatenate([v[name] for name, _ in VECS], axis=1)
    return {k: np.ascontiguousarray(a) for k, a in d.items()}


def more(x, d, v, tables, col, wtiles, wrows):
    w = x["w_in_2"][0]
    at_ = dict(zip(("qa", "ka", "va", "qb", "kb", "vb", "rb", "gb", "qn", "kn", "vn"),
                   np.split(w, np.cumsum((512, 512, 512, 128, 128, 256, 256, 32, 256, 256)), axis=1)))
    pad = np.zeros((D, 96), w.dtype)
    d["w_in2"] = wtiles(np.concatenate([at_["ka"], at_["kn"], at_["kb"], at_["gb"], pad, at_["qa"], at_["qn"],
                                        at_["qb"], at_["vb"], at_["rb"]], axis=1))
    d["w_v2"] = wrows(np.concatenate([at_["va"], at_["vn"], at_["vb"]], axis=1))
    d["w_mod"] = wtiles(x["w_mod_2"][0])
    d["w_out2"] = wtiles(x["w_out_2"][0])
    d["ctx"] = x["ctx_2"][0].T.reshape(KD, P, NCTX).transpose(1, 0, 2)
    dec = np.zeros((32, 2, P), w.dtype)
    for i in range(2):
        dec[16 * i:16 * i + 16, i] = x["gla_w_decay_2"][0, i]
    d["w_dec"] = dec
    d["cos2"], d["sin2"], d["near"] = tables["cos2"], tables["sin2"], tables["near"].reshape(P, TT, 640)
    p = np.arange(P)
    dr = np.clip(np.arange(18)[None, :] - p[:, None] // 64 - 1, 0, 14)
    dc = np.clip(np.arange(64)[None, :] - p[:, None] % 64 + 15, 0, 30)
    d["rpb"] = x["na_rel_bias_2"][0][:, dr[:, :, None], dc[:, None, :]].transpose(1, 0, 2, 3).reshape(P, 4, 18 * 64)
    d["w_route"] = wrows(np.concatenate([x["w_router_group_2"][0], x["w_router_expert_2"][0]], axis=1))
    d["w_eup"], d["w_edown"] = x["w_expert_up_2"][0], x["w_expert_down_2"][0]
    rest = np.zeros((P - 36,), w.dtype)
    lam = np.zeros((P, 4), w.dtype)
    lam[0:64] = x["diff_lambda_2"][0].T
    v.update({"c": np.concatenate([col(x["c_2"][0]), col(x["c_ctx_2"])], axis=1), "g1": col(x["norm1_g_2"][0]),
              "g2": col(x["norm2_g_2"][0]), "final_g": col(x["final_g_2"]), "b_mod": col(x["b_mod_2"][0]), "lam": lam,
              "sub_g": x["diff_sub_g_2"][0][:, None], "gla_g": np.tile(x["gla_norm_g_2"][0], 2)[:, None],
              "b_dec": x["gla_b_decay_2"][0].T,
              "b_route": np.concatenate([x["b_router_group_2"][0], x["b_router_expert_2"][0], rest])[:, None]})


def kernel(**inputs):
    import concourse.bacc as bacc
    from concourse.bass_utils import run_bass_kernel_spmd

    nc = bacc.Bacc("TRN2", target_bir_lowering=False, num_devices=1)
    arrays = lay_out({k: np.asarray(a) for k, a in inputs.items()})
    din = {k: nc.dram_tensor(f"in_{k}", a.shape, mybir.dt.from_np(a.dtype), kind="ExternalInput").ap()
           for k, a in arrays.items()}
    out = nc.dram_tensor("out", (P, KD, T), F32, kind="ExternalOutput").ap()
    program(nc, din, out)
    r = run_bass_kernel_spmd(nc, [{f"in_{k}": a for k, a in arrays.items()}], core_ids=[0])
    y = r.results[0]["out"]
    return y.transpose(1, 0, 2).reshape(D, T).T[None]
```

```python
from contextlib import ExitStack

import numpy as np

import concourse.bass as bass
from concourse import mybir

F32 = mybir.dt.float32
I32 = mybir.dt.int32
U32 = mybir.dt.uint32
ACT = mybir.ActivationFunctionType
ALU = mybir.AluOpType
AX = mybir.AxisListType

P = 128
T = 1024
D = 1024
KD = D // P
NMEM = 256
NCTX = 256
FF = 2816
KF = FF // P
BANK = 512
EPS = 1e-6
NEG = -1e30
SCALE = 64.0 ** -0.5


class Phase:

    def __init__(self, nc, tag):
        self.nc, self.tag, self.ctx, self.sems = nc, tag, ExitStack(), []

    def __enter__(self):
        return self

    def __exit__(self, *e):
        self.nc.clear_and_free_semaphores(self.sems)
        self.nc.all_engine_barrier(sem_only=True)
        return self.ctx.__exit__(*e)

    def sb(self, name, shape, dt=F32):
        return self.ctx.enter_context(self.nc.sbuf_tensor(f"{self.tag}_{name}", shape, dt))

    def ps(self, name, shape, dt=F32):
        return self.ctx.enter_context(self.nc.psum_tensor(f"{self.tag}_{name}", shape, dt))

    def sem(self, name):
        self.sems.append(self.nc.alloc_semaphore(f"{self.tag}_{name}"))
        return self.sems[-1]


class Steps:

    def __init__(self, eng, sem):
        self.eng, self.sem, self.n, self.i, self.k = eng, sem, 0, None, 0

    def enter(self, i, per):
        self.i, self.per, self.k = i, per, 0

    def leave(self, trips):
        assert self.k == self.per, (self.k, self.per)
        self.n, self.i = self.n + trips * self.per, None

    def done(self, ins):
        ins.then_inc(self.sem, 1)
        if self.i is None:
            self.n += 1
            self.eng.wait_ge(self.sem, self.n)
        else:
            self.k += 1
            self.eng.wait_ge(self.sem, self.i * self.per + (self.n + self.k))


def chunks(n, size=BANK):
    return [(a, min(size, n - a)) for a in range(0, n, size)]


def at(ap, i):
    return ap[:, bass.ds(i, 1), :].rearrange("p a n -> p (a n)")


def cols(ap):
    return [ap[:, k, :] for k in range(ap.shape[1])]


def load_all(nc, tag, pairs):
    with Phase(nc, tag) as ph:
        loaded = ph.sem("loaded")
        with nc.Block() as block:
            @block.sync
            def _(sp):
                for dst, src in pairs:
                    sp.dma_start(dst, src).then_inc(loaded, 16)
                sp.wait_ge(loaded, 16 * len(pairs))


def store_all(nc, tag, pairs):
    load_all(nc, tag, pairs)


def rms_norm(nc, tag, cst, x, out, gain, shift=None, width=D):
    K, n = x.shape[1], x.shape[2]
    parts = chunks(n)
    with Phase(nc, tag) as ph:
        sq = ph.sb("sq", [P, 2, BANK])
        sd = ph.sb("sd", [P, 2, BANK])
        ms = ph.ps("ms", [P, 2, BANK])
        sq_ready, summed, sd_ready = ph.sem("sq_ready"), ph.sem("summed"), ph.sem("sd_ready")
        step = ph.sem("step")
        with nc.Block() as block:
            @block.scalar
            def _(act):
                def root(h):
                    a, w = parts[h]
                    act.wait_ge(summed, K * (h + 1))
                    nc.scalar.activation(sd[:, h % 2, 0:w], ms[:, h % 2, 0:w], ACT.Sqrt, bias=cst["eps"],
                                         scale=1.0 / width).then_inc(sd_ready, 1)
                for h, (a, w) in enumerate(parts):
                    for k in range(K):
                        j = h * K + k
                        if j >= 2:
                            act.wait_ge(summed, j - 1)
                        nc.scalar.activation(sq[:, j % 2, 0:w], x[:, k, a:a + w], ACT.Square).then_inc(sq_ready, 1)
                    root(h)

            @block.tensor
            def _(pe):
                for h, (a, w) in enumerate(parts):
                    if h >= 2:
                        pe.wait_ge(sd_ready, h - 1)
                    for k in range(K):
                        j = h * K + k
                        pe.wait_ge(sq_ready, j + 1)
                        nc.tensor.matmul(ms[:, h % 2, 0:w], cst["ones"], sq[:, j % 2, 0:w], start=(k == 0),
                                         stop=(k == K - 1)).then_inc(summed, 1)

            @block.vector
            def _(dve):
                st = Steps(dve, step)
                for h, (a, w) in enumerate(parts):
                    dve.wait_ge(sd_ready, h + 1)
                    st.done(nc.vector.reciprocal(sd[:, h % 2, 0:w], sd[:, h % 2, 0:w]))
                    for k in range(K):
                        last = nc.vector.scalar_tensor_tensor(out=out[:, k, a:a + w], in0=x[:, k, a:a + w],
                                                              scalar=gain[:, k:k + 1], in1=sd[:, h % 2, 0:w],
                                                              op0=ALU.mult, op1=ALU.mult)
                    if shift is not None:
                        st.done(last)
                        for k in range(K):
                            nc.vector.tensor_scalar(out[:, k, a:a + w], out[:, k, a:a + w], shift[:, k:k + 1],
                                                    None, ALU.add)


def project(nc, tag, w_dram, src, n, count, dst=None, add_to=None, gate=None, first=0):
    K = len(src)
    parts = chunks(n)
    wide = len(parts) * BANK
    R = 4 if K <= KD else 2
    with Phase(nc, tag) as ph:
        w = ph.sb("w", [P, R, K, P])
        acc = ph.ps("acc", [P, 2, wide])
        w_ready = [ph.sem(f"w_ready{u}") for u in range(R)]
        mm_done, acc_free = ph.sem("mm_done"), ph.sem("acc_free")
        rounds, tail = count // R, count % R

        def sweep(eng, body):
            if rounds:
                with eng.Fori(0, rounds) as i:
                    for u in range(R):
                        body(i, u)
            for u in range(tail):
                body(rounds, u)

        with nc.Block() as block:
            @block.sync
            def _(sp):
                def load(i, u):
                    sp.wait_ge(mm_done, i * R + (u + 1))
                    sp.dma_start(w[:, u], w_dram[bass.ds(i * R + (u + first), 1)].rearrange(
                        "a p (k n) -> p (a k) n", k=K)).then_inc(w_ready[u], 16)
                sweep(sp, load)

            @block.tensor
            def _(pe):
                pe.sem_inc(mm_done, R)

                def tile(i, u):
                    pe.wait_ge(w_ready[u], i * 16 + 16)
                    pe.wait_ge(acc_free, i * R + (u + 1))
                    for a, width in parts:
                        for k in range(K):
                            mm = nc.tensor.matmul(acc[:, u % 2, a:a + width], w[:, u, k, :], src[k][:, a:a + width],
                                                  start=(k == 0), stop=(k == K - 1))
                    mm.then_inc(mm_done, 1)
                sweep(pe, tile)

            if dst is not None:
                @block.scalar
                def _(act):
                    act.sem_inc(acc_free, 2)

                    def keep(i, u):
                        act.wait_ge(mm_done, i * R + (u + 1 + R))
                        nc.scalar.activation(at(dst, i * R + u), acc[:, u % 2, 0:n], ACT.Copy).then_inc(acc_free, 1)
                    sweep(act, keep)
            else:
                @block.vector
                def _(dve):
                    dve.sem_inc(acc_free, 2)

                    def add(i, u):
                        dve.wait_ge(mm_done, i * R + (u + 1 + R))
                        o = at(add_to, i * R + u)
                        if gate is None:
                            nc.vector.tensor_tensor(o, acc[:, u % 2, 0:n], o, ALU.add).then_inc(acc_free, 1)
                        else:
                            nc.vector.scalar_tensor_tensor(out=o, in0=acc[:, u % 2, 0:n],
                                                           scalar=gate[:, bass.ds(i * R + u, 1)], in1=o,
                                                           op0=ALU.mult, op1=ALU.add).then_inc(acc_free, 1)
                    sweep(dve, add)


def project_rows(nc, tag, w_dram, src, n, dst):
    K, cols = w_dram.shape[1], w_dram.shape[2]
    cc = chunks(cols)
    tiles = n // P
    with Phase(nc, tag) as ph:
        w = ph.sb("w", [P, K, BANK])
        acc = ph.ps("acc", [P, 2, BANK])
        w_ready, mm_done, acc_free = ph.sem("w_ready"), ph.sem("mm_done"), ph.sem("acc_free")
        with nc.Block() as block:
            @block.sync
            def _(sp):
                for c, (a, width) in enumerate(cc):
                    if c:
                        sp.wait_ge(mm_done, c * tiles)
                    sp.dma_start(w[:, :, 0:width], w_dram[:, :, a:a + width]).then_inc(w_ready, 16)

            @block.tensor
            def _(pe):
                for c, (a, width) in enumerate(cc):
                    pe.wait_ge(w_ready, 16 * (c + 1))
                    for t in range(tiles):
                        j = c * tiles + t
                        if j >= 2:
                            pe.wait_ge(acc_free, j - 1)
                        for k in range(K):
                            mm = nc.tensor.matmul(acc[:, j % 2, 0:width], src[k][:, t * P:(t + 1) * P],
                                                  w[:, k, 0:width], start=(k == 0), stop=(k == K - 1))
                        mm.then_inc(mm_done, 1)

            @block.scalar
            def _(act):
                for c, (a, width) in enumerate(cc):
                    for t in range(tiles):
                        j = c * tiles + t
                        act.wait_ge(mm_done, j + 1)
                        nc.scalar.activation(dst[:, t, a:a + width], acc[:, j % 2, 0:width],
                                             ACT.Copy).then_inc(acc_free, 1)


def head_prep(nc, tag, cst, x, n, tiles, gain=None, rope=None, blk=("blk64", 64)):
    parts = chunks(n)
    wide = len(parts) * BANK
    per = 2 * ((2 if gain is not None else 0) + (3 if rope else 0))
    assert tiles % 2 == 0
    with Phase(nc, tag) as ph:
        sq = ph.sb("sq", [P, 2, n])
        sd = ph.sb("sd", [P, 2, n])
        turn = ph.sb("turn", [P, n])
        ms, rot_ps = ph.ps("ms", [P, 2, wide]), ph.ps("rot", [P, 2, wide])
        sq_ready, summed, sd_ready, normed = (ph.sem(s) for s in ("sq_ready", "summed", "sd_ready", "normed"))
        turned, rot_used, step = ph.sem("turned"), ph.sem("rot_used"), ph.sem("step")
        with nc.Block() as block:
            if gain is not None:
                @block.scalar
                def _(act):
                    with act.Fori(0, tiles // 2) as i:
                        for u in range(2):
                            act.wait_ge(summed, i * 2 + (u + 1))
                            nc.scalar.activation(sq[:, u, :], at(x, i * 2 + u), ACT.Square).then_inc(sq_ready, 1)
                        for u in range(2):
                            act.wait_ge(summed, i * 2 + (u + 3))
                            act.wait_ge(normed, i * 2 + (u + 1))
                            nc.scalar.activation(sd[:, u, :], ms[:, u, 0:n], ACT.Sqrt, bias=cst["eps"],
                                                 scale=1.0 / blk[1]).then_inc(sd_ready, 1)

            @block.tensor
            def _(pe):
                if gain is not None:
                    pe.sem_inc(summed, 2)
                    pe.sem_inc(sd_ready, 2)
                with pe.Fori(0, tiles // 2) as i:
                    if gain is not None:
                        for u in range(2):
                            pe.wait_ge(sq_ready, i * 2 + (u + 1))
                            pe.wait_ge(sd_ready, i * 2 + (u + 1))
                            for a, w in parts:
                                mm = nc.tensor.matmul(ms[:, u, a:a + w], cst[blk[0]], sq[:, u, a:a + w], start=True,
                                                      stop=True)
                            mm.then_inc(summed, 1)
                    if rope:
                        for u in range(2):
                            if gain is not None:
                                pe.wait_ge(normed, i * 2 + (u + 3))
                            pe.wait_ge(rot_used, i * 2 + (u + 1))
                            for a, w in parts:
                                mm = nc.tensor.matmul(rot_ps[:, u, a:a + w], rope[0], at(x, i * 2 + u)[:, a:a + w],
                                                      start=True, stop=True)
                            mm.then_inc(turned, 1)

            @block.vector
            def _(dve):
                st = Steps(dve, step)
                dve.sem_inc(normed, 2)
                dve.sem_inc(rot_used, 2)
                with dve.Fori(0, tiles // 2) as i:
                    st.enter(i, per)
                    if gain is not None:
                        for u in range(2):
                            xi = at(x, i * 2 + u)
                            dve.wait_ge(sd_ready, i * 2 + (u + 3))
                            st.done(nc.vector.reciprocal(sd[:, u, :], sd[:, u, :]))
                            st.done(nc.vector.scalar_tensor_tensor(out=xi, in0=xi, scalar=gain[:, bass.ds(i * 2 + u, 1)],
                                                                   in1=sd[:, u, :], op0=ALU.mult, op1=ALU.mult))
                            dve.sem_inc(normed, 1)
                    if rope:
                        for u in range(2):
                            xi = at(x, i * 2 + u)
                            dve.wait_ge(turned, i * 2 + (u + 1))
                            st.done(nc.vector.tensor_tensor(turn[:], rot_ps[:, u, 0:n], rope[2], ALU.mult))
                            dve.sem_inc(rot_used, 1)
                            st.done(nc.vector.tensor_tensor(xi, xi, rope[1], ALU.mult))
                            st.done(nc.vector.tensor_tensor(xi, xi, turn[:], ALU.add))
                st.leave(tiles // 2)


def attention(nc, tag, cst, pairs, q, keys, v, KT, bias=None, diff=None, window=None, scratch=None):
    out = q
    tiles = T // P
    nk = sum(n for _, n in keys)
    seen = KT if window is None else len(window[0])
    NS = seen * P
    ng = -(-seen // 4)
    wide = -(-NS // BANK) * BANK
    PTS = 1 if wide > 2 * BANK else 2
    if window is not None:
        units = [(t, u) for t in range(tiles) for u in range(2)]
    elif diff is not None:
        units = [(t, u) for t in range(tiles) for u in range(2)]
    else:
        units = [(c * 4 + t, u) for c in range(2) for u in range(2) for t in range(4)]
    U = len(units)
    merged = 2 if diff is not None else 1
    M = U // merged
    share = 1 if window is not None else 4
    J = M // share
    G = M * ng
    LAG = 1 if diff is not None else 2
    NP = (LAG + 2) * merged
    early, late = (range(0, 1), range(1, ng)) if diff is not None else (range(0, ng), range(0, 0))
    PT = 1 if scratch is not None else 2
    with Phase(nc, tag) as ph:
        spare = scratch[:].rearrange("p a b -> p (a b)") if scratch is not None else None
        if spare is not None and NP * NS + T + nk <= spare.shape[1]:
            qs, ks = spare[:, NP * NS:NP * NS + T], spare[:, NP * NS + T:NP * NS + T + nk]
        else:
            qs, ks = ph.sb("qs", [P, T]), ph.sb("ks", [P, nk])
        if spare is None:
            prob = ph.sb("prob", [P, NP, NS])
        else:
            prob = spare[:, 0:NP * NS].rearrange("p (a b) -> p a b", a=NP)
        vs = ph.sb("vs", [P, KT, P])
        probT = ph.sb("probT", [P, PT, seen, share * P])
        negm = ph.sb("negm", [P, NP])
        den = ph.sb("den", [P, NP])
        s_ps = ph.ps("s_ps", [P, 2, wide])
        t_ps = ph.ps("t_ps", [P, PTS, 4, P])
        o_ps = ph.ps("o_ps", [P, PTS, BANK])
        rd_ready, scaled = ph.sem("rd_ready"), ph.sem("scaled")
        v_staged, staged, s_ready, s_free = (ph.sem(s) for s in ("v_staged", "staged", "s_ready", "s_free"))
        max_ready, p_ready, d_ready = (ph.sem(s) for s in ("max_ready", "p_ready", "d_ready"))
        t_ready, t_free, o_ready, o_free, step = (ph.sem(s) for s in ("t_ready", "t_free", "o_ready", "o_free", "step"))
        NST = 1 + len(keys)
        with nc.Block() as block:
            @block.gpsimd
            def _(pool):
                with pool.Fori(0, pairs) as m:
                    pool.wait_ge(o_ready, m * J + 2)
                    nc.gpsimd.tensor_copy(vs[:], v[:, :, bass.ds(m * P, P)]).then_inc(v_staged, 1)

            @block.tensor
            def _(pe):
                pe.sem_inc(o_ready, 2)
                pe.sem_inc(t_ready, (LAG + 2) * ng)
                with pe.Fori(0, pairs) as m:
                    pe.wait_ge(staged, m * NST + NST)

                    def scores(n):
                        t, u = units[n]
                        pe.wait_ge(s_free, m * U + (n + 1))
                        r = slice(64 * u, 64 * u + 64)
                        if window is None:
                            runs = [(a, a, w) for a, w in chunks(nk)]
                        else:
                            k0, nw = window[t][0] * P, (seen - 2) * P
                            runs = [(a, k0 + a, w) for a, w in chunks(nw)]
                            runs += [(a, nk - NCTX + a - nw, min(w, BANK - a % BANK)) for a, w in [(nw, NCTX)]]
                        for o, a, w in runs:
                            mm = nc.tensor.matmul(s_ps[:, n % 2, o:o + w], qs[r, t * P:(t + 1) * P], ks[r, a:a + w],
                                                  start=True, stop=True)
                        mm.then_inc(s_ready, 1)

                    def turn(k, groups):
                        if 0 in groups:
                            pe.wait_ge(d_ready, m * M + (k + 1))
                        p = prob[:, (k % (LAG + 2)) * merged, :]
                        for g in groups:
                            j = k * ng + g
                            pe.wait_ge(t_free, m * G + (j + 1))
                            for x in range(4 * g, min(4 * g + 4, seen)):
                                mm = nc.tensor.transpose(t_ps[:, j % PTS, x - 4 * g, :], p[:, x * P:(x + 1) * P],
                                                         cst["ident"])
                            mm.then_inc(t_ready, 1)

                    def values(j):
                        if j == 0:
                            pe.wait_ge(v_staged, m + 1)
                        pe.wait_ge(t_free, m * G + (PTS + (j + 1) * share * ng))
                        pe.wait_ge(o_free, m * J + (j + 1))
                        t = units[j * share * merged][0]
                        for x in range(seen):
                            kt = x if window is None else window[t][x]
                            mm = nc.tensor.matmul(o_ps[:, j % PTS, 0:share * P], vs[:, kt, :],
                                                  probT[:, j % PT, x, :], start=(x == 0), stop=(x == seen - 1))
                        mm.then_inc(o_ready, 1)

                    for n in range(merged):
                        scores(n)
                    for k in range(M + LAG):
                        new = range((k + 1) * merged, min((k + 2) * merged, U))
                        full = k > LAG and (k - LAG) % share == 0
                        for n in new[:1]:
                            scores(n)
                        if full and PT == 1:
                            values((k - LAG) // share - 1)
                        if k >= LAG:
                            turn(k - LAG, early)
                        for n in new[1:]:
                            scores(n)
                        if k >= LAG and late:
                            turn(k - LAG, late)
                        if full and PT == 2:
                            values((k - LAG) // share - 1)
                    values(J - 1)

            @block.scalar
            def _(act):
                act.sem_inc(t_free, PTS)
                act.sem_inc(p_ready, NP)
                if bias is None:
                    act.sem_inc(s_free, 2)
                with act.Fori(0, pairs) as m:
                    act.wait_ge(o_ready, m * J + 2)
                    nc.scalar.activation(qs[:, 0:T], at(q, m), ACT.Copy).then_inc(staged, 1)
                    if len(keys) > 1:
                        nc.scalar.activation(ks[:, T:nk], at(keys[1][0], m), ACT.Copy).then_inc(staged, 1)

                    def exps(n):
                        act.wait_ge(max_ready, m * U + (n + 1))
                        src, sc = (s_ps[:, n % 2, 0:NS], SCALE) if bias is None else (prob[:, n % NP, :], 1.0)
                        if bias is None:
                            act.wait_ge(t_ready, m * G + (n // merged + 1) * ng)
                        ins = nc.scalar.activation(prob[:, n % NP, :], src, ACT.Exp, bias=negm[:, n % NP:n % NP + 1],
                                                   scale=sc, accum_out=den[:, n % NP:n % NP + 1])
                        ins.then_inc(p_ready, 1)
                        if bias is None:
                            act.wait_ge(p_ready, m * U + (n + 1 + NP))
                            act.sem_inc(s_free, 1)

                    def keep(k, groups):
                        if k % share == 0 and 0 in groups:
                            act.wait_ge(o_ready, m * J + (k // share + 3 - PT))
                        for g in groups:
                            j = k * ng + g
                            act.wait_ge(t_ready, m * G + (j + 1 + (LAG + 2) * ng))
                            x1 = min(4, seen - 4 * g)
                            nc.scalar.activation(
                                probT[:, (k // share) % PT, 4 * g:4 * g + x1, (k % share) * P:(k % share + 1) * P],
                                t_ps[:, j % PTS, 0:x1, :], ACT.Copy).then_inc(t_free, 1)

                    for n in range(merged):
                        exps(n)
                    for k in range(M + LAG):
                        new = range((k + 1) * merged, min((k + 2) * merged, U))
                        if diff is not None and k < M:
                            a = (k % (LAG + 2)) * merged
                            act.wait_ge(rd_ready, m * M + (k + 1))
                            nc.scalar.activation(prob[:, a, :], prob[:, a, :], ACT.Copy,
                                                 scale=den[:, a:a + 1]).then_inc(scaled, 1)
                        if k >= LAG:
                            keep(k - LAG, early)
                        for n in new[:1]:
                            exps(n)
                        if k >= LAG and late:
                            keep(k - LAG, late)
                        for n in new[1:]:
                            exps(n)

            @block.vector
            def _(dve):
                st = Steps(dve, step)
                dve.sem_inc(o_free, PTS)
                if bias is not None:
                    dve.sem_inc(s_free, 2)
                nb = len(bias(0, 0, 0)) if bias is not None else 0
                per = U * (nb if nb else 1) + merged * M
                with dve.Fori(0, pairs) as m:
                    st.enter(m, per)
                    dve.wait_ge(o_ready, m * J + 2)
                    nc.vector.tensor_copy(ks[:, 0:keys[0][1]], at(keys[0][0], m)).then_inc(staged, 1)

                    def top(n):
                        t, u = units[n]
                        dve.wait_ge(s_ready, m * U + (n + 1))
                        s = s_ps[:, n % 2, 0:NS]
                        nm = negm[:, n % NP:n % NP + 1]
                        if bias is not None:
                            dve.wait_ge(t_ready, m * G + (n + 1) * ng)
                            b = bias(m, u, t)
                            w = b[0].shape[1]
                            p = prob[:, n % NP, :]
                            ins = nc.vector.scalar_tensor_tensor(out=p[:, 0:w], in0=s[:, 0:w], scalar=SCALE, in1=b[0],
                                                                 op0=ALU.mult, op1=ALU.add)
                            if w < NS:
                                ins = nc.vector.tensor_scalar(p[:, w:NS], s[:, w:NS], SCALE, None, ALU.mult)
                            st.done(ins)
                            dve.sem_inc(s_free, 1)
                            for more in b[1:]:
                                st.done(nc.vector.tensor_tensor(p[:, 0:w], p[:, 0:w], more, ALU.add))
                            nc.vector.tensor_reduce(nm, p, AX.X, ALU.max, negate=True).then_inc(max_ready, 1)
                        else:
                            dve.wait_ge(p_ready, m * U + (n + 1))
                            st.done(nc.vector.tensor_reduce(nm, s, AX.X, ALU.max, negate=True))
                            nc.vector.tensor_scalar(nm, nm, SCALE, None, ALU.mult).then_inc(max_ready, 1)

                    def invert(k):
                        dve.wait_ge(p_ready, m * U + ((k + 1) * merged + NP))
                        a = (k % (LAG + 2)) * merged
                        st.done(nc.vector.reciprocal(den[:, a:a + merged], den[:, a:a + merged]))
                        if diff is not None:
                            dve.sem_inc(rd_ready, 1)
                            st.done(nc.vector.tensor_scalar(den[:, a + 1:a + 2], den[:, a + 1:a + 2], diff, None,
                                                            ALU.mult))

                    def mix(k):
                        a = (k % (LAG + 2)) * merged
                        if diff is None:
                            nc.vector.tensor_scalar(prob[:, a, :], prob[:, a, :], den[:, a:a + 1], None,
                                                    ALU.mult).then_inc(d_ready, 1)
                        else:
                            dve.wait_ge(scaled, m * M + (k + 1))
                            nc.vector.scalar_tensor_tensor(out=prob[:, a, :], in0=prob[:, a + 1, :],
                                                           scalar=den[:, a + 1:a + 2], in1=prob[:, a, :],
                                                           op0=ALU.mult, op1=ALU.add).then_inc(d_ready, 1)

                    def result(j):
                        t, u = units[j * share * merged]
                        dve.wait_ge(o_ready, m * J + (j + 3))
                        rows = slice(0, P) if diff is not None else slice(64 * u, 64 * u + 64)
                        nc.vector.tensor_copy(at(out, m)[rows, t * P:(t + share) * P],
                                              o_ps[rows, j % PTS, 0:share * P]).then_inc(o_free, 1)

                    for n in range(merged):
                        top(n)
                    for k in range(M + LAG):
                        new = range((k + 1) * merged, min((k + 2) * merged, U))
                        if k < M:
                            invert(k)
                            if diff is None:
                                mix(k)
                        for n in new[:1]:
                            top(n)
                        if diff is not None and k < M:
                            mix(k)
                        for n in new[1:]:
                            top(n)
                        if k > LAG and (k - LAG) % share == 0:
                            result((k - LAG) // share - 1)
                    result(J - 1)
                st.leave(pairs)


def rope_tables(nc, tag, cst, pos_dram, cos, sin):
    MAGIC = 12582912.0
    C1, C2 = 6.28125, 2 * np.pi - 6.28125
    C2a = float(np.float32(np.round(C2 * 2 ** 20) / 2 ** 20))
    C3 = float(np.float32(2 * np.pi - C1 - C2a))
    with Phase(nc, tag) as ph:
        posi = ph.sb("posi", [P, T], I32)
        ang, turns, red = ph.sb("ang", [P, T]), ph.sb("turns", [P, T]), ph.sb("red", [P, T])
        loaded, step, reduced, used = (ph.sem(s) for s in ("loaded", "step", "reduced", "used"))
        with nc.Block() as block:
            @block.sync
            def _(sp):
                sp.dma_start(posi[:], pos_dram.partition_broadcast(P)).then_inc(loaded, 16)

            @block.vector
            def _(dve):
                st = Steps(dve, step)
                dve.wait_ge(loaded, 16)
                st.done(nc.vector.tensor_copy(ang[:], posi[:]))
                st.done(nc.vector.tensor_scalar(ang[:], ang[:], cst["freq"], None, ALU.mult))
                for j, quarter in enumerate((0.0, 0.25)):
                    if j:
                        dve.wait_ge(used, 1)
                    st.done(nc.vector.tensor_scalar(turns[:], ang[:], 1 / (2 * np.pi), quarter, ALU.mult, ALU.add))
                    st.done(nc.vector.tensor_scalar(turns[:], turns[:], MAGIC, None, ALU.add))
                    st.done(nc.vector.tensor_scalar(turns[:], turns[:], MAGIC, None, ALU.subtract))
                    st.done(nc.vector.scalar_tensor_tensor(out=red[:], in0=turns[:], scalar=-C1, in1=ang[:],
                                                           op0=ALU.mult, op1=ALU.add))
                    st.done(nc.vector.scalar_tensor_tensor(out=red[:], in0=turns[:], scalar=-C2a, in1=red[:],
                                                           op0=ALU.mult, op1=ALU.add))
                    st.done(nc.vector.scalar_tensor_tensor(out=red[:], in0=turns[:], scalar=-C3, in1=red[:],
                                                           op0=ALU.mult, op1=ALU.add))
                    st.done(nc.vector.tensor_scalar(red[:], red[:], quarter * 2 * np.pi, 3.1415925, ALU.add, ALU.min))
                    nc.vector.tensor_scalar(red[:], red[:], -3.1415925, None, ALU.max).then_inc(reduced, 1)

            @block.scalar
            def _(act):
                for j, table in enumerate((sin, cos)):
                    act.wait_ge(reduced, j + 1)
                    nc.scalar.activation(table, red[:], ACT.Sin).then_inc(used, 1)


def conv_mixer(nc, tag, cst, a, g, taps, taps_b, ln_g, ln_b):
    K = taps.shape[2]
    half = K // 2
    C = a.shape[1]
    parts = chunks(T)
    with Phase(nc, tag) as ph:
        y = ph.sb("y", [P, C, T])
        sq = ph.sb("sq", [P, C, T])
        sd = ph.sb("sd", [P, T])
        mean_ps, var_ps = ph.ps("mean", [P, T]), ph.ps("var", [P, T])
        gated, conved, mean_ready, centred, squared, var_ready, sd_ready, normed, step = (ph.sem(s) for s in (
            "gated", "conved", "mean_ready", "centred", "squared", "var_ready", "sd_ready", "normed", "step"))
        with nc.Block() as block:
            @block.scalar
            def _(act):
                for c in range(C):
                    nc.scalar.activation(g[:, c, :], g[:, c, :], ACT.Sigmoid).then_inc(gated, 1)
                for c in range(C):
                    act.wait_ge(centred, c + 1)
                    nc.scalar.activation(sq[:, c, :], y[:, c, :], ACT.Square).then_inc(squared, 1)
                act.wait_ge(var_ready, 1)
                nc.scalar.activation(sd[:], var_ps[:], ACT.Sqrt, bias=cst["eps"], scale=1.0 / (C * P)).then_inc(sd_ready, 1)
                for c in range(C):
                    act.wait_ge(normed, c + 1)
                    nc.scalar.activation(a[:, c, :], y[:, c, :], ACT.Silu, bias=ln_b[:, c:c + 1])

            @block.tensor
            def _(pe):
                for o, w in parts:
                    for c in range(C):
                        pe.wait_ge(conved, c + 1)
                        mm = nc.tensor.matmul(mean_ps[:, o:o + w], cst["ones"], y[:, c, o:o + w], start=(c == 0),
                                              stop=(c == C - 1))
                mm.then_inc(mean_ready, 1)
                for o, w in parts:
                    for c in range(C):
                        pe.wait_ge(squared, c + 1)
                        mm = nc.tensor.matmul(var_ps[:, o:o + w], cst["ones"], sq[:, c, o:o + w], start=(c == 0),
                                              stop=(c == C - 1))
                mm.then_inc(var_ready, 1)

            @block.vector
            def _(dve):
                st = Steps(dve, step)
                for c in range(C):
                    dve.wait_ge(gated, c + 1)
                    st.done(nc.vector.tensor_tensor(a[:, c, :], a[:, c, :], g[:, c, :], ALU.mult))
                    st.done(nc.vector.tensor_scalar(y[:, c, :], a[:, c, :], taps[:, c, half:half + 1],
                                                    taps_b[:, c:c + 1], ALU.mult, ALU.add))
                    for t in range(K):
                        if t == half:
                            continue
                        s = t - half
                        lo, hi = max(0, -s), T - max(0, s)
                        st.done(nc.vector.scalar_tensor_tensor(out=y[:, c, lo:hi], in0=a[:, c, lo + s:hi + s],
                                                               scalar=taps[:, c, t:t + 1], in1=y[:, c, lo:hi],
                                                               op0=ALU.mult, op1=ALU.add))
                    dve.sem_inc(conved, 1)
                dve.wait_ge(mean_ready, 1)
                for c in range(C):
                    nc.vector.scalar_tensor_tensor(out=y[:, c, :], in0=mean_ps[:], scalar=-1.0 / (C * P),
                                                   in1=y[:, c, :], op0=ALU.mult, op1=ALU.add).then_inc(centred, 1)
                dve.wait_ge(sd_ready, 1)
                st.done(nc.vector.reciprocal(sd[:], sd[:]))
                for c in range(C):
                    nc.vector.scalar_tensor_tensor(out=y[:, c, :], in0=y[:, c, :], scalar=ln_g[:, c:c + 1],
                                                   in1=sd[:], op0=ALU.mult, op1=ALU.mult).then_inc(normed, 1)


def ffn_up(nc, tag, w_dram, src, hidden):
    K = len(src)
    W = K * 2 * P
    parts = chunks(T)
    with Phase(nc, tag) as ph:
        w = ph.sb("w", [P, 2, W + 8])
        y = ph.sb("y", [P, 2, T])
        acc = ph.ps("acc", [P, 2, 2, T // 2])
        acc2 = ph.ps("acc2", [P, 2, 2, T // 2])
        accs = (acc, acc2)
        w_ready = [ph.sem("w_ready0"), ph.sem("w_ready1")]
        mm_done, middle, conved, silu_done, hid_done, step = (ph.sem(s) for s in (
            "mm_done", "middle", "conved", "silu_done", "hid_done", "step"))
        with nc.Block() as block:
            @block.sync
            def _(sp):
                with sp.Fori(0, KF // 2) as i:
                    for u in range(2):
                        sp.wait_ge(hid_done, i * 2 + (u + 1))
                        sp.dma_start(w[:, u], w_dram[bass.ds(i * 2 + u, 1)].rearrange(
                            "a p n -> p (a n)")).then_inc(w_ready[u], 16)

            @block.tensor
            def _(pe):
                with pe.Fori(0, KF // 2) as i:
                    for u in range(2):
                        pe.wait_ge(w_ready[u], i * 16 + 16)
                        pe.wait_ge(hid_done, i * 2 + (u + 1))
                        for s in range(2):
                            for c, (a, width) in enumerate(parts):
                                for k in range(K):
                                    mm = nc.tensor.matmul(accs[u][:, s, c, :], w[:, u, (2 * k + s) * P:(2 * k + s + 1) * P],
                                                          src[k][:, a:a + width], start=(k == 0), stop=(k == K - 1))
                            mm.then_inc(mm_done, 1)

            @block.scalar
            def _(act):
                with act.Fori(0, KF // 2) as i:
                    for u in range(2):
                        act.wait_ge(hid_done, i * 2 + (u + 2))
                        for s in range(2):
                            act.wait_ge(mm_done, i * 4 + (2 * u + s + 1))
                            f = accs[u][:, s].rearrange("p c n -> p (c n)")
                            nc.scalar.activation(y[:, s, :], f, ACT.Identity, bias=w[:, u, W + 4 * s + 3:W + 4 * s + 4],
                                                 scale=w[:, u, W + 4 * s + 1:W + 4 * s + 2]).then_inc(middle, 1)
                        act.wait_ge(conved, i * 2 + (u + 1))
                        nc.scalar.activation(y[:, 0, :], y[:, 0, :], ACT.Silu).then_inc(silu_done, 1)

            @block.vector
            def _(dve):
                st = Steps(dve, step)
                dve.sem_inc(hid_done, 2)
                with dve.Fori(0, KF // 2) as i:
                    st.enter(i, 8)
                    for u in range(2):
                        for s in range(2):
                            dve.wait_ge(middle, i * 4 + (2 * u + s + 1))
                            f = accs[u][:, s].rearrange("p c n -> p (c n)")
                            st.done(nc.vector.scalar_tensor_tensor(out=y[:, s, 1:T], in0=f[:, 0:T - 1],
                                                                   scalar=w[:, u, W + 4 * s:W + 4 * s + 1],
                                                                   in1=y[:, s, 1:T], op0=ALU.mult, op1=ALU.add))
                            st.done(nc.vector.scalar_tensor_tensor(out=y[:, s, 0:T - 1], in0=f[:, 1:T],
                                                                   scalar=w[:, u, W + 4 * s + 2:W + 4 * s + 3],
                                                                   in1=y[:, s, 0:T - 1], op0=ALU.mult, op1=ALU.add))
                            if s == 0:
                                dve.sem_inc(conved, 1)
                        dve.wait_ge(silu_done, i * 2 + (u + 1))
                        nc.vector.tensor_tensor(at(hidden, i * 2 + u), y[:, 0, :], y[:, 1, :], ALU.mult).then_inc(hid_done, 1)
                st.leave(KF // 2)




def modulation(nc, tag, cst, vecs, din, mod, a1, ac, a2, ac_shift, neg_lam, sub_g):
    with Phase(nc, tag + "s") as ph:
        cs = ph.sb("cs", [P, 2, KD])
        act_c = ph.sb("act_c", [P, KD, 2])
        lam = ph.sb("lam", [P, 2])
        sum_ps = ph.ps("sum", [P, 2])
        silu_done, step, prod_ready, sum_ready, exp_ready, ready = (ph.sem(s) for s in (
            "silu_done", "step", "prod_ready", "sum_ready", "exp_ready", "ready"))
        with nc.Block() as block:
            @block.scalar
            def _(act):
                nc.scalar.activation(cs[:].rearrange("p a k -> p (a k)"), vecs["c"], ACT.Silu).then_inc(silu_done, 1)
                act.wait_ge(sum_ready, 1)
                nc.scalar.activation(lam[:], sum_ps[:], ACT.Exp).then_inc(exp_ready, 1)

            @block.tensor
            def _(pe):
                pe.wait_ge(prod_ready, 1)
                nc.tensor.matmul(sum_ps[:], cst["ones"], lam[:], start=True, stop=True).then_inc(sum_ready, 1)

            @block.vector
            def _(dve):
                st = Steps(dve, step)
                l = vecs["lam"]
                nc.vector.tensor_tensor(lam[:, 0:1], l[:, 0:1], l[:, 1:2], ALU.mult)
                nc.vector.tensor_tensor(lam[:, 1:2], l[:, 2:3], l[:, 3:4], ALU.mult).then_inc(prod_ready, 1)
                dve.wait_ge(silu_done, 1)
                for a in range(2):
                    nc.vector.tensor_copy(act_c[:, :, a:a + 1], cs[:, a, :].unsqueeze(2))
                nc.vector.tensor_scalar(sub_g, vecs["sub_g"], 0.8, None, ALU.mult)
                dve.wait_ge(exp_ready, 1)
                st.done(nc.vector.tensor_tensor(neg_lam, lam[:, 1:2], lam[:, 0:1], ALU.subtract))
                nc.vector.tensor_scalar(neg_lam, neg_lam, -0.2, None, ALU.add)
        project(nc, tag, din["w_mod"], cols(act_c), 2, 6 * KD, dst=mod)
    with Phase(nc, tag + "g") as ph:
        step = ph.sem("step")
        with nc.Block() as block:
            @block.vector
            def _(dve):
                st = Steps(dve, step)
                for a in range(2):
                    st.done(nc.vector.tensor_tensor(mod[:, :, a], mod[:, :, a], vecs["b_mod"], ALU.add))
                for o, g, j, a in ((a1, "g1", 1, 0), (ac, "g1", 1, 1), (a2, "g2", 4, 0)):
                    nc.vector.scalar_tensor_tensor(out=o, in0=mod[:, j * KD:(j + 1) * KD, a], scalar=1.0,
                                                   in1=vecs[g], op0=ALU.add, op1=ALU.mult)
                nc.vector.tensor_copy(ac_shift, mod[:, 0:KD, 1])


def gla_decay(nc, tag, cst, w_dec, b_dec, low, n, decay):
    parts = chunks(n)
    with Phase(nc, tag) as ph:
        z = ph.sb("z", [P, 2, n])
        e = ph.sb("e", [P, 2, n])
        z_ps = ph.ps("z_ps", [P, 2, len(parts) * BANK])
        z_ready, z_kept, log_ready, sum_ready, step, own = (ph.sem(s) for s in (
            "z_ready", "z_kept", "log_ready", "sum_ready", "step", "own"))
        with nc.Block() as block:
            @block.tensor
            def _(pe):
                for d in range(2):
                    for a, w in parts:
                        mm = nc.tensor.matmul(z_ps[:, d, a:a + w], w_dec[0:32, d, :], low[0:32, a:a + w], start=True,
                                              stop=True)
                    mm.then_inc(z_ready, 1)

            @block.scalar
            def _(act):
                st = Steps(act, own)
                for d in range(2):
                    act.wait_ge(z_ready, d + 1)
                    st.done(nc.scalar.activation(z[:, d, :], z_ps[:, d, 0:n], ACT.Identity, bias=b_dec[:, d:d + 1]))
                    act.sem_inc(z_kept, 1)
                    st.done(nc.scalar.activation(e[:, d, :], z[:, d, :], ACT.Abs))
                    st.done(nc.scalar.activation(e[:, d, :], e[:, d, :], ACT.Exp, scale=-1.0))
                    nc.scalar.activation(e[:, d, :], e[:, d, :], ACT.Ln, bias=cst["one"]).then_inc(log_ready, 1)
                for d in range(2):
                    act.wait_ge(sum_ready, d + 1)
                    nc.scalar.activation(decay[:, d, :], z[:, d, :], ACT.Exp, scale=1.0 / 16)

            @block.vector
            def _(dve):
                for d in range(2):
                    dve.wait_ge(log_ready, d + 1)
                    nc.vector.scalar_tensor_tensor(out=z[:, d, :], in0=z[:, d, :], scalar=0.0, in1=e[:, d, :],
                                                   op0=ALU.min, op1=ALU.subtract).then_inc(sum_ready, 1)


def gla_context(nc, tag, cst, k, vb, decay, state):
    n = NCTX
    with Phase(nc, tag) as ph:
        tail = ph.sb("tail", [P, 2, n])
        zero = ph.sb("zero", [P, n])
        kt = ph.sb("kt", [P, 2, 2, P])
        t_ps = ph.ps("t_ps", [P, 2, 2, P])
        s_ps = ph.ps("s_ps", [P, 2, 4 * 64])
        scaled, turned, kept, done, step = (ph.sem(s) for s in ("scaled", "turned", "kept", "done", "step"))
        with nc.Block() as block:
            @block.vector
            def _(dve):
                st = Steps(dve, step)
                nc.vector.memset(zero[:], 0.0)
                nc.vector.memset(tail[:, 0, n - 1:n], 1.0)
                st.done(nc.vector.memset(tail[:, 1, 0:1], 1.0))
                nc.vector.tensor_tensor_scan(tail[:, 0, n - 2::-1], decay[:, 0, n - 1:0:-1], zero[:, 1:n], 1.0,
                                             ALU.mult, ALU.add)
                st.done(nc.vector.tensor_tensor_scan(tail[:, 1, 1:n], decay[:, 1, 0:n - 1], zero[:, 1:n], 1.0,
                                                     ALU.mult, ALU.add))
                for d in range(2):
                    nc.vector.tensor_tensor(tail[:, d, :], tail[:, d, :], k, ALU.mult).then_inc(scaled, 1)
                dve.wait_ge(turned, 1)
                nc.vector.tensor_copy(kt[:], t_ps[:]).then_inc(kept, 1)
                dve.wait_ge(done, 1)
                for d in range(2):
                    for h in range(4):
                        r = slice(32 * h, 32 * h + 32)
                        nc.vector.tensor_copy(state[r, :, d], s_ps[r, d, 64 * h:64 * h + 64])

            @block.tensor
            def _(pe):
                pe.wait_ge(scaled, 2)
                for d in range(2):
                    for t in range(2):
                        mm = nc.tensor.transpose(t_ps[:, d, t, :], tail[:, d, t * P:(t + 1) * P], cst["ident"])
                mm.then_inc(turned, 1)
                pe.wait_ge(kept, 1)
                for d in range(2):
                    for t in range(2):
                        mm = nc.tensor.matmul(s_ps[:, d, :], kt[:, d, t, :], vb[:, t, :], start=(t == 0), stop=(t == 1))
                mm.then_inc(done, 1)


def gla_scan(nc, tag, cst, q, k, decay, state, v_dram, o_dram):
    DV = 64
    with Phase(nc, tag) as ph:
        vb = ph.sb("vb", [P, 2, T])
        kv = ph.sb("kv", [P, 2, T])
        s = ph.sb("s", [P, 2, 2, T])
        qs = ph.sb("qs", [P, 2, T])
        init = ph.sb("init", [P, 2, 2])
        orow = ph.sb("orow", [4, 2, T])
        o_ps = ph.ps("o_ps", [P, 2, T])
        v_ready = [ph.sem("v_ready0"), ph.sem("v_ready1")]
        stored = [ph.sem("stored0"), ph.sem("stored1")]
        kv_ready, scanned, summed, weighted, o_ready, o_kept, step, qscaled = (ph.sem(x) for x in (
            "kv_ready", "scanned", "summed", "weighted", "o_ready", "o_kept", "step", "qscaled"))
        with nc.Block() as block:
            @block.sync
            def _(sp):
                with sp.Fori(0, DV // 2) as i:
                    for u in range(2):
                        sp.wait_ge(kv_ready, i * 2 + (u + 1))
                        for h in range(4):
                            row = v_dram[h, bass.ds(i * 2 + u, 1), :].rearrange("a t -> (a t)")
                            sp.dma_start(vb[32 * h:32 * h + 32, u, :], row.partition_broadcast(32)).then_inc(v_ready[u], 16)

            @block.gpsimd
            def _(pool):
                pool.sem_inc(kv_ready, 2)
                with pool.Fori(0, DV // 2) as i:
                    def outer(j, u):
                        pool.wait_ge(v_ready[u], j * 64 + 64)
                        pool.wait_ge(scanned, j * 2 + (u + 1))
                        nc.gpsimd.tensor_tensor(kv[:, u, :], k, vb[:, u, :], ALU.mult).then_inc(kv_ready, 1)

                    for u in range(2):
                        outer(i, u)
                    for u in range(2):
                        pool.wait_ge(scanned, i * 2 + (u + 3))
                        nc.gpsimd.tensor_tensor(s[:, u, 0, :], s[:, u, 0, :], s[:, u, 1, :], ALU.add).then_inc(summed, 1)

            @block.vector
            def _(dve):
                st = Steps(dve, step)
                dve.sem_inc(scanned, 2)
                st.done(nc.vector.tensor_scalar(q, q, 32.0 ** -0.5, None, ALU.mult))
                with dve.Fori(0, DV // 2) as i:
                    st.enter(i, 2)

                    def scan(u):
                        dve.wait_ge(kv_ready, i * 2 + (u + 3))
                        st.done(nc.vector.tensor_copy(init[:, u, :], at(state, i * 2 + u)))
                        nc.vector.tensor_tensor_scan(s[:, u, 0, :], decay[:, 0, :], kv[:, u, :], init[:, u, 0:1],
                                                     ALU.mult, ALU.add)
                        nc.vector.tensor_tensor_scan(s[:, u, 1, ::-1], decay[:, 1, ::-1], kv[:, u, ::-1],
                                                     init[:, u, 1:2], ALU.mult, ALU.add).then_inc(scanned, 1)

                    def weigh(u):
                        dve.wait_ge(summed, i * 2 + (u + 1))
                        dve.wait_ge(o_ready, i * 2 + (u + 1))
                        nc.vector.tensor_tensor(qs[:, u, :], s[:, u, 0, :], q, ALU.mult).then_inc(weighted, 1)

                    scan(0)
                    scan(1)
                    weigh(0)
                    weigh(1)
                st.leave(DV // 2)

            @block.tensor
            def _(pe):
                pe.sem_inc(o_ready, 2)
                with pe.Fori(0, DV // 2) as i:
                    for u in range(2):
                        pe.wait_ge(weighted, i * 2 + (u + 1))
                        pe.wait_ge(o_kept, i * 2 + (u + 1))
                        for a, w in chunks(T):
                            mm = nc.tensor.matmul(o_ps[0:4, u, a:a + w], cst["heads32"], qs[:, u, a:a + w], start=True,
                                                  stop=True)
                        mm.then_inc(o_ready, 1)

            @block.scalar
            def _(act):
                act.sem_inc(o_kept, 2)
                act.sem_inc(stored[0], 16)
                act.sem_inc(stored[1], 16)
                with act.Fori(0, DV // 2) as i:
                    for u in range(2):
                        act.wait_ge(o_ready, i * 2 + (u + 3))
                        act.wait_ge(stored[u], i * 16 + 16)
                        nc.scalar.activation(orow[:, u, :], o_ps[0:4, u, :], ACT.Copy).then_inc(o_kept, 1)
                        act.wait_ge(o_kept, i * 2 + (u + 3))
                        act.dma_start(o_dram[:, bass.ds(i * 2 + u, 1), :].rearrange("h a t -> h (a t)"),
                                      orow[:, u, :]).then_inc(stored[u], 16)
                for u in range(2):
                    act.wait_ge(stored[u], 16 + 16 * (DV // 2))


def gated(nc, tag, x, gate):
    with Phase(nc, tag) as ph:
        silu_done = ph.sem("silu_done")
        with nc.Block() as block:
            @block.scalar
            def _(act):
                for c in range(x.shape[1]):
                    nc.scalar.activation(gate[:, c, :], gate[:, c, :], ACT.Silu).then_inc(silu_done, 1)

            @block.vector
            def _(dve):
                for c in range(x.shape[1]):
                    dve.wait_ge(silu_done, c + 1)
                    nc.vector.tensor_tensor(x[:, c, :], x[:, c, :], gate[:, c, :], ALU.mult)


E_ = 32
NB = 48
NBI = NB + 1
TT = T // P


def router(nc, tag, cst, vecs, din, n, h2_dram, r):
    with Phase(nc, tag) as ph:
        w = ph.sb("w", [P, KD, 36])
        lgT = ph.sb("lgT", [36, T])
        row = ph.sb("row", [P, 2, D])
        lg = ph.sb("lg", [P, TT, 36])
        pen, le, cand, eq = (ph.sb(x, [P, TT, E_]) for x in ("pen", "le", "cand", "eq"))
        oh = ph.sb("oh", [P, 2, TT, E_])
        both = ph.sb("both", [P, TT, E_])
        g4, g4b = ph.sb("g4", [P, TT, 4]), ph.sb("g4b", [P, TT, 4])
        c1, top, low, pg = (ph.sb(x, [P, TT]) for x in ("c1", "top", "low", "pg"))
        base, nblk, incl, onesr = (ph.sb(x, [P, E_]) for x in ("base", "nblk", "incl", "onesr"))
        cmp = ph.sb("cmp", [P, NB, E_])
        bex, cnt = ph.sb("bex", [P, NB]), ph.sb("cnt", [P, 2])
        slotf, blkf = ph.sb("slotf", [P, 2, TT]), ph.sb("blkf", [P, 2, TT])
        l_ps = ph.ps("l_ps", [P, T])
        lt_ps = ph.ps("lt_ps", [P, TT, 36])
        r_ps = ph.ps("r_ps", [P, 2, T // 2])
        pre_ps = ph.ps("pre_ps", [P, TT, E_])
        tot_ps = ph.ps("tot_ps", [P, E_])
        loaded, l_ready, l_kept, lt_ready, lt_kept, row_ready, row_kept, stored, stepv, exp_a, exp_a_done = (
            ph.sem(x) for x in ("loaded", "l_ready", "l_kept", "lt_ready", "lt_kept", "row_ready", "row_kept", "stored",
                                "step", "exp_a", "exp_a_done"))
        both_ready, pre_ready, row_stored = ph.sem("both_ready"), ph.sem("pre_ready"), [ph.sem("row_stored0"), ph.sem("row_stored1")]
        with nc.Block() as block:
            @block.sync
            def _(sp):
                sp.dma_start(w[:], din["w_route"]).then_inc(loaded, 16)
                for t in range(TT):
                    sp.wait_ge(row_kept, 2 * (t + 1))
                    sp.dma_start(h2_dram[t * P:(t + 1) * P, :], row[:, t % 2, :]).then_inc(row_stored[t % 2], 16)
                for u in range(2):
                    sp.wait_ge(row_stored[u], 16 * TT // 2)

            @block.tensor
            def _(pe):
                pe.wait_ge(loaded, 16)
                for a, wd in chunks(T):
                    for k in range(KD):
                        mm = nc.tensor.matmul(l_ps[0:36, a:a + wd], w[:, k, :], n[:, k, a:a + wd], start=(k == 0),
                                              stop=(k == KD - 1))
                mm.then_inc(l_ready, 1)
                pe.wait_ge(l_kept, 1)
                for t in range(TT):
                    mm = nc.tensor.transpose(lt_ps[:, t, :], lgT[:, t * P:(t + 1) * P], cst["ident"][0:36, 0:36])
                mm.then_inc(lt_ready, 1)
                for t in range(TT):
                    for half in range(2):
                        j = 2 * t + half
                        if j >= 2:
                            pe.wait_ge(row_kept, j - 1)
                        for k in range(4):
                            mm = nc.tensor.transpose(r_ps[:, half, k * P:(k + 1) * P],
                                                     n[:, half * 4 + k, t * P:(t + 1) * P], cst["ident"])
                        mm.then_inc(row_ready, 1)
                pe.wait_ge(both_ready, 1)
                for t in range(TT):
                    for s in range(t):
                        nc.tensor.matmul(pre_ps[:, t, :], cst["ones"], both[:, s, :], start=(s == 0), stop=False)
                    nc.tensor.matmul(pre_ps[:, t, :], cst["before"], both[:, t, :], start=(t == 0), stop=True)
                for t in range(TT):
                    mm = nc.tensor.matmul(tot_ps[:], cst["ones"], both[:, t, :], start=(t == 0), stop=(t == TT - 1))
                mm.then_inc(pre_ready, 1)

            @block.scalar
            def _(act):
                act.wait_ge(l_ready, 1)
                nc.scalar.activation(lgT[:], l_ps[0:36, :], ACT.Identity, bias=vecs["b_route"][0:36]).then_inc(l_kept, 1)
                for t in range(TT):
                    for half in range(2):
                        j = 2 * t + half
                        if half == 0 and t >= 2:
                            act.wait_ge(row_stored[t % 2], 16 * (t // 2))
                        act.wait_ge(row_ready, j + 1)
                        nc.scalar.activation(row[:, t % 2, half * 512:half * 512 + 512], r_ps[:, half, :],
                                             ACT.Copy).then_inc(row_kept, 1)
                for j, (x, flat) in enumerate(((g4, "p t g -> p (t g)"), (top, None))):
                    act.wait_ge(exp_a, j + 1)
                    y = x[:].rearrange(flat) if flat else x[:]
                    nc.scalar.activation(y, y, ACT.Exp).then_inc(exp_a_done, 1)

            @block.vector
            def _(dve):
                st = Steps(dve, stepv)
                V = nc.vector

                def spread(x, m):
                    return x.unsqueeze(2).broadcast_to([P, TT, m])

                def choose(logits, m, onehot, best, tmp):
                    index = cst["index"][:, 0:m].unsqueeze(1).broadcast_to([P, TT, m])
                    st.done(V.tensor_reduce(best, logits, AX.X, ALU.max))
                    st.done(V.tensor_tensor(tmp, logits, spread(best, m), ALU.is_equal))
                    st.done(V.tensor_tensor(tmp, tmp, index, ALU.mult))
                    st.done(V.tensor_reduce(c1[:], tmp, AX.X, ALU.min))
                    st.done(V.tensor_tensor(onehot, tmp, spread(c1[:], m), ALU.is_equal))

                dve.wait_ge(lt_ready, 1)
                st.done(V.tensor_copy(lg[:], lt_ps[:]))
                lgG = lg[:, :, 0:4]
                choose(lgG, 4, g4b[:], pg[:], g4[:])
                st.done(V.tensor_tensor(g4[:], lgG, spread(pg[:], 4), ALU.subtract))
                dve.sem_inc(exp_a, 1)
                st.done(V.tensor_scalar(g4b[:], g4b[:], -1.0, 1e30, ALU.add, ALU.mult))
                for g in range(4):
                    st.done(V.tensor_tensor(le[:, :, g * 8:g * 8 + 8], lg[:, :, 4 + g * 8:12 + g * 8],
                                            g4b[:, :, g:g + 1].broadcast_to([P, TT, 8]), ALU.add))
                choose(le[:], E_, oh[:, 0], top[:], cand[:])
                st.done(V.scalar_tensor_tensor(out=pen[:], in0=oh[:, 0], scalar=-2e30, in1=le[:], op0=ALU.mult,
                                               op1=ALU.add))
                choose(pen[:], E_, oh[:, 1], low[:], cand[:])
                st.done(V.tensor_tensor(top[:], low[:], top[:], ALU.subtract))
                dve.sem_inc(exp_a, 1)
                st.done(V.tensor_tensor(both[:], oh[:, 0], oh[:, 1], ALU.add))
                dve.sem_inc(both_ready, 1)
                dve.wait_ge(exp_a_done, 2)
                st.done(V.tensor_reduce(pg[:], g4[:], AX.X, ALU.add))
                st.done(V.tensor_scalar(low[:], top[:], 1.0, None, ALU.add))
                st.done(V.tensor_tensor(low[:], low[:], pg[:], ALU.mult))
                st.done(V.reciprocal(r["gate"][:, 0], low[:]))
                st.done(V.tensor_tensor(r["gate"][:, 1], r["gate"][:, 0], top[:], ALU.mult))
                dve.wait_ge(pre_ready, 1)
                st.done(V.tensor_scalar(nblk[:], tot_ps[:], 127.0, 1.0 / P, ALU.add, ALU.mult))
                st.done(V.tensor_scalar(nblk[:], nblk[:], -0.498, None, ALU.add))
                st.done(V.tensor_scalar(nblk[:], nblk[:], 12582912.0, None, ALU.add))
                st.done(V.tensor_scalar(nblk[:], nblk[:], 12582912.0, None, ALU.subtract))
                st.done(V.memset(onesr[:], 1.0))
                st.done(V.tensor_tensor_scan(incl[:], onesr[:], nblk[:], 0.0, ALU.mult, ALU.add))
                st.done(V.tensor_copy(cnt[:, 0:1], incl[:, E_ - 1:E_]))
                st.done(V.tensor_scalar(cnt[:, 1:2], cnt[:, 0:1], 1.0, 0.5, ALU.add, ALU.mult))
                st.done(V.tensor_scalar(cnt[:, 1:2], cnt[:, 1:2], -0.25, None, ALU.add))
                st.done(V.tensor_scalar(cnt[:, 1:2], cnt[:, 1:2], 12582912.0, None, ALU.add))
                st.done(V.tensor_scalar(cnt[:, 1:2], cnt[:, 1:2], 12582912.0, None, ALU.subtract))
                st.done(V.tensor_copy(r["count"], cnt[:]))
                st.done(V.tensor_tensor(base[:], incl[:], nblk[:], ALU.subtract))
                st.done(V.tensor_scalar(base[:], base[:], float(P), None, ALU.mult))
                st.done(V.tensor_tensor(le[:], pre_ps[:], base[:].unsqueeze(1).broadcast_to([P, TT, E_]), ALU.add))
                for a in range(2):
                    st.done(V.tensor_tensor(cand[:], oh[:, a], le[:], ALU.mult))
                    st.done(V.tensor_reduce(slotf[:, a], cand[:], AX.X, ALU.add))
                st.done(V.tensor_copy(r["slot"], slotf[:]))
                st.done(V.tensor_scalar(blkf[:], slotf[:], 1.0 / P, -0.498, ALU.mult, ALU.add))
                st.done(V.tensor_scalar(blkf[:], blkf[:], 12582912.0, None, ALU.add))
                st.done(V.tensor_scalar(blkf[:], blkf[:], 12582912.0, 1.0 - P * NBI, ALU.subtract, ALU.mult))
                st.done(V.scalar_tensor_tensor(out=slotf[:], in0=slotf[:], scalar=float(NBI), in1=blkf[:],
                                               op0=ALU.mult, op1=ALU.add))
                st.done(V.tensor_copy(r["place"], slotf[:]))
                st.done(V.tensor_tensor(cmp[:], incl[:].unsqueeze(1).broadcast_to([P, NB, E_]),
                                        cst["block"].unsqueeze(2).broadcast_to([P, NB, E_]), ALU.is_le))
                st.done(V.tensor_reduce(bex[:], cmp[:], AX.X, ALU.add))
                st.done(V.tensor_scalar(bex[:], bex[:], float(E_ - 1), None, ALU.min))
                st.done(V.tensor_copy(r["block"], bex[:]))


def dispatch(nc, tag, cst, r, ids_dram, ids):
    with Phase(nc, tag) as ph:
        token = ph.sb("token", [P, TT], I32)
        zero = ph.sb("zero", [P, NBI], I32)
        made, cleared, scattered, read = (ph.sem(x) for x in ("made", "cleared", "scattered", "read"))
        with nc.Block() as block:
            @block.gpsimd
            def _(pool):
                nc.gpsimd.memset(zero[:], 0).then_inc(made, 1)
                nc.gpsimd.iota(token[:], [[P, TT]], base=0, channel_multiplier=1).then_inc(made, 1)
                pool.wait_ge(made, 2)
                pool.dma_start(ids_dram.rearrange("(p b) a -> p (b a)", b=NBI), zero[:]).then_inc(cleared, 16)
                pool.wait_ge(cleared, 16)
                for a in range(2):
                    for t in range(TT):
                        pool.indirect_dma_start(ids_dram, bass.IndirectOffsetOnAxis(ap=r["place"][:, a, t:t + 1], axis=0),
                                                token[:, t:t + 1], None).then_inc(scattered, 16)
                pool.wait_ge(scattered, 16 * 2 * TT)
                pool.dma_start(ids, ids_dram.rearrange("(p b) a -> p (b a)", b=NBI)).then_inc(read, 16)
                pool.wait_ge(read, 16)


def experts(nc, tag, cst, din, r, ids, h2_dram, y_dram, y_filled):
    H = 512
    KH = H // P
    with Phase(nc, tag) as ph:
        wu = ph.sb("wu", [P, 2, KD, 2 * H])
        wd = ph.sb("wd", [P, 2, KH, D])
        xb = ph.sb("xb", [P, 2, D])
        xT = ph.sb("xT", [P, 2, KD, P])
        idx = ph.sb("idx", [P, 2], I32)
        hid = ph.sb("hid", [P, 2, H])
        hT = ph.sb("hT", [P, KH, P])
        y = ph.sb("y", [P, 2, D])
        x_ps = ph.ps("x_ps", [P, KD, P])
        up_ps = ph.ps("up_ps", [P, 2, H])
        h_ps = ph.ps("h_ps", [P, KH, P])
        y_ps = ph.ps("y_ps", [P, D])
        u_ready = [ph.sem("u_ready0"), ph.sem("u_ready1")]
        d_ready = [ph.sem("d_ready0"), ph.sem("d_ready1")]
        x_ready = [ph.sem("x_ready0"), ph.sem("x_ready1")]
        stored = [ph.sem("stored0"), ph.sem("stored1")]
        idx_seen = ph.sem("idx_seen")
        idx_set, turned, xT_ready, up_done, silu_done, hid_ready, h_turned, hT_ready, y_done, y_kept = (ph.sem(x) for x in (
            "idx_set", "turned", "xT_ready", "up_done", "silu_done", "hid_ready", "h_turned", "hT_ready", "y_done",
            "y_kept"))

        def used(eng):
            return eng.value_load(r["count"][0:1, 0:1], min_val=1, max_val=NB)

        with nc.Block() as block:
            @block.sync
            def _(sp):
                nb = used(sp)
                with sp.Fori(0, NB // 2) as i:
                    with sp.If(i * 2 < nb):
                        for u in range(2):
                            e = sp.value_load(r["block"][0:1, bass.ds(i * 2 + u, 1)], min_val=0, max_val=E_ - 1)
                            sp.wait_ge(up_done, i * 2 + (u + 1))
                            sp.dma_start(wu[:, u], din["w_eup"][bass.ds(e, 1)].rearrange(
                                "a (k p) n -> p (a k) n", p=P)).then_inc(u_ready[u], 16)
                            sp.wait_ge(y_done, i * 2 + (u + 1))
                            sp.dma_start(wd[:, u], din["w_edown"][bass.ds(e, 1)].rearrange(
                                "a (k p) n -> p (a k) n", p=P)).then_inc(d_ready[u], 16)

            @block.gpsimd
            def _(pool):
                nb = used(pool)

                def gather(i, u, nth):
                    nc.gpsimd.tensor_copy(idx[:, u:u + 1], ids[:, bass.ds(i * 2 + u, 1)]).then_inc(idx_set, 1)
                    pool.wait_ge(idx_set, nth)
                    pool.sem_inc(idx_seen, 1)
                    pool.indirect_dma_start(xb[:, u, :], None, h2_dram,
                                            bass.IndirectOffsetOnAxis(ap=idx[:, u:u + 1], axis=0)).then_inc(x_ready[u], 16)

                gather(0, 0, 1)
                with pool.Fori(0, NB // 2) as i:
                    with pool.If(i * 2 < nb):
                        pool.wait_ge(turned, i * 2 + 1)
                        gather(i, 1, i * 2 + 2)
                        pool.wait_ge(turned, i * 2 + 2)
                        gather(i + 1, 0, i * 2 + 3)

            @block.tensor
            def _(pe):
                nb = used(pe)
                for s, n in ((turned, 1), (up_done, 2), (h_turned, 1), (y_done, 2)):
                    pe.sem_inc(s, n)

                def turn(i, u):
                    pe.wait_ge(x_ready[u], i * 16 + 16)
                    pe.wait_ge(xT_ready, i * 2 + (u + 1))
                    for k in range(KD):
                        mm = nc.tensor.transpose(x_ps[:, k, :], xb[:, u, k * P:(k + 1) * P], cst["ident"])
                    mm.then_inc(turned, 1)

                def up(i, u):
                    pe.wait_ge(xT_ready, i * 2 + (u + 2))
                    pe.wait_ge(u_ready[u], i * 16 + 16)
                    pe.wait_ge(hid_ready, i * 2 + (u + 1))
                    for s in range(2):
                        for k in range(KD):
                            mm = nc.tensor.matmul(up_ps[:, s, :], xT[:, u, k, :], wu[:, u, k, s * H:(s + 1) * H],
                                                  start=(k == 0), stop=(k == KD - 1))
                    mm.then_inc(up_done, 1)

                def down(i, u):
                    pe.wait_ge(hid_ready, i * 2 + (u + 2))
                    pe.wait_ge(hT_ready, i * 2 + (u + 1))
                    for k in range(KH):
                        mm = nc.tensor.transpose(h_ps[:, k, :], hid[:, 1, k * P:(k + 1) * P], cst["ident"])
                    mm.then_inc(h_turned, 1)
                    pe.wait_ge(hT_ready, i * 2 + (u + 2))
                    pe.wait_ge(d_ready[u], i * 16 + 16)
                    pe.wait_ge(y_kept, i * 2 + (u + 1))
                    for a, w in chunks(D):
                        for k in range(KH):
                            mm = nc.tensor.matmul(y_ps[:, a:a + w], hT[:, k, :], wd[:, u, k, a:a + w], start=(k == 0),
                                                  stop=(k == KH - 1))
                    mm.then_inc(y_done, 1)

                turn(0, 0)
                with pe.Fori(0, NB // 2) as i:
                    with pe.If(i * 2 < nb):
                        up(i, 0)
                        turn(i, 1)
                        down(i, 0)
                        up(i, 1)
                        turn(i + 1, 0)
                        down(i, 1)

            @block.scalar
            def _(act):
                nb = used(act)
                for s, n in ((stored[0], 16), (stored[1], 16), (xT_ready, 1), (y_kept, 1)):
                    act.sem_inc(s, n)

                def keep_x(i, u):
                    act.wait_ge(turned, i * 2 + (u + 2))
                    act.wait_ge(up_done, i * 2 + (u + 1))
                    nc.scalar.activation(xT[:, u], x_ps[:], ACT.Copy).then_inc(xT_ready, 1)

                def silu(i, u):
                    act.wait_ge(up_done, i * 2 + (u + 3))
                    act.wait_ge(hid_ready, i * 2 + (u + 1))
                    nc.scalar.activation(hid[:, 0, :], up_ps[:, 0, :], ACT.Silu).then_inc(silu_done, 1)

                def keep_y(i, u):
                    act.wait_ge(y_done, i * 2 + (u + 3))
                    act.wait_ge(stored[u], i * 16 + 16)
                    nc.scalar.activation(y[:, u, :], y_ps[:], ACT.Copy).then_inc(y_kept, 1)
                    act.wait_ge(y_kept, i * 2 + (u + 2))
                    act.dma_start(y_dram[bass.ds(i * 2 + u, 1)].rearrange("a p n -> p (a n)"),
                                  y[:, u, :]).then_inc(stored[u], 16)

                keep_x(0, 0)
                act.wait_ge(y_filled, 16 * NB)
                with act.Fori(0, NB // 2) as i:
                    with act.If(i * 2 < nb):
                        silu(i, 0)
                        keep_x(i, 1)
                        keep_y(i, 0)
                        silu(i, 1)
                        keep_x(i + 1, 0)
                        keep_y(i, 1)
                pairs = act.value_load(r["count"][0:1, 1:2], min_val=1, max_val=NB // 2)
                for u in range(2):
                    act.wait_ge(stored[u], pairs * 16 + 16)
                act.sem_inc(y_kept, 1)

            @block.vector
            def _(dve):
                nb = used(dve)
                dve.sem_inc(hid_ready, 1)
                dve.sem_inc(hT_ready, 1)
                with dve.Fori(0, NB // 2) as i:
                    with dve.If(i * 2 < nb):
                        for u in range(2):
                            dve.wait_ge(silu_done, i * 2 + (u + 1))
                            dve.wait_ge(h_turned, i * 2 + (u + 1))
                            nc.vector.tensor_tensor(hid[:, 1, :], hid[:, 0, :], up_ps[:, 1, :],
                                                    ALU.mult).then_inc(hid_ready, 1)
                            dve.wait_ge(h_turned, i * 2 + (u + 2))
                            dve.wait_ge(y_done, i * 2 + (u + 2))
                            nc.vector.tensor_copy(hT[:], h_ps[:]).then_inc(hT_ready, 1)


def combine(nc, tag, cst, r, y_dram, gate5, h):
    with Phase(nc, tag) as ph:
        f = ph.sb("f", [P, 2, 2, D])
        f_ps = ph.ps("f_ps", [P, 2, 4, P])
        got = [ph.sem("got0"), ph.sem("got1")]
        mixed, turned, added, step = (ph.sem(x) for x in ("mixed", "turned", "added", "step"))
        with nc.Block() as block:
            @block.gpsimd
            def _(pool):
                for t in range(TT):
                    if t >= 2:
                        pool.wait_ge(turned, 2 * (t - 1))
                    for a in range(2):
                        pool.indirect_dma_start(f[:, t % 2, a, :], None, y_dram,
                                                bass.IndirectOffsetOnAxis(ap=r["slot"][:, a, t:t + 1], axis=0)
                                                ).then_inc(got[t % 2], 16)

            @block.vector
            def _(dve):
                st = Steps(dve, step)
                for t in range(TT):
                    dve.wait_ge(got[t % 2], 32 * (t // 2 + 1))
                    st.done(nc.vector.tensor_scalar(f[:, t % 2, 0, :], f[:, t % 2, 0, :], r["gate"][:, 0, t:t + 1], None,
                                                    ALU.mult))
                    nc.vector.scalar_tensor_tensor(out=f[:, t % 2, 0, :], in0=f[:, t % 2, 1, :],
                                                   scalar=r["gate"][:, 1, t:t + 1], in1=f[:, t % 2, 0, :], op0=ALU.mult,
                                                   op1=ALU.add).then_inc(mixed, 1)
                    for half in range(2):
                        dve.wait_ge(turned, 2 * t + half + 1)
                        for k in range(4):
                            o = h[:, half * 4 + k, t * P:(t + 1) * P]
                            ins = nc.vector.scalar_tensor_tensor(out=o, in0=f_ps[:, half, k, :],
                                                                 scalar=gate5[:, half * 4 + k:half * 4 + k + 1], in1=o,
                                                                 op0=ALU.mult, op1=ALU.add)
                        ins.then_inc(added, 1)

            @block.tensor
            def _(pe):
                for t in range(TT):
                    pe.wait_ge(mixed, t + 1)
                    for half in range(2):
                        if t:
                            pe.wait_ge(added, 2 * t + half - 1)
                        for k in range(4):
                            mm = nc.tensor.transpose(f_ps[:, half, k, :], f[:, t % 2, 0, (half * 4 + k) * P:(half * 4 + k + 1) * P],
                                                     cst["ident"])
                        mm.then_inc(turned, 1)


def second_block(nc, din, cst, vecs, h, y_dram, y_filled, upto):
    h_dram = nc.dram_tensor("h_dram", (P, KD, T), F32).ap()
    v_dram = nc.dram_tensor("v_dram", (2, P, T), F32).ap()
    o_dram = nc.dram_tensor("o_dram", (2, P, T), F32).ap()
    with ExitStack() as outer:
        def keep(name, shape, dt=F32):
            return outer.enter_context(nc.sbuf_tensor(name, shape, dt))

        mod = keep("mod", [P, 6 * KD, 2])
        a1, ac, a2, shc = (keep(x, [P, KD]) for x in ("a1", "ac", "a2", "shc"))
        neg_lam, sub_g = keep("neg_lam", [P, 1]), keep("sub_g", [P, 4])
        modulation(nc, "md", cst, vecs, din, mod, a1[:], ac[:], a2[:], shc[:], neg_lam[:], sub_g[:])

        def m(j):
            return mod[:, j * KD:(j + 1) * KD, 0]

        store_all(nc, "sh", [(h_dram, h[:])])
        with ExitStack() as ctx:
            def sb(name, shape, dt=F32):
                return ctx.enter_context(nc.sbuf_tensor(name, shape, dt))

            pr = sb("pr", [P, 19, T])
            pc = sb("pc", [P, 8, NCTX])
            v2 = sb("v2", [P, TT + 2, 768])
            with nc.sbuf_tensor("vbc", [P, 2, 256], F32) as vbc, nc.sbuf_tensor("state", [P, 64, 2], F32) as state:
                rms_norm(nc, "m1", cst, h, h, a1, m(0))
                project(nc, "q2", din["w_in2"], cols(h), T, 19, dst=pr)
                project_rows(nc, "r2", din["w_v2"][:, :, 0:768], cols(h), T, v2)
                nctx = h[:, 0:2, :].rearrange("p a (b c) -> p (a b) c", c=NCTX)
                load_all(nc, "lc", [(nctx, din["ctx"])])
                rms_norm(nc, "mc", cst, nctx, nctx, ac, shc)
                project(nc, "qc", din["w_in2"], cols(nctx), NCTX, 8, dst=pc)
                project_rows(nc, "rc", din["w_v2"][:, :, 0:768], cols(nctx), NCTX, v2[:, TT:, :])
                project_rows(nc, "rb", din["w_v2"][:, :, 768:1024], cols(nctx), NCTX, vbc)
                if upto == 21:
                    return
                store_all(nc, "sv", [(v_dram.rearrange("a p t -> p a t"), pr[:, 15:17, :])])
                decay = h[:, 0:2, :]
                decay_c = h[:, 2, 0:2 * NCTX].rearrange("p (a t) -> p a t", a=2)
                wdec = h[:, 3, 0:2 * P].rearrange("p (a t) -> p a t", a=2)
                load_all(nc, "ldw", [(wdec[0:32], din["w_dec"])])
                gla_decay(nc, "dx", cst, wdec, vecs["b_dec"], pr[:, 7, :], T, decay)
                gla_decay(nc, "dc", cst, wdec, vecs["b_dec"], pc[:, 7, :], NCTX, decay_c)
                gla_context(nc, "gc", cst, pc[:, 6, :], vbc, decay_c, state)
                gla_scan(nc, "gs", cst, pr[:, 14, :], pr[:, 6, :], decay, state,
                         v_dram.rearrange("a (h v) t -> (a h) v t", v=64), o_dram.rearrange("a (h v) t -> (a h) v t", v=64))
                load_all(nc, "lo", [(pr[:, 15:17, :], o_dram.rearrange("a p t -> p a t"))])
            head_prep(nc, "hg", cst, pr[:, 15:17, :], T, 2, vecs["gla_g"])
            gated(nc, "gg", pr[:, 15:17, :], pr[:, 17:19, :])
            if upto == 22:
                return
            load_all(nc, "lt", [(h[:, 0, :], din["cos2"]), (h[:, 1, :], din["sin2"])])
            rope2 = (cst["rot2"], h[:, 0, :], h[:, 1, :])
            head_prep(nc, "ra", cst, pr[:, 0:4, :], T, 4, None, rope2)
            head_prep(nc, "rq", cst, pr[:, 8:12, :], T, 4, None, rope2)
            attention(nc, "ad", cst, 4, pr[:, 8:12, :], [(pr[:, 0:4, :], T), (pc[:, 0:4, :], NCTX)], v2[:, :, 0:512],
                      TT + 2, diff=neg_lam[:], scratch=h)
            head_prep(nc, "hs", cst, pr[:, 8:12, :], T, 4, sub_g[:], blk=("ones", P))
            with nc.sbuf_tensor("near", [P, TT, 640], F32) as near, nc.sbuf_tensor("tab", [P, 4, 18 * 64], F32) as tab:
                load_all(nc, "ln", [(near[:], din["near"]), (tab[:], din["rpb"])])

                def bias(m_, u, t):
                    d0 = min(max(2 * t - 4, 0), 6) - 2 * t + 8
                    return [at(tab, m_ * 2 + u)[:, d0 * 64:d0 * 64 + 640], near[:, t, :]]
                window = [[min(max(2 * t - 4, 0), 6) // 2 + x for x in range(5)] + [TT, TT + 1] for t in range(TT)]
                attention(nc, "an", cst, 2, pr[:, 12:14, :], [(pr[:, 4:6, :], T), (pc[:, 4:6, :], NCTX)],
                          v2[:, :, 512:768], TT + 2, bias=bias, window=window, scratch=h)
            if upto == 23:
                return
            load_all(nc, "lh", [(h[:], h_dram)])
            mixed = cols(pr[:, 8:12, :]) + cols(pr[:, 15:17, :]) + cols(pr[:, 12:14, :])
            project(nc, "o2", din["w_out2"], mixed, T, KD, add_to=h, gate=m(2))
        if upto == 24:
            return
        h2_dram = nc.dram_tensor("h2_dram", (T, D), F32).ap()
        ids_dram = nc.dram_tensor("ids_dram", (NBI * P, 1), I32).ap()
        slot, gates = keep("slot", [P, 2, TT], I32), keep("gates", [P, 2, TT])
        blk, ids = keep("blk", [P, NB], I32), keep("ids", [P, NBI], I32)
        place, count = keep("place", [P, 2, TT], I32), keep("count", [P, 2], I32)
        r = {"slot": slot[:], "place": place[:], "gate": gates[:], "block": blk[:], "count": count[:]}
        with nc.sbuf_tensor("n2", [P, KD, T], F32) as n:
            rms_norm(nc, "m2", cst, h, n, a2, m(3))
            router(nc, "ro", cst, vecs, din, n, h2_dram, r)
        dispatch(nc, "di", cst, r, ids_dram, ids[:])
        experts(nc, "ex", cst, din, r, ids[:], h2_dram, y_dram.rearrange("(b p) n -> b p n", p=P),
                y_filled)
        combine(nc, "co", cst, r, y_dram, m(5), h)
        rms_norm(nc, "fin", cst, h, h, vecs["final_g"])




def constants():
    f = np.float32
    ident = np.eye(P, dtype=f)
    blk64 = np.kron(np.eye(2), np.ones((64, 64))).astype(f)
    rot1 = np.zeros((P, P), f)
    rot2 = np.zeros((P, P), f)
    freq = np.zeros((P, 1), f)
    inv = (np.float32(500000.0) ** (-np.arange(0, 16, 2, dtype=f) / np.float32(16))).astype(f)
    for h in (0, 64):
        for d in range(8):
            rot1[h + d + 8, h + d], rot1[h + d, h + d + 8] = -1, 1
            freq[h + d] = freq[h + d + 8] = inv[d]
        for b in (0, 32):
            for d in range(16):
                rot2[h + b + d + 16, h + b + d], rot2[h + b + d, h + b + d + 16] = -1, 1
    before = np.triu(np.ones((P, P)), 1).astype(f)
    off = np.arange(-(T - 1) - P, T + P)
    count = sum(((off % dil == 0) & (abs(off) <= window // 2)).astype(int)
                for window, dil in ((128, 1), (512, 4), (2048, 16)))
    logc = np.where(count > 0, np.log(np.maximum(count, 1)), NEG).astype(f)
    y = np.arange(1920)[None, :] - 896 - np.arange(P)[:, None]
    dilated = logc[y + (T - 1) + P]
    t = np.arange(T)
    inv2 = (np.float32(10000.0) ** (-np.arange(16, dtype=f) / np.float32(16))).astype(f)
    ang_r, ang_c = (t // 64).astype(f)[:, None] * inv2, (t % 64).astype(f)[:, None] * inv2
    cos2 = np.tile(np.concatenate([np.cos(ang_r)] * 2 + [np.cos(ang_c)] * 2, axis=1).T, (2, 1)).astype(f)
    sin2 = np.tile(np.concatenate([np.sin(ang_r)] * 2 + [np.sin(ang_c)] * 2, axis=1).T, (2, 1)).astype(f)
    p = np.arange(P)
    near = np.zeros((P, 8, 10, 64), f)
    for q in range(8):
        r, base = 2 * q + p // 64, min(max(2 * q - 4, 0), 6)
        r0 = np.clip(r - 4, 0, 8)
        c0 = np.clip(p % 64 - 8, 0, 48)
        kr, kc = base + np.arange(10), np.arange(64)
        rows = (kr[None] >= r0[:, None]) & (kr[None] < r0[:, None] + 8)
        colm = (kc[None] >= c0[:, None]) & (kc[None] < c0[:, None] + 16)
        near[:, q] = np.where(rows[:, :, None] & colm[:, None, :], 0, NEG)
    small = {"ones": np.ones((P, P), f), "ident": ident, "blk64": blk64, "rot1": rot1, "rot2": rot2,
             "before": before, "freq": freq, "eps": np.full((P, 1), EPS, f), "one": np.ones((P, 1), f),
             "heads32": np.kron(np.eye(4), np.ones((32, 1))).astype(f),
             "index": np.tile(np.arange(E_, dtype=f) - 1024, (P, 1)),
             "block": np.tile(np.arange(NB, dtype=f), (P, 1))}
    return small, {"dilated": dilated, "cos2": cos2, "sin2": sin2, "near": near.reshape(P, 8 * 640)}


def program(nc, din, out, upto=99):
    small, tables = constants()
    with ExitStack() as ctx:
        def sb(name, shape, dt=F32):
            return ctx.enter_context(nc.sbuf_tensor(name, shape, dt))

        width = sum(a.shape[1] for a in small.values())
        pack = sb("pack", [P, width])
        cst, o = {}, 0
        for name, a in small.items():
            cst[name] = pack[:, o:o + a.shape[1]]
            o += a.shape[1]
        vec = sb("vec", [P, din["vec"].shape[1]])
        vecs, o = {}, 0
        for name, n in VECS:
            vecs[name] = vec[:, o:o + n]
            o += n
        h = sb("h", [P, KD, T])
        load_all(nc, "load", [(pack[:], din["pack"]), (vec[:], din["vec"]), (h[:], din["x"])])
        y_dram = nc.dram_tensor("y_dram", (NB * P, T), F32).ap()
        y_filled = nc.alloc_semaphore("y_filled")
        first_block(nc, din, cst, vecs, h, y_dram, y_filled, upto)
        if upto > 20:
            second_block(nc, din, cst, vecs, h, y_dram, y_filled, upto)
        store_all(nc, "store", [(out, h[:])])


def first_block(nc, din, cst, vecs, h, y_dram, y_filled, upto):
    with ExitStack() as ctx:
        def sb(name, shape, dt=F32):
            return ctx.enter_context(nc.sbuf_tensor(name, shape, dt))

        proj = sb("proj", [P, 14, T])
        km = sb("km", [P, 2, NMEM])
        v = sb("v", [P, T // P, 512])
        vm = sb("vm", [P, NMEM // P, NMEM])
        with nc.sbuf_tensor("n", [P, KD, T], F32) as n:
            rms_norm(nc, "n1", cst, h, n, vecs["mix_g"])
            project(nc, "pin", din["w_in"], cols(n), T, 14, dst=proj)
            project_rows(nc, "pv", din["w_v"], cols(n), T, v)
            mem = n[:, 0:2, :].rearrange("p a (b c) -> p (a b) c", c=NMEM)
            load_all(nc, "lm", [(mem, din["mem"])])
            rms_norm(nc, "nm", cst, mem, mem, vecs["mem_g"])
            project(nc, "pkm", din["w_km"], cols(mem), NMEM, 2, dst=km)
            project_rows(nc, "pvm", din["w_vm"], cols(mem), NMEM, vm)
        if upto == 1:
            return
        with nc.sbuf_tensor("cos", [P, T], F32) as cos, nc.sbuf_tensor("sin", [P, T], F32) as sin:
            rope_tables(nc, "rt", cst, din["positions"], cos[:], sin[:])
            rope = (cst["rot1"], cos[:], sin[:])
            head_prep(nc, "hq", cst, proj[:, 0:8, :], T, 8, vecs["qk_g"], rope)
            head_prep(nc, "hm", cst, proj[:, 12:14, :], T, 2, vecs["mq_g"])
            head_prep(nc, "hkm", cst, km, NMEM, 2, vecs["mk_g"])
        conv_mixer(nc, "cv", cst, proj[:, 8:10, :], proj[:, 10:12, :],
                   vecs["cv_w"].rearrange("p (c k) -> p c k", c=2), vecs["cv_b"], vecs["ln_g"], vecs["ln_b"])
        if upto == 2:
            return
        with nc.Block() as block:
            @block.sync
            def _(sp):
                for b in range(NB):
                    sp.dma_start(y_dram[b * P:(b + 1) * P, :], din["cos2"]).then_inc(y_filled, 16)
        with nc.sbuf_tensor("dil", [P, 1920], F32) as dil:
            load_all(nc, "ld", [(dil[:], din["dilated"])])
            attention(nc, "a1", cst, 4, proj[:, 0:4, :], [(proj[:, 4:8, :], T)], v, T // P,
                      bias=lambda m, u, t: [dil[:, 896 - P * t:896 - P * t + T]])
        attention(nc, "am", cst, 2, proj[:, 12:14, :], [(km, NMEM)], vm, NMEM // P)
        if upto == 3:
            return
        mixed = cols(proj[:, 0:4, :]) + cols(proj[:, 8:10, :]) + cols(proj[:, 12:14, :])
        project(nc, "po", din["w_out"], mixed, T, KD, add_to=h)
    if upto == 4:
        return
    with ExitStack() as ctx:
        hidden = ctx.enter_context(nc.sbuf_tensor("hidden", [P, KF, T], F32))
        with nc.sbuf_tensor("nf", [P, KD, T], F32) as n:
            rms_norm(nc, "nf", cst, h, n, vecs["ffn_g"])
            ffn_up(nc, "fu", din["w_up"], cols(n), hidden)
        project(nc, "fd", din["w_down"], cols(hidden), T, KD, add_to=h)


VECS = [("mix_g", KD), ("mem_g", KD), ("ffn_g", KD), ("qk_g", 8), ("mq_g", 2), ("mk_g", 2),
        ("cv_w", 62), ("cv_b", 2), ("ln_g", 2), ("ln_b", 2),
        ("c", 2 * KD), ("g1", KD), ("g2", KD), ("final_g", KD), ("b_mod", 6 * KD), ("lam", 4), ("sub_g", 4),
        ("gla_g", 2), ("b_dec", 2), ("b_route", 1)]


def lay_out(x):
    def col(a):
        return a.reshape(-1, P).T

    def wtiles(w):
        K, M = w.shape[0] // P, w.shape[1] // P
        return w.reshape(K, P, M, P).transpose(2, 1, 0, 3).reshape(M, P, K * P)

    def wrows(w):
        return w.reshape(-1, P, w.shape[1]).transpose(1, 0, 2)

    small, tables = constants()
    w_in = x["w_in"][0]
    v = {"mix_g": col(x["mix_norm_g"][0]), "mem_g": col(x["mem_norm_g"][0]), "ffn_g": col(x["ffn_norm_g"][0]),
         "qk_g": np.stack([np.tile(x[g][0], 2) for g in ("q_norm_g", "k_norm_g") for _ in range(4)], axis=1),
         "mq_g": np.stack([np.tile(x["mq_norm_g"][0], 2)] * 2, axis=1),
         "mk_g": np.stack([np.tile(x["mk_norm_g"][0], 2)] * 2, axis=1),
         "cv_w": x["conv_dw_w"][0].T.reshape(2, P, 31).transpose(1, 0, 2).reshape(P, 62),
         "cv_b": col(x["conv_dw_b"][0]), "ln_g": col(x["conv_ln_g"][0]), "ln_b": col(x["conv_ln_b"][0])}
    d = {"pack": np.concatenate(list(small.values()), axis=1), "dilated": tables["dilated"],
         "x": x["x"][0].T.reshape(KD, P, T).transpose(1, 0, 2),
         "mem": x["mem"][0].T.reshape(KD, P, NMEM).transpose(1, 0, 2),
         "positions": x["positions"][0],
         "w_in": wtiles(np.concatenate([w_in[:, 0:1024], w_in[:, 1536:2304]], axis=1)),
         "w_v": wrows(w_in[:, 1024:1536]),
         "w_km": wtiles(x["w_mem_kv"][0][:, 0:256]), "w_vm": wrows(x["w_mem_kv"][0][:, 256:512]),
         "w_out": wtiles(x["w_out"][0]), "w_down": wtiles(x["w_down"][0])}
    up = x["w_up"][0].reshape(KD, P, 2, KF, P).transpose(3, 1, 0, 2, 4).reshape(KF, P, KD * 2 * P)
    taps = np.concatenate([x["ffn_dw_w"][0], x["ffn_dw_b"]], axis=0).reshape(4, 2, KF, P).transpose(2, 3, 1, 0)
    d["w_up"] = np.concatenate([up, taps.reshape(KF, P, 8)], axis=2)
    more(x, d, v, tables, col, wtiles, wrows)
    d["vec"] = np.concatenate([v[name] for name, _ in VECS], axis=1)
    return {k: np.ascontiguousarray(a) for k, a in d.items()}


def more(x, d, v, tables, col, wtiles, wrows):
    w = x["w_in_2"][0]
    at_ = dict(zip(("qa", "ka", "va", "qb", "kb", "vb", "rb", "gb", "qn", "kn", "vn"),
                   np.split(w, np.cumsum((512, 512, 512, 128, 128, 256, 256, 32, 256, 256)), axis=1)))
    pad = np.zeros((D, 96), w.dtype)
    d["w_in2"] = wtiles(np.concatenate([at_["ka"], at_["kn"], at_["kb"], at_["gb"], pad, at_["qa"], at_["qn"],
                                        at_["qb"], at_["vb"], at_["rb"]], axis=1))
    d["w_v2"] = wrows(np.concatenate([at_["va"], at_["vn"], at_["vb"]], axis=1))
    d["w_mod"] = wtiles(x["w_mod_2"][0])
    d["w_out2"] = wtiles(x["w_out_2"][0])
    d["ctx"] = x["ctx_2"][0].T.reshape(KD, P, NCTX).transpose(1, 0, 2)
    dec = np.zeros((32, 2, P), w.dtype)
    for i in range(2):
        dec[16 * i:16 * i + 16, i] = x["gla_w_decay_2"][0, i]
    d["w_dec"] = dec
    d["cos2"], d["sin2"], d["near"] = tables["cos2"], tables["sin2"], tables["near"].reshape(P, TT, 640)
    p = np.arange(P)
    dr = np.clip(np.arange(18)[None, :] - p[:, None] // 64 - 1, 0, 14)
    dc = np.clip(np.arange(64)[None, :] - p[:, None] % 64 + 15, 0, 30)
    d["rpb"] = x["na_rel_bias_2"][0][:, dr[:, :, None], dc[:, None, :]].transpose(1, 0, 2, 3).reshape(P, 4, 18 * 64)
    d["w_route"] = wrows(np.concatenate([x["w_router_group_2"][0], x["w_router_expert_2"][0]], axis=1))
    d["w_eup"], d["w_edown"] = x["w_expert_up_2"][0], x["w_expert_down_2"][0]
    rest = np.zeros((P - 36,), w.dtype)
    lam = np.zeros((P, 4), w.dtype)
    lam[0:64] = x["diff_lambda_2"][0].T
    v.update({"c": np.concatenate([col(x["c_2"][0]), col(x["c_ctx_2"])], axis=1), "g1": col(x["norm1_g_2"][0]),
              "g2": col(x["norm2_g_2"][0]), "final_g": col(x["final_g_2"]), "b_mod": col(x["b_mod_2"][0]), "lam": lam,
              "sub_g": np.stack([x["diff_sub_g_2"][0]] * 4, axis=1),
              "gla_g": np.stack([np.tile(x["gla_norm_g_2"][0], 2)] * 2, axis=1),
              "b_dec": x["gla_b_decay_2"][0].T,
              "b_route": np.concatenate([x["b_router_group_2"][0], x["b_router_expert_2"][0], rest])[:, None]})


def kernel(**inputs):
    import concourse.bacc as bacc
    from concourse.bass_utils import run_bass_kernel_spmd

    nc = bacc.Bacc("TRN2", target_bir_lowering=False, num_devices=1)
    arrays = lay_out({k: np.asarray(a) for k, a in inputs.items()})
    din = {k: nc.dram_tensor(f"in_{k}", a.shape, mybir.dt.from_np(a.dtype), kind="ExternalInput").ap()
           for k, a in arrays.items()}
    out = nc.dram_tensor("out", (P, KD, T), F32, kind="ExternalOutput").ap()
    program(nc, din, out)
    r = run_bass_kernel_spmd(nc, [{f"in_{k}": a for k, a in arrays.items()}], core_ids=[0])
    y = r.results[0]["out"]
    return y.transpose(1, 0, 2).reshape(D, T).T[None]
```

```python
from contextlib import ExitStack

import numpy as np

import concourse.bass as bass
from concourse import mybir

F32 = mybir.dt.float32
I32 = mybir.dt.int32
U32 = mybir.dt.uint32
ACT = mybir.ActivationFunctionType
ALU = mybir.AluOpType
AX = mybir.AxisListType

P = 128
T = 1024
D = 1024
KD = D // P
NMEM = 256
NCTX = 256
FF = 2816
KF = FF // P
BANK = 512
EPS = 1e-6
NEG = -1e30
SCALE = 64.0 ** -0.5


class Phase:

    def __init__(self, nc, tag):
        self.nc, self.tag, self.ctx, self.sems = nc, tag, ExitStack(), []

    def __enter__(self):
        return self

    def __exit__(self, *e):
        self.nc.clear_and_free_semaphores(self.sems)
        self.nc.all_engine_barrier(sem_only=True)
        return self.ctx.__exit__(*e)

    def sb(self, name, shape, dt=F32):
        return self.ctx.enter_context(self.nc.sbuf_tensor(f"{self.tag}_{name}", shape, dt))

    def ps(self, name, shape, dt=F32):
        return self.ctx.enter_context(self.nc.psum_tensor(f"{self.tag}_{name}", shape, dt))

    def sem(self, name):
        self.sems.append(self.nc.alloc_semaphore(f"{self.tag}_{name}"))
        return self.sems[-1]


class Steps:

    def __init__(self, eng, sem):
        self.eng, self.sem, self.n, self.i, self.k = eng, sem, 0, None, 0

    def enter(self, i, per):
        self.i, self.per, self.k = i, per, 0

    def leave(self, trips):
        assert self.k == self.per, (self.k, self.per)
        self.n, self.i = self.n + trips * self.per, None

    def done(self, ins):
        ins.then_inc(self.sem, 1)
        if self.i is None:
            self.n += 1
            self.eng.wait_ge(self.sem, self.n)
        else:
            self.k += 1
            self.eng.wait_ge(self.sem, self.i * self.per + (self.n + self.k))


def chunks(n, size=BANK):
    return [(a, min(size, n - a)) for a in range(0, n, size)]


def at(ap, i):
    return ap[:, bass.ds(i, 1), :].rearrange("p a n -> p (a n)")


def cols(ap):
    return [ap[:, k, :] for k in range(ap.shape[1])]


class Weights:

    def __init__(self, nc, sb, tag, w_dram, K, count, first=0):
        self.dram, self.K, self.count, self.first = w_dram, K, count, first
        self.R = 4 if K <= KD else 2
        self.w = sb(f"{tag}_w", [P, self.R, K, P])
        self.ready = [nc.alloc_semaphore(f"{tag}_w_ready{u}") for u in range(self.R)]

    def load(self, sp, i, u):
        sp.dma_start(self.w[:, u], self.dram[bass.ds(i * self.R + (u + self.first), 1)].rearrange(
            "a p (k n) -> p (a k) n", k=self.K)).then_inc(self.ready[u], 16)

    def start(self, sp):
        for u in range(min(self.R, self.count)):
            self.load(sp, 0, u)


def load_all(nc, tag, pairs, ahead=None):
    with Phase(nc, tag) as ph:
        loaded = ph.sem("loaded")
        with nc.Block() as block:
            @block.sync
            def _(sp):
                for dst, src in pairs:
                    sp.dma_start(dst, src).then_inc(loaded, 16)
                if ahead:
                    ahead.start(sp)
                sp.wait_ge(loaded, 16 * len(pairs))


def store_all(nc, tag, pairs):
    load_all(nc, tag, pairs)


def rms_norm(nc, tag, cst, x, out, gain, shift=None, width=D, ahead=None):
    K, n = x.shape[1], x.shape[2]
    parts = chunks(n)
    with Phase(nc, tag) as ph:
        sq = ph.sb("sq", [P, 2, BANK])
        sd = ph.sb("sd", [P, 2, BANK])
        ms = ph.ps("ms", [P, 2, BANK])
        sq_ready, summed, sd_ready = ph.sem("sq_ready"), ph.sem("summed"), ph.sem("sd_ready")
        step = ph.sem("step")
        with nc.Block() as block:
            if ahead:
                @block.sync
                def _(sp):
                    ahead.start(sp)

            @block.scalar
            def _(act):
                def root(h):
                    a, w = parts[h]
                    act.wait_ge(summed, K * (h + 1))
                    nc.scalar.activation(sd[:, h % 2, 0:w], ms[:, h % 2, 0:w], ACT.Sqrt, bias=cst["eps"],
                                         scale=1.0 / width).then_inc(sd_ready, 1)
                for h, (a, w) in enumerate(parts):
                    for k in range(K):
                        j = h * K + k
                        if j >= 2:
                            act.wait_ge(summed, j - 1)
                        nc.scalar.activation(sq[:, j % 2, 0:w], x[:, k, a:a + w], ACT.Square).then_inc(sq_ready, 1)
                    root(h)

            @block.tensor
            def _(pe):
                for h, (a, w) in enumerate(parts):
                    if h >= 2:
                        pe.wait_ge(sd_ready, h - 1)
                    for k in range(K):
                        j = h * K + k
                        pe.wait_ge(sq_ready, j + 1)
                        nc.tensor.matmul(ms[:, h % 2, 0:w], cst["ones"], sq[:, j % 2, 0:w], start=(k == 0),
                                         stop=(k == K - 1)).then_inc(summed, 1)

            @block.vector
            def _(dve):
                st = Steps(dve, step)
                for h, (a, w) in enumerate(parts):
                    dve.wait_ge(sd_ready, h + 1)
                    st.done(nc.vector.reciprocal(sd[:, h % 2, 0:w], sd[:, h % 2, 0:w]))
                    for k in range(K):
                        last = nc.vector.scalar_tensor_tensor(out=out[:, k, a:a + w], in0=x[:, k, a:a + w],
                                                              scalar=gain[:, k:k + 1], in1=sd[:, h % 2, 0:w],
                                                              op0=ALU.mult, op1=ALU.mult)
                    if shift is not None:
                        st.done(last)
                        for k in range(K):
                            nc.vector.tensor_scalar(out[:, k, a:a + w], out[:, k, a:a + w], shift[:, k:k + 1],
                                                    None, ALU.add)


def project(nc, tag, w_dram, src, n, count, dst=None, add_to=None, gate=None, first=0, beside=None, thin=None,
            weights=None, ahead=None):
    K = len(src)
    parts = chunks(n)
    wide = len(parts) * BANK
    with Phase(nc, tag) as ph:
        own = weights or Weights(nc, lambda name, shape: ph.ctx.enter_context(nc.sbuf_tensor(name, shape, F32)),
                                 tag, w_dram, K, count, first)
        w, w_ready, R = own.w, own.ready, own.R
        ph.sems += w_ready
        acc = ph.ps("acc", [P, 2, wide])
        mm_done, acc_free = ph.sem("mm_done"), ph.sem("acc_free")
        if thin:
            thin_dram, rows, thin_dst = thin
            G, nt, F = thin_dst.shape[1] // count, rows.shape[1], rows.shape[2]
            assert add_to is not None and count % R == 0 and G * count == thin_dst.shape[1]
            thin_w = ph.sb("thin_w", [P, G, F])
            prod = ph.sb("prod", [P, 2, nt, F])
            thin_ready, multiplied, summed = ph.sem("thin_ready"), ph.sem("multiplied"), ph.sem("summed")
        rounds, tail = count // R, count % R

        def sweep(eng, body):
            if rounds:
                with eng.Fori(0, rounds) as i:
                    for u in range(R):
                        body(i, u)
            for u in range(tail):
                body(rounds, u)

        with nc.Block() as block:
            @block.sync
            def _(sp):
                def load(i, u):
                    sp.wait_ge(mm_done, i * R + (u + 1))
                    own.load(sp, i, u)
                    load_thin(i, u)

                def load_thin(i, u):
                    if thin:
                        sp.wait_ge(multiplied, i * (R * G) + (u * G + G))
                        sp.dma_start(thin_w[:], thin_dram[bass.ds(i * (R * G) + u * G, G)].rearrange(
                            "g p n -> p g n")).then_inc(thin_ready, 16)

                if weights is None:
                    own.start(sp)
                for u in range(min(R, count)):
                    load_thin(0, u)
                if rounds > 1:
                    with sp.Fori(1, rounds) as i:
                        for u in range(R):
                            load(i, u)
                if rounds:
                    for u in range(tail):
                        load(rounds, u)
                if ahead:
                    ahead.start(sp)

            @block.tensor
            def _(pe):
                pe.sem_inc(mm_done, R)

                def tile(i, u):
                    pe.wait_ge(w_ready[u], i * 16 + 16)
                    pe.wait_ge(acc_free, i * R + (u + 1))
                    for a, width in parts:
                        for k in range(K):
                            mm = nc.tensor.matmul(acc[:, u % 2, a:a + width], w[:, u, k, :], src[k][:, a:a + width],
                                                  start=(k == 0), stop=(k == K - 1))
                    mm.then_inc(mm_done, 1)
                sweep(pe, tile)

            if thin:
                @block.scalar
                def _(act):
                    act.sem_inc(summed, 2)

                    def sum_up(i, u):
                        for g in range(G):
                            act.wait_ge(multiplied, i * (R * G) + (u * G + g + 1 + G))
                            for a in range(nt):
                                last = nc.scalar.activation(prod[:, g % 2, a, :], prod[:, g % 2, a, :], ACT.Copy,
                                                            accum_out=thin_dst[:, bass.ds(i * (R * G) + (u * G + g), 1),
                                                                               a])
                            last.then_inc(summed, 1)
                    sweep(act, sum_up)

            if beside:
                @block.vector
                def _(dve):
                    beside[1](dve)

            if dst is not None:
                @block.scalar
                def _(act):
                    act.sem_inc(acc_free, 2)
                    if beside:
                        beside[0](act)

                    def keep(i, u):
                        act.wait_ge(mm_done, i * R + (u + 1 + R))
                        nc.scalar.activation(at(dst, i * R + u), acc[:, u % 2, 0:n], ACT.Copy).then_inc(acc_free, 1)
                    sweep(act, keep)
            else:
                @block.vector
                def _(dve):
                    dve.sem_inc(acc_free, 2)

                    def add(i, u):
                        dve.wait_ge(mm_done, i * R + (u + 1 + R))
                        o = at(add_to, i * R + u)
                        if gate is None:
                            nc.vector.tensor_tensor(o, acc[:, u % 2, 0:n], o, ALU.add).then_inc(acc_free, 1)
                        else:
                            nc.vector.scalar_tensor_tensor(out=o, in0=acc[:, u % 2, 0:n],
                                                           scalar=gate[:, bass.ds(i * R + u, 1)], in1=o,
                                                           op0=ALU.mult, op1=ALU.add).then_inc(acc_free, 1)
                        if thin:
                            dve.wait_ge(thin_ready, (i * R + u) * 16 + 16)
                            for g in range(G):
                                dve.wait_ge(summed, i * (R * G) + (u * G + g + 1))
                                nc.vector.tensor_tensor(prod[:, g % 2], rows, thin_w[:, g, :].unsqueeze(1).broadcast_to(
                                    [P, nt, F]), ALU.mult).then_inc(multiplied, 1)
                    if thin:
                        dve.sem_inc(multiplied, G)
                    sweep(dve, add)


def project_rows(nc, tag, w_dram, src, n, dst):
    K, cols = w_dram.shape[1], w_dram.shape[2]
    cc = chunks(cols)
    tiles = n // P
    with Phase(nc, tag) as ph:
        S = min(2, len(cc))
        w = ph.sb("w", [P, S, K, BANK])
        acc = ph.ps("acc", [P, 2, BANK])
        w_ready = [[ph.sem(f"w_ready{x}_{k}") for k in range(K)] for x in range(S)]
        mm_done, acc_free = ph.sem("mm_done"), ph.sem("acc_free")
        with nc.Block() as block:
            @block.sync
            def _(sp):
                for c, (a, width) in enumerate(cc):
                    if c >= S:
                        sp.wait_ge(mm_done, (c - S + 1) * tiles)
                    for k in range(K):
                        sp.dma_start(w[:, c % S, k, 0:width], w_dram[:, k, a:a + width]).then_inc(w_ready[c % S][k], 16)

            @block.tensor
            def _(pe):
                for c, (a, width) in enumerate(cc):
                    for t in range(tiles):
                        j = c * tiles + t
                        if j >= 2:
                            pe.wait_ge(acc_free, j - 1)
                        for k in range(K):
                            if t == 0:
                                pe.wait_ge(w_ready[c % S][k], 16 * (c // S + 1))
                            mm = nc.tensor.matmul(acc[:, j % 2, 0:width], src[k][:, t * P:(t + 1) * P],
                                                  w[:, c % S, k, 0:width], start=(k == 0), stop=(k == K - 1))
                        mm.then_inc(mm_done, 1)

            @block.scalar
            def _(act):
                for c, (a, width) in enumerate(cc):
                    for t in range(tiles):
                        j = c * tiles + t
                        act.wait_ge(mm_done, j + 1)
                        nc.scalar.activation(dst[:, t, a:a + width], acc[:, j % 2, 0:width],
                                             ACT.Copy).then_inc(acc_free, 1)


def head_norm(nc, tag, cst, x, n, gain, rope=None, turned_tiles=0, blk=64):
    tiles = x.shape[1]
    parts = chunks(n)
    wide = len(parts) * BANK
    per = P // blk
    rows = tiles * per
    window, most = cst[f"window{blk}"], (cst[f"window{blk}"].shape[1] - per) // 2
    with Phase(nc, tag) as ph:
        sq = ph.sb("sq", [P, 2, n])
        r = ph.sb("r", [rows, n])
        heads = ph.sb("heads", [rows, rows, blk])
        turn = ph.sb("turn", [P, n])
        sum_ps, spread_ps, rot_ps = ph.ps("sum", [P, wide]), ph.ps("spread", [P, 2, wide]), ph.ps("rot", [P, wide])
        squared, summed, rooted, inverted, spread, normed = (ph.sem(s) for s in (
            "squared", "summed", "rooted", "inverted", "spread", "normed"))
        rotated, rot_used, step, heads_ready = (ph.sem(s) for s in ("rotated", "rot_used", "step", "heads_ready"))
        with nc.Block() as block:
            @block.scalar
            def _(act):
                for i in range(tiles):
                    if i >= 2:
                        act.wait_ge(summed, i - 1)
                    nc.scalar.activation(sq[:, i % 2, :], x[:, i, :], ACT.Square).then_inc(squared, 1)
                act.wait_ge(summed, tiles)
                nc.scalar.activation(r[:], sum_ps[0:rows, 0:n], ACT.Sqrt, bias=cst["eps"][0:rows],
                                     scale=1.0 / blk).then_inc(rooted, 1)

            @block.tensor
            def _(pe):
                for i in range(tiles):
                    pe.wait_ge(squared, i + 1)
                    for a, w in parts:
                        mm = nc.tensor.matmul(sum_ps[0:rows, a:a + w], window[:, most - per * i:most - per * i + rows],
                                              sq[:, i % 2, a:a + w], start=(i == 0), stop=(i == tiles - 1))
                    mm.then_inc(summed, 1)

                def spread_out(i):
                    if i >= 2:
                        pe.wait_ge(normed, i - 1)
                    mine = heads[:, per * i:per * (i + 1), :].rearrange("p a b -> p (a b)")
                    for a, w in parts:
                        mm = nc.tensor.matmul(spread_ps[:, i % 2, a:a + w], mine, r[:, a:a + w], start=True, stop=True)
                    mm.then_inc(spread, 1)

                def rotate(i):
                    pe.wait_ge(normed, i + 1)
                    if i:
                        pe.wait_ge(rot_used, i)
                    for a, w in parts:
                        mm = nc.tensor.matmul(rot_ps[:, a:a + w], rope[0], x[:, i, a:a + w], start=True, stop=True)
                    mm.then_inc(rotated, 1)

                pe.wait_ge(heads_ready, 1)
                pe.wait_ge(inverted, 1)
                for i in range(tiles + 1):
                    if i < tiles:
                        spread_out(i)
                    if 1 <= i <= turned_tiles:
                        rotate(i - 1)

            @block.vector
            def _(dve):
                st = Steps(dve, step)
                nc.vector.tensor_copy(heads[:], cst["ident"][0:rows, 0:rows].unsqueeze(2).broadcast_to(
                    [rows, rows, blk])).then_inc(heads_ready, 1)
                dve.wait_ge(rooted, 1)
                nc.vector.reciprocal(r[:], r[:]).then_inc(inverted, 1)
                for i in range(tiles + 1):
                    if i < tiles:
                        dve.wait_ge(spread, i + 1)
                        nc.vector.scalar_tensor_tensor(out=x[:, i, :], in0=spread_ps[:, i % 2, 0:n],
                                                       scalar=gain[:, i:i + 1], in1=x[:, i, :], op0=ALU.mult,
                                                       op1=ALU.mult).then_inc(normed, 1)
                    if 1 <= i <= turned_tiles:
                        xi = x[:, i - 1, :]
                        dve.wait_ge(rotated, i)
                        st.done(nc.vector.tensor_tensor(turn[:], rot_ps[:, 0:n], rope[2], ALU.mult))
                        dve.sem_inc(rot_used, 1)
                        dve.wait_ge(normed, i)
                        st.done(nc.vector.tensor_tensor(xi, xi, rope[1], ALU.mult))
                        st.done(nc.vector.tensor_tensor(xi, xi, turn[:], ALU.add))


def rotary(nc, tag, x, rope):
    tiles, n = x.shape[1], x.shape[2]
    parts = chunks(n)
    wide = len(parts) * BANK
    with Phase(nc, tag) as ph:
        turn = ph.sb("turn", [P, n])
        rot_ps = ph.ps("rot", [P, 2, wide])
        turned, rot_used, step = ph.sem("turned"), ph.sem("rot_used"), ph.sem("step")
        with nc.Block() as block:
            @block.tensor
            def _(pe):
                with pe.Fori(0, tiles // 2) as i:
                    for u in range(2):
                        pe.wait_ge(rot_used, i * 2 + (u + 1))
                        for a, w in parts:
                            mm = nc.tensor.matmul(rot_ps[:, u, a:a + w], rope[0], at(x, i * 2 + u)[:, a:a + w],
                                                  start=True, stop=True)
                        mm.then_inc(turned, 1)

            @block.vector
            def _(dve):
                st = Steps(dve, step)
                dve.sem_inc(rot_used, 2)
                with dve.Fori(0, tiles // 2) as i:
                    st.enter(i, 6)
                    for u in range(2):
                        xi = at(x, i * 2 + u)
                        dve.wait_ge(turned, i * 2 + (u + 1))
                        st.done(nc.vector.tensor_tensor(turn[:], rot_ps[:, u, 0:n], rope[2], ALU.mult))
                        dve.sem_inc(rot_used, 1)
                        st.done(nc.vector.tensor_tensor(xi, xi, rope[1], ALU.mult))
                        st.done(nc.vector.tensor_tensor(xi, xi, turn[:], ALU.add))
                st.leave(tiles // 2)


def attention(nc, tag, cst, pairs, q, keys, v, KT, bias=None, diff=None, window=None, scratch=None, ahead=None):
    out = q
    tiles = T // P
    nk = sum(n for _, n in keys)
    seen = KT if window is None else len(window[0])
    NS = seen * P
    ng = -(-seen // 4)
    wide = -(-NS // BANK) * BANK
    PTS = 1 if wide > 2 * BANK else 2
    if window is not None:
        units = [(t, u) for t in range(tiles) for u in range(2)]
    elif diff is not None:
        units = [(t, u) for t in range(tiles) for u in range(2)]
    else:
        units = [(c * 4 + t, u) for c in range(2) for u in range(2) for t in range(4)]
    U = len(units)
    merged = 2 if diff is not None else 1
    M = U // merged
    share = 1 if window is not None else 4
    J = M // share
    G = M * ng
    LAG = 1 if diff is not None else 2
    NP = (LAG + 2) * merged
    early, late = (range(0, 1), range(1, ng)) if diff is not None else (range(0, ng), range(0, 0))
    PT = 1 if scratch is not None else 2
    with Phase(nc, tag) as ph:
        spare = scratch[:].rearrange("p a b -> p (a b)") if scratch is not None else None
        if spare is not None and NP * NS + T + nk <= spare.shape[1]:
            qs, ks = spare[:, NP * NS:NP * NS + T], spare[:, NP * NS + T:NP * NS + T + nk]
        else:
            qs, ks = ph.sb("qs", [P, T]), ph.sb("ks", [P, nk])
        if spare is None:
            prob = ph.sb("prob", [P, NP, NS])
        else:
            prob = spare[:, 0:NP * NS].rearrange("p (a b) -> p a b", a=NP)
        vs = ph.sb("vs", [P, KT, P])
        probT = ph.sb("probT", [P, PT, seen, share * P])
        negm = ph.sb("negm", [P, NP])
        den = ph.sb("den", [P, NP])
        s_ps = ph.ps("s_ps", [P, 2, wide])
        t_ps = ph.ps("t_ps", [P, PTS, 4, P])
        o_ps = ph.ps("o_ps", [P, PTS, BANK])
        rd_ready, scaled = ph.sem("rd_ready"), ph.sem("scaled")
        v_staged, staged, s_ready, s_free = (ph.sem(s) for s in ("v_staged", "staged", "s_ready", "s_free"))
        max_ready, p_ready, d_ready = (ph.sem(s) for s in ("max_ready", "p_ready", "d_ready"))
        t_ready, t_free, o_ready, o_free, step = (ph.sem(s) for s in ("t_ready", "t_free", "o_ready", "o_free", "step"))
        NST = 1 + len(keys)
        with nc.Block() as block:
            if ahead:
                @block.sync
                def _(sp):
                    ahead.start(sp)

            @block.gpsimd
            def _(pool):
                with pool.Fori(0, pairs) as m:
                    pool.wait_ge(o_ready, m * J + 2)
                    nc.gpsimd.tensor_copy(vs[:], v[:, :, bass.ds(m * P, P)]).then_inc(v_staged, 1)

            @block.tensor
            def _(pe):
                pe.sem_inc(o_ready, 2)
                pe.sem_inc(t_ready, (LAG + 2) * ng)
                with pe.Fori(0, pairs) as m:
                    pe.wait_ge(staged, m * NST + NST)

                    def scores(n):
                        t, u = units[n]
                        pe.wait_ge(s_free, m * U + (n + 1))
                        r = slice(64 * u, 64 * u + 64)
                        if window is None:
                            runs = [(a, a, w) for a, w in chunks(nk)]
                        else:
                            k0, nw = window[t][0] * P, (seen - 2) * P
                            runs = [(a, k0 + a, w) for a, w in chunks(nw)]
                            runs += [(a, nk - NCTX + a - nw, min(w, BANK - a % BANK)) for a, w in [(nw, NCTX)]]
                        for o, a, w in runs:
                            mm = nc.tensor.matmul(s_ps[:, n % 2, o:o + w], qs[r, t * P:(t + 1) * P], ks[r, a:a + w],
                                                  start=True, stop=True)
                        mm.then_inc(s_ready, 1)

                    def turn(k, groups):
                        if 0 in groups:
                            pe.wait_ge(d_ready, m * M + (k + 1))
                        p = prob[:, (k % (LAG + 2)) * merged, :]
                        for g in groups:
                            j = k * ng + g
                            pe.wait_ge(t_free, m * G + (j + 1))
                            for x in range(4 * g, min(4 * g + 4, seen)):
                                mm = nc.tensor.transpose(t_ps[:, j % PTS, x - 4 * g, :], p[:, x * P:(x + 1) * P],
                                                         cst["ident"])
                            mm.then_inc(t_ready, 1)

                    def values(j):
                        if j == 0:
                            pe.wait_ge(v_staged, m + 1)
                        pe.wait_ge(t_free, m * G + (PTS + (j + 1) * share * ng))
                        pe.wait_ge(o_free, m * J + (j + 1))
                        t = units[j * share * merged][0]
                        for x in range(seen):
                            kt = x if window is None else window[t][x]
                            mm = nc.tensor.matmul(o_ps[:, j % PTS, 0:share * P], vs[:, kt, :],
                                                  probT[:, j % PT, x, :], start=(x == 0), stop=(x == seen - 1))
                        mm.then_inc(o_ready, 1)

                    for n in range(merged):
                        scores(n)
                    for k in range(M + LAG):
                        new = range((k + 1) * merged, min((k + 2) * merged, U))
                        full = k > LAG and (k - LAG) % share == 0
                        for n in new[:1]:
                            scores(n)
                        if full and PT == 1:
                            values((k - LAG) // share - 1)
                        if k >= LAG:
                            turn(k - LAG, early)
                        for n in new[1:]:
                            scores(n)
                        if k >= LAG and late:
                            turn(k - LAG, late)
                        if full and PT == 2:
                            values((k - LAG) // share - 1)
                    values(J - 1)

            @block.scalar
            def _(act):
                act.sem_inc(t_free, PTS)
                act.sem_inc(p_ready, NP)
                if bias is None:
                    act.sem_inc(s_free, 2)
                with act.Fori(0, pairs) as m:
                    act.wait_ge(o_ready, m * J + 2)
                    nc.scalar.activation(qs[:, 0:T], at(q, m), ACT.Copy).then_inc(staged, 1)
                    if len(keys) > 1:
                        nc.scalar.activation(ks[:, T:nk], at(keys[1][0], m), ACT.Copy).then_inc(staged, 1)

                    def exps(n):
                        act.wait_ge(max_ready, m * U + (n + 1))
                        src, sc = (s_ps[:, n % 2, 0:NS], SCALE) if bias is None else (prob[:, n % NP, :], 1.0)
                        if bias is None:
                            act.wait_ge(t_ready, m * G + (n // merged + 1) * ng)
                        ins = nc.scalar.activation(prob[:, n % NP, :], src, ACT.Exp, bias=negm[:, n % NP:n % NP + 1],
                                                   scale=sc, accum_out=den[:, n % NP:n % NP + 1])
                        ins.then_inc(p_ready, 1)
                        if bias is None:
                            act.wait_ge(p_ready, m * U + (n + 1 + NP))
                            act.sem_inc(s_free, 1)

                    def keep(k, groups):
                        if k % share == 0 and 0 in groups:
                            act.wait_ge(o_ready, m * J + (k // share + 3 - PT))
                        for g in groups:
                            j = k * ng + g
                            act.wait_ge(t_ready, m * G + (j + 1 + (LAG + 2) * ng))
                            x1 = min(4, seen - 4 * g)
                            nc.scalar.activation(
                                probT[:, (k // share) % PT, 4 * g:4 * g + x1, (k % share) * P:(k % share + 1) * P],
                                t_ps[:, j % PTS, 0:x1, :], ACT.Copy).then_inc(t_free, 1)

                    for n in range(merged):
                        exps(n)
                    for k in range(M + LAG):
                        new = range((k + 1) * merged, min((k + 2) * merged, U))
                        if diff is not None and k < M:
                            a = (k % (LAG + 2)) * merged
                            act.wait_ge(rd_ready, m * M + (k + 1))
                            nc.scalar.activation(prob[:, a, :], prob[:, a, :], ACT.Copy,
                                                 scale=den[:, a:a + 1]).then_inc(scaled, 1)
                        if k >= LAG:
                            keep(k - LAG, early)
                        for n in new[:1]:
                            exps(n)
                        if k >= LAG and late:
                            keep(k - LAG, late)
                        for n in new[1:]:
                            exps(n)

            @block.vector
            def _(dve):
                st = Steps(dve, step)
                dve.sem_inc(o_free, PTS)
                if bias is not None:
                    dve.sem_inc(s_free, 2)
                nb = len(bias(0, 0, 0)) if bias is not None else 0
                per = U * (nb if nb else 1) + merged * M
                with dve.Fori(0, pairs) as m:
                    st.enter(m, per)
                    dve.wait_ge(o_ready, m * J + 2)
                    nc.vector.tensor_copy(ks[:, 0:keys[0][1]], at(keys[0][0], m)).then_inc(staged, 1)

                    def top(n):
                        t, u = units[n]
                        dve.wait_ge(s_ready, m * U + (n + 1))
                        s = s_ps[:, n % 2, 0:NS]
                        nm = negm[:, n % NP:n % NP + 1]
                        if bias is not None:
                            dve.wait_ge(t_ready, m * G + (n + 1) * ng)
                            b = bias(m, u, t)
                            w = b[0].shape[1]
                            p = prob[:, n % NP, :]
                            ins = nc.vector.scalar_tensor_tensor(out=p[:, 0:w], in0=s[:, 0:w], scalar=SCALE, in1=b[0],
                                                                 op0=ALU.mult, op1=ALU.add)
                            if w < NS:
                                ins = nc.vector.tensor_scalar(p[:, w:NS], s[:, w:NS], SCALE, None, ALU.mult)
                            st.done(ins)
                            dve.sem_inc(s_free, 1)
                            for more in b[1:]:
                                st.done(nc.vector.tensor_tensor(p[:, 0:w], p[:, 0:w], more, ALU.add))
                            nc.vector.tensor_reduce(nm, p, AX.X, ALU.max, negate=True).then_inc(max_ready, 1)
                        else:
                            dve.wait_ge(p_ready, m * U + (n + 1))
                            st.done(nc.vector.tensor_reduce(nm, s, AX.X, ALU.max, negate=True))
                            nc.vector.tensor_scalar(nm, nm, SCALE, None, ALU.mult).then_inc(max_ready, 1)

                    def invert(k):
                        dve.wait_ge(p_ready, m * U + ((k + 1) * merged + NP))
                        a = (k % (LAG + 2)) * merged
                        st.done(nc.vector.reciprocal(den[:, a:a + merged], den[:, a:a + merged]))
                        if diff is not None:
                            dve.sem_inc(rd_ready, 1)
                            st.done(nc.vector.tensor_scalar(den[:, a + 1:a + 2], den[:, a + 1:a + 2], diff, None,
                                                            ALU.mult))

                    def mix(k):
                        a = (k % (LAG + 2)) * merged
                        if diff is None:
                            nc.vector.tensor_scalar(prob[:, a, :], prob[:, a, :], den[:, a:a + 1], None,
                                                    ALU.mult).then_inc(d_ready, 1)
                        else:
                            dve.wait_ge(scaled, m * M + (k + 1))
                            nc.vector.scalar_tensor_tensor(out=prob[:, a, :], in0=prob[:, a + 1, :],
                                                           scalar=den[:, a + 1:a + 2], in1=prob[:, a, :],
                                                           op0=ALU.mult, op1=ALU.add).then_inc(d_ready, 1)

                    def result(j):
                        t, u = units[j * share * merged]
                        dve.wait_ge(o_ready, m * J + (j + 3))
                        rows = slice(0, P) if diff is not None else slice(64 * u, 64 * u + 64)
                        nc.vector.tensor_copy(at(out, m)[rows, t * P:(t + share) * P],
                                              o_ps[rows, j % PTS, 0:share * P]).then_inc(o_free, 1)

                    for n in range(merged):
                        top(n)
                    for k in range(M + LAG):
                        new = range((k + 1) * merged, min((k + 2) * merged, U))
                        if k < M:
                            invert(k)
                            if diff is None:
                                mix(k)
                        for n in new[:1]:
                            top(n)
                        if diff is not None and k < M:
                            mix(k)
                        for n in new[1:]:
                            top(n)
                        if k > LAG and (k - LAG) % share == 0:
                            result((k - LAG) // share - 1)
                    result(J - 1)
                st.leave(pairs)


def rope_tables(nc, tag, cst, pos_dram, cos, sin):
    MAGIC = 12582912.0
    C1, C2 = 6.28125, 2 * np.pi - 6.28125
    C2a = float(np.float32(np.round(C2 * 2 ** 20) / 2 ** 20))
    C3 = float(np.float32(2 * np.pi - C1 - C2a))
    with Phase(nc, tag) as ph:
        posi = ph.sb("posi", [P, T], I32)
        ang, turns, red = ph.sb("ang", [P, T]), ph.sb("turns", [P, T]), ph.sb("red", [P, T])
        loaded, step, reduced, used = (ph.sem(s) for s in ("loaded", "step", "reduced", "used"))
        with nc.Block() as block:
            @block.sync
            def _(sp):
                sp.dma_start(posi[:], pos_dram.partition_broadcast(P)).then_inc(loaded, 16)

            @block.vector
            def _(dve):
                st = Steps(dve, step)
                dve.wait_ge(loaded, 16)
                st.done(nc.vector.tensor_copy(ang[:], posi[:]))
                st.done(nc.vector.tensor_scalar(ang[:], ang[:], cst["freq"], None, ALU.mult))
                for j, quarter in enumerate((0.0, 0.25)):
                    if j:
                        dve.wait_ge(used, 1)
                    st.done(nc.vector.tensor_scalar(turns[:], ang[:], 1 / (2 * np.pi), quarter, ALU.mult, ALU.add))
                    st.done(nc.vector.tensor_scalar(turns[:], turns[:], MAGIC, None, ALU.add))
                    st.done(nc.vector.tensor_scalar(turns[:], turns[:], MAGIC, None, ALU.subtract))
                    st.done(nc.vector.scalar_tensor_tensor(out=red[:], in0=turns[:], scalar=-C1, in1=ang[:],
                                                           op0=ALU.mult, op1=ALU.add))
                    st.done(nc.vector.scalar_tensor_tensor(out=red[:], in0=turns[:], scalar=-C2a, in1=red[:],
                                                           op0=ALU.mult, op1=ALU.add))
                    st.done(nc.vector.scalar_tensor_tensor(out=red[:], in0=turns[:], scalar=-C3, in1=red[:],
                                                           op0=ALU.mult, op1=ALU.add))
                    st.done(nc.vector.tensor_scalar(red[:], red[:], quarter * 2 * np.pi, 3.1415925, ALU.add, ALU.min))
                    nc.vector.tensor_scalar(red[:], red[:], -3.1415925, None, ALU.max).then_inc(reduced, 1)

            @block.scalar
            def _(act):
                for j, table in enumerate((sin, cos)):
                    act.wait_ge(reduced, j + 1)
                    nc.scalar.activation(table, red[:], ACT.Sin).then_inc(used, 1)


def conv_taps(nc, a, g, y, taps, taps_b, gated, conved, step):
    K = taps.shape[2]
    half = K // 2
    C = a.shape[1]

    def scalar(act):
        for c in range(C):
            nc.scalar.activation(g[:, c, :], g[:, c, :], ACT.Sigmoid).then_inc(gated, 1)

    def vector(dve):
        st = Steps(dve, step)
        for c in range(C):
            dve.wait_ge(gated, c + 1)
            st.done(nc.vector.tensor_tensor(a[:, c, :], a[:, c, :], g[:, c, :], ALU.mult))
            st.done(nc.vector.tensor_scalar(y[:, c, :], a[:, c, :], taps[:, c, half:half + 1],
                                            taps_b[:, c:c + 1], ALU.mult, ALU.add))
            for t in range(K):
                if t == half:
                    continue
                s = t - half
                lo, hi = max(0, -s), T - max(0, s)
                st.done(nc.vector.scalar_tensor_tensor(out=y[:, c, lo:hi], in0=a[:, c, lo + s:hi + s],
                                                       scalar=taps[:, c, t:t + 1], in1=y[:, c, lo:hi],
                                                       op0=ALU.mult, op1=ALU.add))
            dve.sem_inc(conved, 1)
    return scalar, vector


def layer_norm_silu(nc, tag, cst, y, ln_g, ln_b):
    C = y.shape[1]
    parts = chunks(T)
    with Phase(nc, tag) as ph:
        sq = ph.sb("sq", [P, C, T])
        sd = ph.sb("sd", [P, T])
        mean_ps, var_ps = ph.ps("mean", [P, T]), ph.ps("var", [P, T])
        mean_ready, centred, squared, var_ready, sd_ready, normed, inverted = (ph.sem(s) for s in (
            "mean_ready", "centred", "squared", "var_ready", "sd_ready", "normed", "inverted"))
        with nc.Block() as block:
            @block.scalar
            def _(act):
                for c in range(C):
                    act.wait_ge(centred, c + 1)
                    nc.scalar.activation(sq[:, c, :], y[:, c, :], ACT.Square).then_inc(squared, 1)
                act.wait_ge(var_ready, 1)
                nc.scalar.activation(sd[:], var_ps[:], ACT.Sqrt, bias=cst["eps"], scale=1.0 / (C * P)).then_inc(sd_ready, 1)
                for c in range(C):
                    act.wait_ge(normed, c + 1)
                    nc.scalar.activation(y[:, c, :], y[:, c, :], ACT.Silu, bias=ln_b[:, c:c + 1])

            @block.tensor
            def _(pe):
                for o, w in parts:
                    for c in range(C):
                        mm = nc.tensor.matmul(mean_ps[:, o:o + w], cst["ones"], y[:, c, o:o + w], start=(c == 0),
                                              stop=(c == C - 1))
                mm.then_inc(mean_ready, 1)
                for o, w in parts:
                    for c in range(C):
                        pe.wait_ge(squared, c + 1)
                        mm = nc.tensor.matmul(var_ps[:, o:o + w], cst["ones"], sq[:, c, o:o + w], start=(c == 0),
                                              stop=(c == C - 1))
                mm.then_inc(var_ready, 1)

            @block.vector
            def _(dve):
                dve.wait_ge(mean_ready, 1)
                for c in range(C):
                    nc.vector.scalar_tensor_tensor(out=y[:, c, :], in0=mean_ps[:], scalar=-1.0 / (C * P),
                                                   in1=y[:, c, :], op0=ALU.mult, op1=ALU.add).then_inc(centred, 1)
                dve.wait_ge(centred, C)
                dve.wait_ge(sd_ready, 1)
                nc.vector.reciprocal(sd[:], sd[:]).then_inc(inverted, 1)
                dve.wait_ge(inverted, 1)
                for c in range(C):
                    nc.vector.scalar_tensor_tensor(out=y[:, c, :], in0=y[:, c, :], scalar=ln_g[:, c:c + 1],
                                                   in1=sd[:], op0=ALU.mult, op1=ALU.mult).then_inc(normed, 1)


class UpWeights:

    def __init__(self, nc, sb, w_dram):
        self.dram = w_dram
        self.w = sb("up_w", [P, 2, KD * 2 * P + 8])
        self.ready = [nc.alloc_semaphore("up_ready0"), nc.alloc_semaphore("up_ready1")]

    def load(self, sp, i, u):
        sp.dma_start(self.w[:, u], self.dram[bass.ds(i * 2 + u, 1)].rearrange(
            "a p n -> p (a n)")).then_inc(self.ready[u], 16)

    def start(self, sp):
        self.load(sp, 0, 0)
        self.load(sp, 0, 1)


def ffn_up(nc, tag, weights, src, hidden):
    K = len(src)
    W = K * 2 * P
    parts = chunks(T)
    with Phase(nc, tag) as ph:
        w, w_ready = weights.w, weights.ready
        ph.sems += w_ready
        y = ph.sb("y", [P, 2, T])
        acc = ph.ps("acc", [P, 2, 2, T // 2])
        acc2 = ph.ps("acc2", [P, 2, 2, T // 2])
        accs = (acc, acc2)
        mm_done, middle, conved, silu_done, hid_done, step = (ph.sem(s) for s in (
            "mm_done", "middle", "conved", "silu_done", "hid_done", "step"))
        with nc.Block() as block:
            @block.sync
            def _(sp):
                with sp.Fori(1, KF // 2) as i:
                    for u in range(2):
                        sp.wait_ge(hid_done, i * 2 + (u + 1))
                        weights.load(sp, i, u)

            @block.tensor
            def _(pe):
                with pe.Fori(0, KF // 2) as i:
                    for u in range(2):
                        pe.wait_ge(w_ready[u], i * 16 + 16)
                        pe.wait_ge(hid_done, i * 2 + (u + 1))
                        for s in range(2):
                            for c, (a, width) in enumerate(parts):
                                for k in range(K):
                                    mm = nc.tensor.matmul(accs[u][:, s, c, :], w[:, u, (2 * k + s) * P:(2 * k + s + 1) * P],
                                                          src[k][:, a:a + width], start=(k == 0), stop=(k == K - 1))
                            mm.then_inc(mm_done, 1)

            @block.scalar
            def _(act):
                with act.Fori(0, KF // 2) as i:
                    for u in range(2):
                        act.wait_ge(hid_done, i * 2 + (u + 2))
                        for s in range(2):
                            act.wait_ge(mm_done, i * 4 + (2 * u + s + 1))
                            f = accs[u][:, s].rearrange("p c n -> p (c n)")
                            nc.scalar.activation(y[:, s, :], f, ACT.Identity, bias=w[:, u, W + 4 * s + 3:W + 4 * s + 4],
                                                 scale=w[:, u, W + 4 * s + 1:W + 4 * s + 2]).then_inc(middle, 1)
                        act.wait_ge(conved, i * 2 + (u + 1))
                        nc.scalar.activation(y[:, 0, :], y[:, 0, :], ACT.Silu).then_inc(silu_done, 1)

            @block.vector
            def _(dve):
                st = Steps(dve, step)
                dve.sem_inc(hid_done, 2)
                with dve.Fori(0, KF // 2) as i:
                    st.enter(i, 8)
                    for u in range(2):
                        for s in range(2):
                            dve.wait_ge(middle, i * 4 + (2 * u + s + 1))
                            f = accs[u][:, s].rearrange("p c n -> p (c n)")
                            st.done(nc.vector.scalar_tensor_tensor(out=y[:, s, 1:T], in0=f[:, 0:T - 1],
                                                                   scalar=w[:, u, W + 4 * s:W + 4 * s + 1],
                                                                   in1=y[:, s, 1:T], op0=ALU.mult, op1=ALU.add))
                            st.done(nc.vector.scalar_tensor_tensor(out=y[:, s, 0:T - 1], in0=f[:, 1:T],
                                                                   scalar=w[:, u, W + 4 * s + 2:W + 4 * s + 3],
                                                                   in1=y[:, s, 0:T - 1], op0=ALU.mult, op1=ALU.add))
                            if s == 0:
                                dve.sem_inc(conved, 1)
                        dve.wait_ge(silu_done, i * 2 + (u + 1))
                        nc.vector.tensor_tensor(at(hidden, i * 2 + u), y[:, 0, :], y[:, 1, :], ALU.mult).then_inc(hid_done, 1)
                st.leave(KF // 2)




def modulation_scalars(nc, tag, cst, vecs, neg_lam, sub_g):
    with Phase(nc, tag) as ph:
        lam = ph.sb("lam", [P, 2])
        sum_ps = ph.ps("sum", [P, 2])
        step, prod_ready, sum_ready, exp_ready, ready = (ph.sem(s) for s in (
            "step", "prod_ready", "sum_ready", "exp_ready", "ready"))
        with nc.Block() as block:
            @block.scalar
            def _(act):
                act.wait_ge(sum_ready, 1)
                nc.scalar.activation(lam[:], sum_ps[:], ACT.Exp).then_inc(exp_ready, 1)

            @block.tensor
            def _(pe):
                pe.wait_ge(prod_ready, 1)
                nc.tensor.matmul(sum_ps[:], cst["ones"], lam[:], start=True, stop=True).then_inc(sum_ready, 1)

            @block.vector
            def _(dve):
                st = Steps(dve, step)
                l = vecs["lam"]
                nc.vector.tensor_tensor(lam[:, 0:1], l[:, 0:1], l[:, 1:2], ALU.mult)
                nc.vector.tensor_tensor(lam[:, 1:2], l[:, 2:3], l[:, 3:4], ALU.mult).then_inc(prod_ready, 1)
                nc.vector.tensor_scalar(sub_g, vecs["sub_g"], 0.8, None, ALU.mult)
                dve.wait_ge(exp_ready, 1)
                st.done(nc.vector.tensor_tensor(neg_lam, lam[:, 1:2], lam[:, 0:1], ALU.subtract))
                nc.vector.tensor_scalar(neg_lam, neg_lam, -0.2, None, ALU.add)


def silu_rows(nc, tag, src_dram, rows, ahead):
    with Phase(nc, tag) as ph:
        loaded = ph.sem("loaded")
        flat = rows.rearrange("p a n -> p (a n)")
        with nc.Block() as block:
            @block.sync
            def _(sp):
                sp.dma_start(flat, src_dram.partition_broadcast(P)).then_inc(loaded, 16)
                ahead.start(sp)

            @block.scalar
            def _(act):
                act.wait_ge(loaded, 16)
                nc.scalar.activation(flat, flat, ACT.Silu)


def modulation_gains(nc, tag, vecs, mod, a1, ac, a2, ac_shift):
    with Phase(nc, tag) as ph:
        step = ph.sem("step")
        with nc.Block() as block:
            @block.vector
            def _(dve):
                st = Steps(dve, step)
                for a in range(2):
                    st.done(nc.vector.tensor_tensor(mod[:, :, a], mod[:, :, a], vecs["b_mod"], ALU.add))
                for o, g, j, a in ((a1, "g1", 1, 0), (ac, "g1", 1, 1), (a2, "g2", 4, 0)):
                    nc.vector.scalar_tensor_tensor(out=o, in0=mod[:, j * KD:(j + 1) * KD, a], scalar=1.0,
                                                   in1=vecs[g], op0=ALU.add, op1=ALU.mult)
                nc.vector.tensor_copy(ac_shift, mod[:, 0:KD, 1])


def gla_decay(nc, tag, cst, w_dec, b_dec, low, n, decay):
    parts = chunks(n)
    with Phase(nc, tag) as ph:
        z = ph.sb("z", [P, 2, n])
        e = ph.sb("e", [P, 2, n])
        z_ps = ph.ps("z_ps", [P, 2, len(parts) * BANK])
        z_ready, z_kept, log_ready, sum_ready, step, own = (ph.sem(s) for s in (
            "z_ready", "z_kept", "log_ready", "sum_ready", "step", "own"))
        with nc.Block() as block:
            @block.tensor
            def _(pe):
                for d in range(2):
                    for a, w in parts:
                        mm = nc.tensor.matmul(z_ps[:, d, a:a + w], w_dec[0:32, d, :], low[0:32, a:a + w], start=True,
                                              stop=True)
                    mm.then_inc(z_ready, 1)

            @block.scalar
            def _(act):
                st = Steps(act, own)
                for d in range(2):
                    act.wait_ge(z_ready, d + 1)
                    st.done(nc.scalar.activation(z[:, d, :], z_ps[:, d, 0:n], ACT.Identity, bias=b_dec[:, d:d + 1]))
                    act.sem_inc(z_kept, 1)
                    st.done(nc.scalar.activation(e[:, d, :], z[:, d, :], ACT.Abs))
                    st.done(nc.scalar.activation(e[:, d, :], e[:, d, :], ACT.Exp, scale=-1.0))
                    nc.scalar.activation(e[:, d, :], e[:, d, :], ACT.Ln, bias=cst["one"]).then_inc(log_ready, 1)
                for d in range(2):
                    act.wait_ge(sum_ready, d + 1)
                    nc.scalar.activation(decay[:, d, :], z[:, d, :], ACT.Exp, scale=1.0 / 16)

            @block.vector
            def _(dve):
                for d in range(2):
                    dve.wait_ge(log_ready, d + 1)
                    nc.vector.scalar_tensor_tensor(out=z[:, d, :], in0=z[:, d, :], scalar=0.0, in1=e[:, d, :],
                                                   op0=ALU.min, op1=ALU.subtract).then_inc(sum_ready, 1)


def gla_context(nc, tag, cst, k, vb, decay, state):
    n = NCTX
    with Phase(nc, tag) as ph:
        tail = ph.sb("tail", [P, 2, n])
        zero = ph.sb("zero", [P, n])
        kt = ph.sb("kt", [P, 2, 2, P])
        t_ps = ph.ps("t_ps", [P, 2, 2, P])
        s_ps = ph.ps("s_ps", [P, 2, 4 * 64])
        scaled, turned, kept, done, step = (ph.sem(s) for s in ("scaled", "turned", "kept", "done", "step"))
        with nc.Block() as block:
            @block.vector
            def _(dve):
                st = Steps(dve, step)
                nc.vector.memset(zero[:], 0.0)
                nc.vector.memset(tail[:, 0, n - 1:n], 1.0)
                st.done(nc.vector.memset(tail[:, 1, 0:1], 1.0))
                nc.vector.tensor_tensor_scan(tail[:, 0, n - 2::-1], decay[:, 0, n - 1:0:-1], zero[:, 1:n], 1.0,
                                             ALU.mult, ALU.add)
                st.done(nc.vector.tensor_tensor_scan(tail[:, 1, 1:n], decay[:, 1, 0:n - 1], zero[:, 1:n], 1.0,
                                                     ALU.mult, ALU.add))
                for d in range(2):
                    nc.vector.tensor_tensor(tail[:, d, :], tail[:, d, :], k, ALU.mult).then_inc(scaled, 1)
                dve.wait_ge(turned, 1)
                nc.vector.tensor_copy(kt[:], t_ps[:]).then_inc(kept, 1)
                dve.wait_ge(done, 1)
                for d in range(2):
                    for h in range(4):
                        r = slice(32 * h, 32 * h + 32)
                        nc.vector.tensor_copy(state[r, :, d], s_ps[r, d, 64 * h:64 * h + 64])

            @block.tensor
            def _(pe):
                pe.wait_ge(scaled, 2)
                for d in range(2):
                    for t in range(2):
                        mm = nc.tensor.transpose(t_ps[:, d, t, :], tail[:, d, t * P:(t + 1) * P], cst["ident"])
                mm.then_inc(turned, 1)
                pe.wait_ge(kept, 1)
                for d in range(2):
                    for t in range(2):
                        mm = nc.tensor.matmul(s_ps[:, d, :], kt[:, d, t, :], vb[:, t, :], start=(t == 0), stop=(t == 1))
                mm.then_inc(done, 1)


def gla_scan(nc, tag, cst, q, k, decay, state, v_dram, o_dram, vb):
    DV = 64
    groups = DV // 4
    with Phase(nc, tag) as ph:
        kv = ph.sb("kv", [P, 4, T])
        s = ph.sb("s", [P, 2, 2, T])
        qs = ph.sb("qs", [P, 2, T])
        init = ph.sb("init", [P, 2, 2])
        orow = ph.sb("orow", [4, 2, T])
        o_ps = ph.ps("o_ps", [P, 2, T])
        v_ready = [ph.sem(f"v_ready{c}") for c in range(4)]
        stored = [ph.sem("stored0"), ph.sem("stored1")]
        kv_ready, kv3_ready, scanned, summed, weighted, o_ready, o_kept, step = (ph.sem(x) for x in (
            "kv_ready", "kv3_ready", "scanned", "summed", "weighted", "o_ready", "o_kept", "step"))
        with nc.Block() as block:
            @block.sync
            def _(sp):
                with sp.Fori(0, groups) as i:
                    for c in range(4):
                        if c < 3:
                            sp.wait_ge(kv_ready, i * 3 + (c + 1))
                        else:
                            sp.wait_ge(kv3_ready, i + 1)
                        for h in range(4):
                            row = v_dram[h, bass.ds(i * 4 + c, 1), :].rearrange("a t -> (a t)")
                            sp.dma_start(vb[32 * h:32 * h + 32, c, :], row.partition_broadcast(32)).then_inc(v_ready[c], 16)

            @block.gpsimd
            def _(pool):
                pool.sem_inc(kv_ready, 3)

                def outer(i, c):
                    pool.wait_ge(v_ready[c], i * 64 + 64)
                    pool.wait_ge(scanned, i * 4 + (c + 1))
                    nc.gpsimd.tensor_tensor(kv[:, c, :], k, vb[:, c, :], ALU.mult).then_inc(kv_ready, 1)

                def add(i, c):
                    pool.wait_ge(scanned, i * 4 + (c + 5))
                    nc.gpsimd.tensor_tensor(s[:, c % 2, 0, :], s[:, c % 2, 0, :], s[:, c % 2, 1, :],
                                            ALU.add).then_inc(summed, 1)

                def group(i, more):
                    add(i, 0)
                    outer(i, 2)
                    add(i, 1)
                    if more:
                        outer(i + 1, 0)
                    add(i, 2)
                    if more:
                        outer(i + 1, 1)
                    add(i, 3)

                outer(0, 0)
                outer(0, 1)
                with pool.Fori(0, groups - 1) as i:
                    group(i, True)
                group(groups - 1, False)

            @block.vector
            def _(dve):
                st = Steps(dve, step)
                dve.sem_inc(scanned, 4)
                dve.sem_inc(kv3_ready, 1)
                st.done(nc.vector.tensor_scalar(q, q, 32.0 ** -0.5, None, ALU.mult))

                def scan(i, c):
                    if c < 3:
                        dve.wait_ge(kv_ready, i * 3 + (c + 4))
                    else:
                        dve.wait_ge(kv3_ready, i + 2)
                    u = c % 2
                    st.done(nc.vector.tensor_copy(init[:, u, :], at(state, i * 4 + c)))
                    nc.vector.tensor_tensor_scan(s[:, u, 0, :], decay[:, 0, :], kv[:, c, :], init[:, u, 0:1],
                                                 ALU.mult, ALU.add)
                    nc.vector.tensor_tensor_scan(s[:, u, 1, ::-1], decay[:, 1, ::-1], kv[:, c, ::-1],
                                                 init[:, u, 1:2], ALU.mult, ALU.add).then_inc(scanned, 1)

                def weigh(i, c):
                    dve.wait_ge(summed, i * 4 + (c + 1))
                    dve.wait_ge(o_ready, i * 4 + (c + 1))
                    nc.vector.tensor_tensor(qs[:, c % 2, :], s[:, c % 2, 0, :], q, ALU.mult).then_inc(weighted, 1)

                def group(i, more):
                    scan(i, 1)
                    weigh(i, 0)
                    dve.wait_ge(v_ready[3], i * 64 + 64)
                    nc.vector.tensor_tensor(kv[:, 3, :], k, vb[:, 3, :], ALU.mult).then_inc(kv3_ready, 1)
                    scan(i, 2)
                    weigh(i, 1)
                    scan(i, 3)
                    weigh(i, 2)
                    if more:
                        scan(i + 1, 0)
                    weigh(i, 3)

                scan(0, 0)
                with dve.Fori(0, groups - 1) as i:
                    st.enter(i, 4)
                    group(i, True)
                st.leave(groups - 1)
                group(groups - 1, False)

            @block.tensor
            def _(pe):
                pe.sem_inc(o_ready, 2)
                with pe.Fori(0, DV // 2) as i:
                    for u in range(2):
                        pe.wait_ge(weighted, i * 2 + (u + 1))
                        pe.wait_ge(o_kept, i * 2 + (u + 1))
                        for a, w in chunks(T):
                            mm = nc.tensor.matmul(o_ps[0:4, u, a:a + w], cst["heads32"], qs[:, u, a:a + w], start=True,
                                                  stop=True)
                        mm.then_inc(o_ready, 1)

            @block.scalar
            def _(act):
                act.sem_inc(o_kept, 2)
                act.sem_inc(stored[0], 16)
                act.sem_inc(stored[1], 16)
                with act.Fori(0, DV // 2) as i:
                    for u in range(2):
                        act.wait_ge(o_ready, i * 2 + (u + 3))
                        act.wait_ge(stored[u], i * 16 + 16)
                        nc.scalar.activation(orow[:, u, :], o_ps[0:4, u, :], ACT.Copy).then_inc(o_kept, 1)
                        act.wait_ge(o_kept, i * 2 + (u + 3))
                        act.dma_start(o_dram[:, bass.ds(i * 2 + u, 1), :].rearrange("h a t -> h (a t)"),
                                      orow[:, u, :]).then_inc(stored[u], 16)
                for u in range(2):
                    act.wait_ge(stored[u], 16 + 16 * (DV // 2))


def gated(nc, tag, x, gate):
    with Phase(nc, tag) as ph:
        silu_done = ph.sem("silu_done")
        with nc.Block() as block:
            @block.scalar
            def _(act):
                for c in range(x.shape[1]):
                    nc.scalar.activation(gate[:, c, :], gate[:, c, :], ACT.Silu).then_inc(silu_done, 1)

            @block.vector
            def _(dve):
                for c in range(x.shape[1]):
                    dve.wait_ge(silu_done, c + 1)
                    nc.vector.tensor_tensor(x[:, c, :], x[:, c, :], gate[:, c, :], ALU.mult)


E_ = 32
NB = 48
NBI = NB + 1
TT = T // P


def router(nc, tag, cst, vecs, din, n, h2_dram, r):
    with Phase(nc, tag) as ph:
        w = ph.sb("w", [P, KD, 36])
        lgT = ph.sb("lgT", [36, T])
        row = ph.sb("row", [P, 2, D])
        lg = ph.sb("lg", [P, TT, 36])
        pen, le, cand, eq = (ph.sb(x, [P, TT, E_]) for x in ("pen", "le", "cand", "eq"))
        oh = ph.sb("oh", [P, 2, TT, E_])
        both = ph.sb("both", [P, TT, E_])
        g4, g4b = ph.sb("g4", [P, TT, 4]), ph.sb("g4b", [P, TT, 4])
        c1, top, low, pg = (ph.sb(x, [P, TT]) for x in ("c1", "top", "low", "pg"))
        base, nblk, incl, onesr = (ph.sb(x, [P, E_]) for x in ("base", "nblk", "incl", "onesr"))
        cmp = ph.sb("cmp", [P, NB, E_])
        bex, cnt = ph.sb("bex", [P, NB]), ph.sb("cnt", [P, 2])
        slotf, blkf = ph.sb("slotf", [P, 2, TT]), ph.sb("blkf", [P, 2, TT])
        l_ps = ph.ps("l_ps", [P, T])
        lt_ps = ph.ps("lt_ps", [P, TT, 36])
        r_ps = ph.ps("r_ps", [P, 2, T // 2])
        pre_ps = ph.ps("pre_ps", [P, TT, E_])
        tot_ps = ph.ps("tot_ps", [P, E_])
        loaded, l_ready, l_kept, lt_ready, lt_kept, row_ready, row_kept, stored, stepv, exp_a, exp_a_done = (
            ph.sem(x) for x in ("loaded", "l_ready", "l_kept", "lt_ready", "lt_kept", "row_ready", "row_kept", "stored",
                                "step", "exp_a", "exp_a_done"))
        both_ready, pre_ready, row_stored = ph.sem("both_ready"), ph.sem("pre_ready"), [ph.sem("row_stored0"), ph.sem("row_stored1")]
        with nc.Block() as block:
            @block.sync
            def _(sp):
                sp.dma_start(w[:], din["w_route"]).then_inc(loaded, 16)
                for t in range(TT):
                    sp.wait_ge(row_kept, 2 * (t + 1))
                    sp.dma_start(h2_dram[t * P:(t + 1) * P, :], row[:, t % 2, :]).then_inc(row_stored[t % 2], 16)
                for u in range(2):
                    sp.wait_ge(row_stored[u], 16 * TT // 2)

            @block.tensor
            def _(pe):
                pe.wait_ge(loaded, 16)
                for a, wd in chunks(T):
                    for k in range(KD):
                        mm = nc.tensor.matmul(l_ps[0:36, a:a + wd], w[:, k, :], n[:, k, a:a + wd], start=(k == 0),
                                              stop=(k == KD - 1))
                mm.then_inc(l_ready, 1)
                pe.wait_ge(l_kept, 1)
                for t in range(TT):
                    mm = nc.tensor.transpose(lt_ps[:, t, :], lgT[:, t * P:(t + 1) * P], cst["ident"][0:36, 0:36])
                mm.then_inc(lt_ready, 1)
                for t in range(TT):
                    for half in range(2):
                        j = 2 * t + half
                        if j >= 2:
                            pe.wait_ge(row_kept, j - 1)
                        for k in range(4):
                            mm = nc.tensor.transpose(r_ps[:, half, k * P:(k + 1) * P],
                                                     n[:, half * 4 + k, t * P:(t + 1) * P], cst["ident"])
                        mm.then_inc(row_ready, 1)
                pe.wait_ge(both_ready, 1)
                for t in range(TT):
                    for s in range(t):
                        nc.tensor.matmul(pre_ps[:, t, :], cst["ones"], both[:, s, :], start=(s == 0), stop=False)
                    nc.tensor.matmul(pre_ps[:, t, :], cst["before"], both[:, t, :], start=(t == 0), stop=True)
                for t in range(TT):
                    mm = nc.tensor.matmul(tot_ps[:], cst["ones"], both[:, t, :], start=(t == 0), stop=(t == TT - 1))
                mm.then_inc(pre_ready, 1)

            @block.scalar
            def _(act):
                act.wait_ge(l_ready, 1)
                nc.scalar.activation(lgT[:], l_ps[0:36, :], ACT.Identity, bias=vecs["b_route"][0:36]).then_inc(l_kept, 1)
                for t in range(TT):
                    for half in range(2):
                        j = 2 * t + half
                        if half == 0 and t >= 2:
                            act.wait_ge(row_stored[t % 2], 16 * (t // 2))
                        act.wait_ge(row_ready, j + 1)
                        nc.scalar.activation(row[:, t % 2, half * 512:half * 512 + 512], r_ps[:, half, :],
                                             ACT.Copy).then_inc(row_kept, 1)
                for j, (x, flat) in enumerate(((g4, "p t g -> p (t g)"), (top, None))):
                    act.wait_ge(exp_a, j + 1)
                    y = x[:].rearrange(flat) if flat else x[:]
                    nc.scalar.activation(y, y, ACT.Exp).then_inc(exp_a_done, 1)

            @block.vector
            def _(dve):
                st = Steps(dve, stepv)
                V = nc.vector

                def spread(x, m):
                    return x.unsqueeze(2).broadcast_to([P, TT, m])

                def choose(logits, m, onehot, best, tmp):
                    index = cst["index"][:, 0:m].unsqueeze(1).broadcast_to([P, TT, m])
                    st.done(V.tensor_reduce(best, logits, AX.X, ALU.max))
                    st.done(V.tensor_tensor(tmp, logits, spread(best, m), ALU.is_equal))
                    st.done(V.tensor_tensor(tmp, tmp, index, ALU.mult))
                    st.done(V.tensor_reduce(c1[:], tmp, AX.X, ALU.min))
                    st.done(V.tensor_tensor(onehot, tmp, spread(c1[:], m), ALU.is_equal))

                dve.wait_ge(lt_ready, 1)
                st.done(V.tensor_copy(lg[:], lt_ps[:]))
                lgG = lg[:, :, 0:4]
                choose(lgG, 4, g4b[:], pg[:], g4[:])
                st.done(V.tensor_tensor(g4[:], lgG, spread(pg[:], 4), ALU.subtract))
                dve.sem_inc(exp_a, 1)
                st.done(V.tensor_scalar(g4b[:], g4b[:], -1.0, 1e30, ALU.add, ALU.mult))
                for g in range(4):
                    st.done(V.tensor_tensor(le[:, :, g * 8:g * 8 + 8], lg[:, :, 4 + g * 8:12 + g * 8],
                                            g4b[:, :, g:g + 1].broadcast_to([P, TT, 8]), ALU.add))
                choose(le[:], E_, oh[:, 0], top[:], cand[:])
                st.done(V.scalar_tensor_tensor(out=pen[:], in0=oh[:, 0], scalar=-2e30, in1=le[:], op0=ALU.mult,
                                               op1=ALU.add))
                choose(pen[:], E_, oh[:, 1], low[:], cand[:])
                st.done(V.tensor_tensor(top[:], low[:], top[:], ALU.subtract))
                dve.sem_inc(exp_a, 1)
                st.done(V.tensor_tensor(both[:], oh[:, 0], oh[:, 1], ALU.add))
                dve.sem_inc(both_ready, 1)
                dve.wait_ge(exp_a_done, 2)
                st.done(V.tensor_reduce(pg[:], g4[:], AX.X, ALU.add))
                st.done(V.tensor_scalar(low[:], top[:], 1.0, None, ALU.add))
                st.done(V.tensor_tensor(low[:], low[:], pg[:], ALU.mult))
                st.done(V.reciprocal(r["gate"][:, 0], low[:]))
                st.done(V.tensor_tensor(r["gate"][:, 1], r["gate"][:, 0], top[:], ALU.mult))
                dve.wait_ge(pre_ready, 1)
                st.done(V.tensor_scalar(nblk[:], tot_ps[:], 127.0, 1.0 / P, ALU.add, ALU.mult))
                st.done(V.tensor_scalar(nblk[:], nblk[:], -0.498, None, ALU.add))
                st.done(V.tensor_scalar(nblk[:], nblk[:], 12582912.0, None, ALU.add))
                st.done(V.tensor_scalar(nblk[:], nblk[:], 12582912.0, None, ALU.subtract))
                st.done(V.memset(onesr[:], 1.0))
                st.done(V.tensor_tensor_scan(incl[:], onesr[:], nblk[:], 0.0, ALU.mult, ALU.add))
                st.done(V.tensor_copy(cnt[:, 0:1], incl[:, E_ - 1:E_]))
                st.done(V.tensor_scalar(cnt[:, 1:2], cnt[:, 0:1], 1.0, 0.5, ALU.add, ALU.mult))
                st.done(V.tensor_scalar(cnt[:, 1:2], cnt[:, 1:2], -0.25, None, ALU.add))
                st.done(V.tensor_scalar(cnt[:, 1:2], cnt[:, 1:2], 12582912.0, None, ALU.add))
                st.done(V.tensor_scalar(cnt[:, 1:2], cnt[:, 1:2], 12582912.0, None, ALU.subtract))
                st.done(V.tensor_copy(r["count"], cnt[:]))
                st.done(V.tensor_tensor(base[:], incl[:], nblk[:], ALU.subtract))
                st.done(V.tensor_scalar(base[:], base[:], float(P), None, ALU.mult))
                st.done(V.tensor_tensor(le[:], pre_ps[:], base[:].unsqueeze(1).broadcast_to([P, TT, E_]), ALU.add))
                for a in range(2):
                    st.done(V.tensor_tensor(cand[:], oh[:, a], le[:], ALU.mult))
                    st.done(V.tensor_reduce(slotf[:, a], cand[:], AX.X, ALU.add))
                st.done(V.tensor_copy(r["slot"], slotf[:]))
                st.done(V.tensor_scalar(blkf[:], slotf[:], 1.0 / P, -0.498, ALU.mult, ALU.add))
                st.done(V.tensor_scalar(blkf[:], blkf[:], 12582912.0, None, ALU.add))
                st.done(V.tensor_scalar(blkf[:], blkf[:], 12582912.0, 1.0 - P * NBI, ALU.subtract, ALU.mult))
                st.done(V.scalar_tensor_tensor(out=slotf[:], in0=slotf[:], scalar=float(NBI), in1=blkf[:],
                                               op0=ALU.mult, op1=ALU.add))
                st.done(V.tensor_copy(r["place"], slotf[:]))
                st.done(V.tensor_tensor(cmp[:], incl[:].unsqueeze(1).broadcast_to([P, NB, E_]),
                                        cst["block"].unsqueeze(2).broadcast_to([P, NB, E_]), ALU.is_le))
                st.done(V.tensor_reduce(bex[:], cmp[:], AX.X, ALU.add))
                st.done(V.tensor_scalar(bex[:], bex[:], float(E_ - 1), None, ALU.min))
                st.done(V.tensor_copy(r["block"], bex[:]))


def expert_of(eng, r, block):
    at_block = bass.ds(block, 1) if not isinstance(block, int) else slice(block, block + 1)
    return eng.value_load(r["block"][0:1, at_block], min_val=0, max_val=E_ - 1)


def load_up(sp, din, e, wu, u, u_ready):
    sp.dma_start(wu[:, u], din["w_eup"][bass.ds(e, 1)].rearrange("a (k p) n -> p (a k) n", p=P)).then_inc(u_ready[u], 16)


def dispatch(nc, tag, cst, r, ids_dram, ids, din, wu, u_ready):
    with Phase(nc, tag) as ph:
        token = ph.sb("token", [P, TT], I32)
        zero = ph.sb("zero", [P, NBI], I32)
        made, cleared, scattered, read = (ph.sem(x) for x in ("made", "cleared", "scattered", "read"))
        with nc.Block() as block:
            @block.sync
            def _(sp):
                sp.wait_ge(cleared, 16)
                load_up(sp, din, expert_of(sp, r, 0), wu, 0, u_ready)

            @block.gpsimd
            def _(pool):
                nc.gpsimd.memset(zero[:], 0).then_inc(made, 1)
                nc.gpsimd.iota(token[:], [[P, TT]], base=0, channel_multiplier=1).then_inc(made, 1)
                pool.wait_ge(made, 2)
                pool.dma_start(ids_dram.rearrange("(p b) a -> p (b a)", b=NBI), zero[:]).then_inc(cleared, 16)
                pool.wait_ge(cleared, 16)
                for a in range(2):
                    for t in range(TT):
                        pool.indirect_dma_start(ids_dram, bass.IndirectOffsetOnAxis(ap=r["place"][:, a, t:t + 1], axis=0),
                                                token[:, t:t + 1], None).then_inc(scattered, 16)
                pool.wait_ge(scattered, 16 * 2 * TT)
                pool.dma_start(ids, ids_dram.rearrange("(p b) a -> p (b a)", b=NBI)).then_inc(read, 16)
                pool.wait_ge(read, 16)


def experts(nc, tag, cst, din, r, ids, h2_dram, y_dram, y_filled, wu, u_ready):
    H = 512
    KH = H // P
    with Phase(nc, tag) as ph:
        ph.sems += u_ready
        wd = ph.sb("wd", [P, 2, KH, D])
        xb = ph.sb("xb", [P, 2, D])
        xT = ph.sb("xT", [P, 2, KD, P])
        idx = ph.sb("idx", [P, 2], I32)
        hid = ph.sb("hid", [P, 2, H])
        hT = ph.sb("hT", [P, KH, P])
        y = ph.sb("y", [P, 2, D])
        x_ps = ph.ps("x_ps", [P, KD, P])
        up_ps = ph.ps("up_ps", [P, 2, H])
        h_ps = ph.ps("h_ps", [P, KH, P])
        y_ps = ph.ps("y_ps", [P, D])
        d_ready = [ph.sem("d_ready0"), ph.sem("d_ready1")]
        x_ready = [ph.sem("x_ready0"), ph.sem("x_ready1")]
        stored = [ph.sem("stored0"), ph.sem("stored1")]
        idx_seen = ph.sem("idx_seen")
        gate_done = ph.sem("gate_done")
        idx_set, turned, xT_ready, up_done, silu_done, hid_ready, h_turned, hT_ready, y_done, y_kept = (ph.sem(x) for x in (
            "idx_set", "turned", "xT_ready", "up_done", "silu_done", "hid_ready", "h_turned", "hT_ready", "y_done",
            "y_kept"))

        def used(eng):
            return eng.value_load(r["count"][0:1, 0:1], min_val=1, max_val=NB)

        with nc.Block() as block:
            @block.sync
            def _(sp):
                nb = used(sp)
                sp.wait_ge(x_ready[0], 16)

                def load(i, u, up):
                    e = expert_of(sp, r, i * 2 + u)
                    if up:
                        sp.wait_ge(up_done, i * 2 + (u + 1))
                        load_up(sp, din, e, wu, u, u_ready)
                    sp.wait_ge(y_done, i * 2 + (u + 1))
                    sp.dma_start(wd[:, u], din["w_edown"][bass.ds(e, 1)].rearrange(
                        "a (k p) n -> p (a k) n", p=P)).then_inc(d_ready[u], 16)

                load(0, 0, False)
                load(0, 1, True)
                with sp.Fori(1, NB // 2) as i:
                    with sp.If(i * 2 < nb):
                        for u in range(2):
                            load(i, u, True)

            @block.gpsimd
            def _(pool):
                nb = used(pool)

                def gather(i, u, nth):
                    nc.gpsimd.tensor_copy(idx[:, u:u + 1], ids[:, bass.ds(i * 2 + u, 1)]).then_inc(idx_set, 1)
                    pool.wait_ge(idx_set, nth)
                    pool.sem_inc(idx_seen, 1)
                    pool.indirect_dma_start(xb[:, u, :], None, h2_dram,
                                            bass.IndirectOffsetOnAxis(ap=idx[:, u:u + 1], axis=0)).then_inc(x_ready[u], 16)

                gather(0, 0, 1)
                with pool.Fori(0, NB // 2) as i:
                    with pool.If(i * 2 < nb):
                        pool.wait_ge(turned, i * 2 + 1)
                        gather(i, 1, i * 2 + 2)
                        pool.wait_ge(turned, i * 2 + 2)
                        gather(i + 1, 0, i * 2 + 3)

            @block.tensor
            def _(pe):
                nb = used(pe)
                for s, n in ((turned, 1), (up_done, 2), (h_turned, 1), (y_done, 2)):
                    pe.sem_inc(s, n)

                def turn(i, u, part):
                    if part == 0:
                        pe.wait_ge(x_ready[u], i * 16 + 16)
                        pe.wait_ge(xT_ready, i * 2 + (u + 1))
                    for k in range(part * KD // 2, (part + 1) * KD // 2):
                        mm = nc.tensor.transpose(x_ps[:, k, :], xb[:, u, k * P:(k + 1) * P], cst["ident"])
                    if part == 1:
                        mm.then_inc(turned, 1)

                def up(i, u):
                    pe.wait_ge(xT_ready, i * 2 + (u + 2))
                    pe.wait_ge(u_ready[u], i * 16 + 16)
                    pe.wait_ge(hid_ready, i * 2 + (u + 1))
                    for s in range(2):
                        for k in range(KD):
                            mm = nc.tensor.matmul(up_ps[:, s, :], xT[:, u, k, :], wu[:, u, k, s * H:(s + 1) * H],
                                                  start=(k == 0), stop=(k == KD - 1))
                        mm.then_inc(up_done if s else gate_done, 1)

                def down(i, u, turn_between):
                    pe.wait_ge(hid_ready, i * 2 + (u + 2))
                    pe.wait_ge(hT_ready, i * 2 + (u + 1))
                    for k in range(KH):
                        mm = nc.tensor.transpose(h_ps[:, k, :], hid[:, 1, k * P:(k + 1) * P], cst["ident"])
                    mm.then_inc(h_turned, 1)
                    turn_between()
                    pe.wait_ge(hT_ready, i * 2 + (u + 2))
                    pe.wait_ge(d_ready[u], i * 16 + 16)
                    pe.wait_ge(y_kept, i * 2 + (u + 1))
                    for a, w in chunks(D):
                        for k in range(KH):
                            mm = nc.tensor.matmul(y_ps[:, a:a + w], hT[:, k, :], wd[:, u, k, a:a + w], start=(k == 0),
                                                  stop=(k == KH - 1))
                    mm.then_inc(y_done, 1)

                turn(0, 0, 0)
                turn(0, 0, 1)
                with pe.Fori(0, NB // 2) as i:
                    with pe.If(i * 2 < nb):
                        up(i, 0)
                        turn(i, 1, 0)
                        down(i, 0, lambda: turn(i, 1, 1))
                        up(i, 1)
                        turn(i + 1, 0, 0)
                        down(i, 1, lambda: turn(i + 1, 0, 1))

            @block.scalar
            def _(act):
                nb = used(act)
                for s, n in ((stored[0], 16), (stored[1], 16), (xT_ready, 1), (y_kept, 1)):
                    act.sem_inc(s, n)

                def keep_x(i, u):
                    act.wait_ge(turned, i * 2 + (u + 2))
                    act.wait_ge(up_done, i * 2 + (u + 1))
                    nc.scalar.activation(xT[:, u], x_ps[:], ACT.Copy).then_inc(xT_ready, 1)

                def silu(i, u):
                    act.wait_ge(gate_done, i * 2 + (u + 1))
                    act.wait_ge(hid_ready, i * 2 + (u + 1))
                    nc.scalar.activation(hid[:, 0, :], up_ps[:, 0, :], ACT.Silu).then_inc(silu_done, 1)

                def keep_y(i, u):
                    act.wait_ge(y_done, i * 2 + (u + 3))
                    act.wait_ge(stored[u], i * 16 + 16)
                    nc.scalar.activation(y[:, u, :], y_ps[:], ACT.Copy).then_inc(y_kept, 1)
                    act.wait_ge(y_kept, i * 2 + (u + 2))
                    act.dma_start(y_dram[bass.ds(i * 2 + u, 1)].rearrange("a p n -> p (a n)"),
                                  y[:, u, :]).then_inc(stored[u], 16)

                keep_x(0, 0)
                act.wait_ge(y_filled, 16)
                with act.Fori(0, NB // 2) as i:
                    with act.If(i * 2 < nb):
                        silu(i, 0)
                        keep_x(i, 1)
                        keep_y(i, 0)
                        silu(i, 1)
                        keep_x(i + 1, 0)
                        keep_y(i, 1)
                pairs = act.value_load(r["count"][0:1, 1:2], min_val=1, max_val=NB // 2)
                for u in range(2):
                    act.wait_ge(stored[u], pairs * 16 + 16)
                act.sem_inc(y_kept, 1)

            @block.vector
            def _(dve):
                nb = used(dve)
                dve.sem_inc(hid_ready, 1)
                dve.sem_inc(hT_ready, 1)
                with dve.Fori(0, NB // 2) as i:
                    with dve.If(i * 2 < nb):
                        for u in range(2):
                            dve.wait_ge(silu_done, i * 2 + (u + 1))
                            dve.wait_ge(up_done, i * 2 + (u + 3))
                            dve.wait_ge(h_turned, i * 2 + (u + 1))
                            nc.vector.tensor_tensor(hid[:, 1, :], hid[:, 0, :], up_ps[:, 1, :],
                                                    ALU.mult).then_inc(hid_ready, 1)
                            dve.wait_ge(h_turned, i * 2 + (u + 2))
                            dve.wait_ge(y_done, i * 2 + (u + 2))
                            nc.vector.tensor_copy(hT[:], h_ps[:]).then_inc(hT_ready, 1)


def combine(nc, tag, cst, r, y_dram, gate5, h):
    with Phase(nc, tag) as ph:
        f = ph.sb("f", [P, 2, 2, D])
        f_ps = ph.ps("f_ps", [P, 2, 4, P])
        got = [ph.sem("got0"), ph.sem("got1")]
        mixed, turned, added, step = (ph.sem(x) for x in ("mixed", "turned", "added", "step"))
        with nc.Block() as block:
            @block.gpsimd
            def _(pool):
                for t in range(TT):
                    if t >= 2:
                        pool.wait_ge(turned, 2 * (t - 1))
                    for a in range(2):
                        pool.indirect_dma_start(f[:, t % 2, a, :], None, y_dram,
                                                bass.IndirectOffsetOnAxis(ap=r["slot"][:, a, t:t + 1], axis=0)
                                                ).then_inc(got[t % 2], 16)

            @block.vector
            def _(dve):
                st = Steps(dve, step)
                for t in range(TT):
                    dve.wait_ge(got[t % 2], 32 * (t // 2 + 1))
                    st.done(nc.vector.tensor_scalar(f[:, t % 2, 0, :], f[:, t % 2, 0, :], r["gate"][:, 0, t:t + 1], None,
                                                    ALU.mult))
                    nc.vector.scalar_tensor_tensor(out=f[:, t % 2, 0, :], in0=f[:, t % 2, 1, :],
                                                   scalar=r["gate"][:, 1, t:t + 1], in1=f[:, t % 2, 0, :], op0=ALU.mult,
                                                   op1=ALU.add).then_inc(mixed, 1)
                    for half in range(2):
                        dve.wait_ge(turned, 2 * t + half + 1)
                        for k in range(4):
                            o = h[:, half * 4 + k, t * P:(t + 1) * P]
                            ins = nc.vector.scalar_tensor_tensor(out=o, in0=f_ps[:, half, k, :],
                                                                 scalar=gate5[:, half * 4 + k:half * 4 + k + 1], in1=o,
                                                                 op0=ALU.mult, op1=ALU.add)
                        ins.then_inc(added, 1)

            @block.tensor
            def _(pe):
                for t in range(TT):
                    pe.wait_ge(mixed, t + 1)
                    for half in range(2):
                        if t:
                            pe.wait_ge(added, 2 * t + half - 1)
                        for k in range(4):
                            mm = nc.tensor.transpose(f_ps[:, half, k, :], f[:, t % 2, 0, (half * 4 + k) * P:(half * 4 + k + 1) * P],
                                                     cst["ident"])
                        mm.then_inc(turned, 1)


def second_block(nc, din, cst, vecs, h, mod, neg_lam, sub_g, y_dram, y_filled, upto):
    h_dram = nc.dram_tensor("h_dram", (P, KD, T), F32).ap()
    v_dram = nc.dram_tensor("v_dram", (2, P, T), F32).ap()
    o_dram = nc.dram_tensor("o_dram", (2, P, T), F32).ap()
    with ExitStack() as outer:
        def keep(name, shape, dt=F32):
            return outer.enter_context(nc.sbuf_tensor(name, shape, dt))

        a1, ac, a2, shc = (keep(x, [P, KD]) for x in ("a1", "ac", "a2", "shc"))
        modulation_gains(nc, "mg", vecs, mod, a1[:], ac[:], a2[:], shc[:])

        def m(j):
            return mod[:, j * KD:(j + 1) * KD, 0]

        store_all(nc, "sh", [(h_dram, h[:])])
        with ExitStack() as ctx:
            def sb(name, shape, dt=F32):
                return ctx.enter_context(nc.sbuf_tensor(name, shape, dt))

            pr = sb("pr", [P, 19, T])
            pc = sb("pc", [P, 8, NCTX])
            v2 = sb("v2", [P, TT + 2, 768])
            with nc.sbuf_tensor("vbc", [P, 2, 256], F32) as vbc, nc.sbuf_tensor("state", [P, 64, 2], F32) as state:
                with ExitStack() as inner:
                    w_q2 = Weights(nc, lambda name, shape: inner.enter_context(nc.sbuf_tensor(name, shape, F32)), "q2",
                                   din["w_in2"], KD, 19)
                    rms_norm(nc, "m1", cst, h, h, a1, m(0), ahead=w_q2)
                    project(nc, "q2", din["w_in2"], cols(h), T, 19, dst=pr, weights=w_q2)
                project_rows(nc, "r2", din["w_v2"][:, :, 0:768], cols(h), T, v2)
                nctx = h[:, 0:2, :].rearrange("p a (b c) -> p (a b) c", c=NCTX)
                load_all(nc, "lc", [(nctx, din["ctx"])])
                rms_norm(nc, "mc", cst, nctx, nctx, ac, shc)
                project(nc, "qc", din["w_in2"], cols(nctx), NCTX, 8, dst=pc)
                project_rows(nc, "rc", din["w_v2"][:, :, 0:768], cols(nctx), NCTX, v2[:, TT:, :])
                project_rows(nc, "rb", din["w_v2"][:, :, 768:1024], cols(nctx), NCTX, vbc)
                if upto == 21:
                    return
                store_all(nc, "sv", [(v_dram.rearrange("a p t -> p a t"), pr[:, 15:17, :])])
                decay = h[:, 0:2, :]
                decay_c = h[:, 2, 0:2 * NCTX].rearrange("p (a t) -> p a t", a=2)
                wdec = h[:, 3, 0:2 * P].rearrange("p (a t) -> p a t", a=2)
                load_all(nc, "ldw", [(wdec[0:32], din["w_dec"])])
                gla_decay(nc, "dx", cst, wdec, vecs["b_dec"], pr[:, 7, :], T, decay)
                gla_decay(nc, "dc", cst, wdec, vecs["b_dec"], pc[:, 7, :], NCTX, decay_c)
                gla_context(nc, "gc", cst, pc[:, 6, :], vbc, decay_c, state)
                gla_scan(nc, "gs", cst, pr[:, 14, :], pr[:, 6, :], decay, state,
                         v_dram.rearrange("a (h v) t -> (a h) v t", v=64), o_dram.rearrange("a (h v) t -> (a h) v t", v=64),
                         h[:, 4:8, :])
                load_all(nc, "lo", [(pr[:, 15:17, :], o_dram.rearrange("a p t -> p a t"))])
            head_norm(nc, "hg", cst, pr[:, 15:17, :], T, vecs["gla_g"])
            gated(nc, "gg", pr[:, 15:17, :], pr[:, 17:19, :])
            if upto == 22:
                return
            load_all(nc, "lt", [(h[:, 0, :], din["cos2"]), (h[:, 1, :], din["sin2"])])
            rope2 = (cst["rot2"], h[:, 0, :], h[:, 1, :])
            rotary(nc, "ra", pr[:, 0:4, :], rope2)
            rotary(nc, "rq", pr[:, 8:12, :], rope2)
            attention(nc, "ad", cst, 4, pr[:, 8:12, :], [(pr[:, 0:4, :], T), (pc[:, 0:4, :], NCTX)], v2[:, :, 0:512],
                      TT + 2, diff=neg_lam[:], scratch=h)
            head_norm(nc, "hs", cst, pr[:, 8:12, :], T, sub_g[:], blk=P)
            with nc.sbuf_tensor("near", [P, TT, 640], F32) as near, nc.sbuf_tensor("tab", [P, 4, 18 * 64], F32) as tab:
                load_all(nc, "ln", [(near[:], din["near"]), (tab[:], din["rpb"])])

                def bias(m_, u, t):
                    d0 = min(max(2 * t - 4, 0), 6) - 2 * t + 8
                    return [at(tab, m_ * 2 + u)[:, d0 * 64:d0 * 64 + 640], near[:, t, :]]
                window = [[min(max(2 * t - 4, 0), 6) // 2 + x for x in range(5)] + [TT, TT + 1] for t in range(TT)]
                attention(nc, "an", cst, 2, pr[:, 12:14, :], [(pr[:, 4:6, :], T), (pc[:, 4:6, :], NCTX)],
                          v2[:, :, 512:768], TT + 2, bias=bias, window=window, scratch=h)
            if upto == 23:
                return
            w_o2 = Weights(nc, sb, "o2", din["w_out2"], KD, KD)
            load_all(nc, "lh", [(h[:], h_dram)], ahead=w_o2)
            mixed = cols(pr[:, 8:12, :]) + cols(pr[:, 15:17, :]) + cols(pr[:, 12:14, :])
            project(nc, "o2", din["w_out2"], mixed, T, KD, add_to=h, gate=m(2), weights=w_o2)
        if upto == 24:
            return
        h2_dram = nc.dram_tensor("h2_dram", (T, D), F32).ap()
        ids_dram = nc.dram_tensor("ids_dram", (NBI * P, 1), I32).ap()
        slot, gates = keep("slot", [P, 2, TT], I32), keep("gates", [P, 2, TT])
        blk, ids = keep("blk", [P, NB], I32), keep("ids", [P, NBI], I32)
        place, count = keep("place", [P, 2, TT], I32), keep("count", [P, 2], I32)
        r = {"slot": slot[:], "place": place[:], "gate": gates[:], "block": blk[:], "count": count[:]}
        with nc.sbuf_tensor("n2", [P, KD, T], F32) as n:
            rms_norm(nc, "m2", cst, h, n, a2, m(3))
            router(nc, "ro", cst, vecs, din, n, h2_dram, r)
        wu = keep("wu", [P, 2, KD, D])
        u_ready = [nc.alloc_semaphore("u_ready0"), nc.alloc_semaphore("u_ready1")]
        dispatch(nc, "di", cst, r, ids_dram, ids[:], din, wu, u_ready)
        experts(nc, "ex", cst, din, r, ids[:], h2_dram, y_dram.rearrange("(b p) n -> b p n", p=P),
                y_filled, wu, u_ready)
        combine(nc, "co", cst, r, y_dram, m(5), h)
        rms_norm(nc, "fin", cst, h, h, vecs["final_g"])




def constants():
    f = np.float32
    ident = np.eye(P, dtype=f)
    rot1 = np.zeros((P, P), f)
    rot2 = np.zeros((P, P), f)
    freq = np.zeros((P, 1), f)
    inv = (np.float32(500000.0) ** (-np.arange(0, 16, 2, dtype=f) / np.float32(16))).astype(f)
    for h in (0, 64):
        for d in range(8):
            rot1[h + d + 8, h + d], rot1[h + d, h + d + 8] = -1, 1
            freq[h + d] = freq[h + d + 8] = inv[d]
        for b in (0, 32):
            for d in range(16):
                rot2[h + b + d + 16, h + b + d], rot2[h + b + d, h + b + d + 16] = -1, 1
    before = np.triu(np.ones((P, P)), 1).astype(f)
    off = np.arange(-(T - 1) - P, T + P)
    count = sum(((off % dil == 0) & (abs(off) <= window // 2)).astype(int)
                for window, dil in ((128, 1), (512, 4), (2048, 16)))
    logc = np.where(count > 0, np.log(np.maximum(count, 1)), NEG).astype(f)
    y = np.arange(1920)[None, :] - 896 - np.arange(P)[:, None]
    dilated = logc[y + (T - 1) + P]
    t = np.arange(T)
    inv2 = (np.float32(10000.0) ** (-np.arange(16, dtype=f) / np.float32(16))).astype(f)
    ang_r, ang_c = (t // 64).astype(f)[:, None] * inv2, (t % 64).astype(f)[:, None] * inv2
    cos2 = np.tile(np.concatenate([np.cos(ang_r)] * 2 + [np.cos(ang_c)] * 2, axis=1).T, (2, 1)).astype(f)
    sin2 = np.tile(np.concatenate([np.sin(ang_r)] * 2 + [np.sin(ang_c)] * 2, axis=1).T, (2, 1)).astype(f)
    p = np.arange(P)
    near = np.zeros((P, 8, 10, 64), f)
    for q in range(8):
        r, base = 2 * q + p // 64, min(max(2 * q - 4, 0), 6)
        r0 = np.clip(r - 4, 0, 8)
        c0 = np.clip(p % 64 - 8, 0, 48)
        kr, kc = base + np.arange(10), np.arange(64)
        rows = (kr[None] >= r0[:, None]) & (kr[None] < r0[:, None] + 8)
        colm = (kc[None] >= c0[:, None]) & (kc[None] < c0[:, None] + 16)
        near[:, q] = np.where(rows[:, :, None] & colm[:, None, :], 0, NEG)
    window64, window128 = np.zeros((P, 38), f), np.zeros((P, 7), f)
    window64[0:64, 18] = window64[64:, 19] = window128[:, 3] = 1
    small = {"ones": np.ones((P, P), f), "ident": ident, "window64": window64, "window128": window128, "rot1": rot1, "rot2": rot2,
             "before": before, "freq": freq, "eps": np.full((P, 1), EPS, f), "one": np.ones((P, 1), f),
             "heads32": np.kron(np.eye(4), np.ones((32, 1))).astype(f),
             "index": np.tile(np.arange(E_, dtype=f) - 1024, (P, 1)),
             "block": np.tile(np.arange(NB, dtype=f), (P, 1))}
    return small, {"dilated": dilated, "cos2": cos2, "sin2": sin2, "near": near.reshape(P, 8 * 640)}


def program(nc, din, out, upto=99):
    small, tables = constants()
    with ExitStack() as ctx:
        def sb(name, shape, dt=F32):
            return ctx.enter_context(nc.sbuf_tensor(name, shape, dt))

        width = sum(a.shape[1] for a in small.values())
        pack = sb("pack", [P, width])
        cst, o = {}, 0
        for name, a in small.items():
            cst[name] = pack[:, o:o + a.shape[1]]
            o += a.shape[1]
        vec = sb("vec", [P, din["vec"].shape[1]])
        vecs, o = {}, 0
        for name, n in VECS:
            vecs[name] = vec[:, o:o + n]
            o += n
        h = sb("h", [P, KD, T])
        load_all(nc, "load", [(pack[:], din["pack"]), (vec[:], din["vec"]), (h[:], din["x"])])
        y_dram = nc.dram_tensor("y_dram", (NB * P, T), F32).ap()
        y_filled = nc.alloc_semaphore("y_filled")
        mod = sb("mod", [P, 6 * KD, 2])
        neg_lam, sub_g = sb("neg_lam", [P, 1]), sb("sub_g", [P, 4])
        modulation_scalars(nc, "mi", cst, vecs, neg_lam[:], sub_g[:])
        first_block(nc, din, cst, vecs, h, mod, y_dram, y_filled, upto)
        if upto > 20:
            second_block(nc, din, cst, vecs, h, mod, neg_lam, sub_g, y_dram, y_filled, upto)
        store_all(nc, "store", [(out, h[:])])


def first_block(nc, din, cst, vecs, h, mod, y_dram, y_filled, upto):
    with ExitStack() as ctx:
        def sb(name, shape, dt=F32):
            return ctx.enter_context(nc.sbuf_tensor(name, shape, dt))

        proj = sb("proj", [P, 14, T])
        km = sb("km", [P, 2, NMEM])
        v = sb("v", [P, T // P, 512])
        conv = sb("conv", [P, 2, T])
        vm = sb("vm", [P, NMEM // P, NMEM])
        with ExitStack() as inner:
            def isb(name, shape):
                return inner.enter_context(nc.sbuf_tensor(name, shape, F32))

            n = isb("n", [P, KD, T])
            w_pc = Weights(nc, isb, "pc", din["w_in"], KD, 4)
            w_pin = Weights(nc, isb, "pin", din["w_in"], KD, 10, first=4)
            rms_norm(nc, "n1", cst, h, n, vecs["mix_g"], ahead=w_pc)
            project(nc, "pc", din["w_in"], cols(n), T, 4, dst=proj, weights=w_pc, ahead=w_pin)
            with nc.semaphore("gated") as gated_, nc.semaphore("conved") as conved, nc.semaphore("conv_step") as step:
                taps = conv_taps(nc, proj[:, 0:2, :], proj[:, 2:4, :], conv[:], vecs["cv_w"].rearrange(
                    "p (c k) -> p c k", c=2), vecs["cv_b"], gated_, conved, step)
                project(nc, "pin", din["w_in"], cols(n), T, 10, dst=proj[:, 4:14, :], first=4, beside=taps, weights=w_pin)
            project_rows(nc, "pv", din["w_v"], cols(n), T, v)
            mem = n[:, 0:2, :].rearrange("p a (b c) -> p (a b) c", c=NMEM)
            load_all(nc, "lm", [(mem, din["mem"])])
            rms_norm(nc, "nm", cst, mem, mem, vecs["mem_g"])
            project(nc, "pkm", din["w_km"], cols(mem), NMEM, 2, dst=km)
            project_rows(nc, "pvm", din["w_vm"], cols(mem), NMEM, vm)
        if upto == 1:
            return
        with nc.sbuf_tensor("cos", [P, T], F32) as cos, nc.sbuf_tensor("sin", [P, T], F32) as sin:
            rope_tables(nc, "rt", cst, din["positions"], cos[:], sin[:])
            rope = (cst["rot1"], cos[:], sin[:])
            head_norm(nc, "hq", cst, proj[:, 4:14, :], T, vecs["q_g"], rope, turned_tiles=8)
            head_norm(nc, "hkm", cst, km, NMEM, vecs["mk_g"])
        layer_norm_silu(nc, "cv", cst, conv, vecs["ln_g"], vecs["ln_b"])
        if upto == 2:
            return
        with nc.sbuf_tensor("dil", [P, 1920], F32) as dil:
            load_all(nc, "ld", [(dil[:], din["dilated"])])
            with nc.Block() as block:
                @block.sync
                def _(sp):
                    sp.dma_start(y_dram.rearrange("(b p) n -> p b n", p=P),
                                 din["cos2"].unsqueeze(1).to_broadcast([P, NB, T])).then_inc(y_filled, 16)
            attention(nc, "a1", cst, 4, proj[:, 4:8, :], [(proj[:, 8:12, :], T)], v, T // P,
                      bias=lambda m, u, t: [dil[:, 896 - P * t:896 - P * t + T]])
        w_po = Weights(nc, sb, "po", din["w_out"], KD, KD)
        attention(nc, "am", cst, 2, proj[:, 12:14, :], [(km, NMEM)], vm, NMEM // P, ahead=w_po)
        if upto == 3:
            return
        mixed = cols(proj[:, 4:8, :]) + cols(conv) + cols(proj[:, 12:14, :])
        project(nc, "po", din["w_out"], mixed, T, KD, add_to=h, weights=w_po)
    if upto == 4:
        return
    with ExitStack() as ctx:
        hidden = ctx.enter_context(nc.sbuf_tensor("hidden", [P, KF, T], F32))
        with ExitStack() as inner:
            def isb(name, shape):
                return inner.enter_context(nc.sbuf_tensor(name, shape, F32))

            n = isb("nf", [P, KD, T])
            w_up = UpWeights(nc, isb, din["w_up"])
            rms_norm(nc, "nf", cst, h, n, vecs["ffn_g"], ahead=w_up)
            ffn_up(nc, "fu", w_up, cols(n), hidden)
        c_rows = ctx.enter_context(nc.sbuf_tensor("c_rows", [P, 2, D], F32))
        w_fd = Weights(nc, lambda name, shape: ctx.enter_context(nc.sbuf_tensor(name, shape, F32)), "fd",
                       din["w_down"], KF, KD)
        silu_rows(nc, "sc", din["c"], c_rows[:], w_fd)
        project(nc, "fd", din["w_down"], cols(hidden), T, KD, add_to=h, thin=(din["w_mod"], c_rows[:], mod),
                weights=w_fd)


VECS = [("mix_g", KD), ("mem_g", KD), ("ffn_g", KD), ("q_g", 10), ("mk_g", 2),
        ("cv_w", 62), ("cv_b", 2), ("ln_g", 2), ("ln_b", 2),
        ("g1", KD), ("g2", KD), ("final_g", KD), ("b_mod", 6 * KD), ("lam", 4), ("sub_g", 4),
        ("gla_g", 2), ("b_dec", 2), ("b_route", 1)]


def lay_out(x):
    def col(a):
        return a.reshape(-1, P).T

    def wtiles(w):
        K, M = w.shape[0] // P, w.shape[1] // P
        return w.reshape(K, P, M, P).transpose(2, 1, 0, 3).reshape(M, P, K * P)

    def wrows(w):
        return w.reshape(-1, P, w.shape[1]).transpose(1, 0, 2)

    small, tables = constants()
    w_in = x["w_in"][0]
    v = {"mix_g": col(x["mix_norm_g"][0]), "mem_g": col(x["mem_norm_g"][0]), "ffn_g": col(x["ffn_norm_g"][0]),
         "q_g": np.stack([np.tile(x[g][0], 2) for g, m in (("q_norm_g", 4), ("k_norm_g", 4), ("mq_norm_g", 2))
                          for _ in range(m)], axis=1),
         "mk_g": np.stack([np.tile(x["mk_norm_g"][0], 2)] * 2, axis=1),
         "cv_w": x["conv_dw_w"][0].T.reshape(2, P, 31).transpose(1, 0, 2).reshape(P, 62),
         "cv_b": col(x["conv_dw_b"][0]), "ln_g": col(x["conv_ln_g"][0]), "ln_b": col(x["conv_ln_b"][0])}
    d = {"pack": np.concatenate(list(small.values()), axis=1), "dilated": tables["dilated"],
         "x": x["x"][0].T.reshape(KD, P, T).transpose(1, 0, 2),
         "mem": x["mem"][0].T.reshape(KD, P, NMEM).transpose(1, 0, 2),
         "positions": x["positions"][0],
         "w_in": wtiles(np.concatenate([w_in[:, 1536:2048], w_in[:, 0:1024], w_in[:, 2048:2304]], axis=1)),
         "w_v": wrows(w_in[:, 1024:1536]),
         "w_km": wtiles(x["w_mem_kv"][0][:, 0:256]), "w_vm": wrows(x["w_mem_kv"][0][:, 256:512]),
         "w_out": wtiles(x["w_out"][0]), "w_down": wtiles(x["w_down"][0])}
    up = x["w_up"][0].reshape(KD, P, 2, KF, P).transpose(3, 1, 0, 2, 4).reshape(KF, P, KD * 2 * P)
    taps = np.concatenate([x["ffn_dw_w"][0], x["ffn_dw_b"]], axis=0).reshape(4, 2, KF, P).transpose(2, 3, 1, 0)
    d["w_up"] = np.concatenate([up, taps.reshape(KF, P, 8)], axis=2)
    more(x, d, v, tables, col, wtiles, wrows)
    d["vec"] = np.concatenate([v[name] for name, _ in VECS], axis=1)
    return {k: np.ascontiguousarray(a) for k, a in d.items()}


def more(x, d, v, tables, col, wtiles, wrows):
    w = x["w_in_2"][0]
    at_ = dict(zip(("qa", "ka", "va", "qb", "kb", "vb", "rb", "gb", "qn", "kn", "vn"),
                   np.split(w, np.cumsum((512, 512, 512, 128, 128, 256, 256, 32, 256, 256)), axis=1)))
    pad = np.zeros((D, 96), w.dtype)
    d["w_in2"] = wtiles(np.concatenate([at_["ka"], at_["kn"], at_["kb"], at_["gb"], pad, at_["qa"], at_["qn"],
                                        at_["qb"], at_["vb"], at_["rb"]], axis=1))
    d["w_v2"] = wrows(np.concatenate([at_["va"], at_["vn"], at_["vb"]], axis=1))
    d["w_mod"] = x["w_mod_2"][0].T.reshape(6 * KD, P, D)
    d["w_out2"] = wtiles(x["w_out_2"][0])
    d["ctx"] = x["ctx_2"][0].T.reshape(KD, P, NCTX).transpose(1, 0, 2)
    dec = np.zeros((32, 2, P), w.dtype)
    for i in range(2):
        dec[16 * i:16 * i + 16, i] = x["gla_w_decay_2"][0, i]
    d["w_dec"] = dec
    d["cos2"], d["sin2"], d["near"] = tables["cos2"], tables["sin2"], tables["near"].reshape(P, TT, 640)
    p = np.arange(P)
    dr = np.clip(np.arange(18)[None, :] - p[:, None] // 64 - 1, 0, 14)
    dc = np.clip(np.arange(64)[None, :] - p[:, None] % 64 + 15, 0, 30)
    d["rpb"] = x["na_rel_bias_2"][0][:, dr[:, :, None], dc[:, None, :]].transpose(1, 0, 2, 3).reshape(P, 4, 18 * 64)
    d["w_route"] = wrows(np.concatenate([x["w_router_group_2"][0], x["w_router_expert_2"][0]], axis=1))
    d["w_eup"], d["w_edown"] = x["w_expert_up_2"][0], x["w_expert_down_2"][0]
    rest = np.zeros((P - 36,), w.dtype)
    lam = np.zeros((P, 4), w.dtype)
    lam[0:64] = x["diff_lambda_2"][0].T
    d["c"] = np.concatenate([x["c_2"][0], x["c_ctx_2"]])
    v.update({"g1": col(x["norm1_g_2"][0]),
              "g2": col(x["norm2_g_2"][0]), "final_g": col(x["final_g_2"]), "b_mod": col(x["b_mod_2"][0]), "lam": lam,
              "sub_g": np.stack([x["diff_sub_g_2"][0]] * 4, axis=1),
              "gla_g": np.stack([np.tile(x["gla_norm_g_2"][0], 2)] * 2, axis=1),
              "b_dec": x["gla_b_decay_2"][0].T,
              "b_route": np.concatenate([x["b_router_group_2"][0], x["b_router_expert_2"][0], rest])[:, None]})


def kernel(**inputs):
    import concourse.bacc as bacc
    from concourse.bass_utils import run_bass_kernel_spmd

    nc = bacc.Bacc("TRN2", target_bir_lowering=False, num_devices=1)
    arrays = lay_out({k: np.asarray(a) for k, a in inputs.items()})
    din = {k: nc.dram_tensor(f"in_{k}", a.shape, mybir.dt.from_np(a.dtype), kind="ExternalInput").ap()
           for k, a in arrays.items()}
    out = nc.dram_tensor("out", (P, KD, T), F32, kind="ExternalOutput").ap()
    program(nc, din, out)
    r = run_bass_kernel_spmd(nc, [{f"in_{k}": a for k, a in arrays.items()}], core_ids=[0])
    y = r.results[0]["out"]
    return y.transpose(1, 0, 2).reshape(D, T).T[None]
```
